# Optimizing a Trainium2 kernel written in Bass

```python
import math
import jax, jax.numpy as jnp
from jax import lax
import numpy as np

D_MODEL = 1024
BATCH = 1
SEQ = 512
DEPTH = 1
DEC_BATCH = 8
DEC_SEQ = 8
PAST_LEN = 4096
PAGE_SIZE = 128

H_R = 4
DK_R = 128
DV_R = 256
QK_R = H_R * DK_R
V_R = H_R * DV_R
H_M = 4
DH_M = 256
W_M = H_M * DH_M
CONV_W = 4
N_KEYS = 128
N_EXPERTS = N_KEYS * N_KEYS
P_HEADS = 8
P_DKEY = 256
P_HALF = P_DKEY // 2
P_TOPK = 16
P_BLOCK = 256
CHUNK = 128
ROPE_BASE = 10000.0
EPS = 1e-6
IN_SIZES = (QK_R, QK_R, V_R, V_R, W_M, W_M, W_M, H_M, H_M, D_MODEL, D_MODEL)
IN_WIDTH = 2 * QK_R + 2 * V_R + 3 * W_M + 2 * H_M + 2 * D_MODEL

kernel_name = 'hybrid_retention_mlstm_peer_step'

def _split_points():
    pts, acc = [], 0
    for s in IN_SIZES[:-1]:
        acc += s
        pts.append(acc)
    return pts

def rmsnorm(x, g):
    xf = x.astype(jnp.float32)
    y = xf * lax.rsqrt(jnp.mean(xf * xf, axis=-1, keepdims=True) + EPS) * g.astype(jnp.float32)
    return y.astype(x.dtype)

def head_norm(x, g):
    mu = jnp.mean(x, axis=-1, keepdims=True)
    xc = x - mu
    var = jnp.mean(xc * xc, axis=-1, keepdims=True)
    return xc * lax.rsqrt(var + EPS) * g.astype(jnp.float32)

def rope(x, pos):
    half = x.shape[-1] // 2
    freqs = jnp.exp(-math.log(ROPE_BASE) * jnp.arange(half, dtype=jnp.float32) / half)
    ang = pos[:, None] * freqs[None, :]
    cos = jnp.cos(ang)[None, :, None, :]
    sin = jnp.sin(ang)[None, :, None, :]
    x1, x2 = x[..., :half], x[..., half:]
    return jnp.concatenate([x1 * cos - x2 * sin, x1 * sin + x2 * cos], axis=-1)

def _chunk_len(T):
    return CHUNK if T % CHUNK == 0 else T

def _to_chunks(a, L):
    B, T = a.shape[0], a.shape[1]
    a = a.reshape((B, T // L, L) + a.shape[2:])
    perm = (1, 0, 3, 2) + tuple(range(4, a.ndim))
    return a.transpose(perm)

def _from_chunks(a):
    nc, B, H, L, d = a.shape
    return a.transpose(1, 0, 3, 2, 4).reshape(B, nc * L, H, d)

def retention_chunked(q, k, v, S0):
    T = q.shape[1]
    L = _chunk_len(T)
    log_gamma = jnp.log1p(-jnp.exp2(-5.0 - jnp.arange(H_R, dtype=jnp.float32)))
    idx = jnp.arange(L, dtype=jnp.float32)
    diff = idx[:, None] - idx[None, :]
    causal = diff >= 0
    dmat = jnp.where(causal[None], jnp.exp(log_gamma[:, None, None] * jnp.where(causal, diff, 0.0)[None]), 0.0)
    q_dec = jnp.exp(log_gamma[:, None] * (idx[None, :] + 1.0))
    k_dec = jnp.exp(log_gamma[:, None] * (L - 1.0 - idx[None, :]))
    c_dec = jnp.exp(log_gamma * L)

    def step(S, inp):
        qi, ki, vi = inp
        sc = jnp.einsum('bhtd,bhsd->bhts', qi, ki) * dmat[None]
        inner = jnp.einsum('bhts,bhsv->bhtv', sc, vi)
        cross = jnp.einsum('bhtd,bhdv->bhtv', qi, S) * q_dec[None, :, :, None]
        S_new = c_dec[None, :, None, None] * S + jnp.einsum('bhsd,bhsv->bhdv', ki * k_dec[None, :, :, None], vi)
        return S_new, inner + cross

    S, out = lax.scan(step, S0, (_to_chunks(q, L), _to_chunks(k, L), _to_chunks(v, L)))
    return _from_chunks(out), S

def mlstm_chunked(q, k, v, i_pre, logf, C0, n0, m0):
    T = q.shape[1]
    L = _chunk_len(T)
    ar = jnp.arange(L)
    causal = ar[:, None] >= ar[None, :]

    def step(carry, inp):
        C, n, m = carry
        qi, ki, vi, ii, fi = inp
        b = jnp.cumsum(fi, axis=-1)
        logD = jnp.where(causal, b[..., :, None] - b[..., None, :] + ii[..., None, :], -jnp.inf)
        m_t = jnp.maximum(b + m[..., None], jnp.max(logD, axis=-1))
        dw = jnp.exp(logD - m_t[..., None])
        w_prev = jnp.exp(b + m[..., None] - m_t)
        sc = jnp.einsum('bhtd,bhsd->bhts', qi, ki) * dw
        num = jnp.einsum('bhts,bhsv->bhtv', sc, vi) + w_prev[..., None] * jnp.einsum('bhtd,bhdv->bhtv', qi, C)
        den = jnp.sum(sc, axis=-1) + w_prev * jnp.einsum('bhtd,bhd->bht', qi, n)
        h = num / jnp.maximum(jnp.abs(den), jnp.exp(-m_t))[..., None]
        m_new = m_t[..., -1]
        wk = jnp.exp(b[..., -1:] - b + ii - m_new[..., None])
        dec = jnp.exp(b[..., -1] + m - m_new)
        C_new = dec[..., None, None] * C + jnp.einsum('bhsd,bhsv->bhdv', ki * wk[..., None], vi)
        n_new = dec[..., None] * n + jnp.einsum('bhs,bhsd->bhd', wk, ki)
        return (C_new, n_new, m_new), h

    (C, n, m), h = lax.scan(step, (C0, n0, m0),
                            (_to_chunks(q, L), _to_chunks(k, L), _to_chunks(v, L),
                             _to_chunks(i_pre, L), _to_chunks(logf, L)))
    return _from_chunks(h), C, n, m

def causal_conv(x, buf, w, b):
    T = x.shape[1]
    xp = jnp.concatenate([buf.astype(x.dtype), x], axis=1)
    out = b
    for j in range(CONV_W):
        out = out + xp[:, j:j + T] * w[j]
    return out, xp[:, xp.shape[1] - (CONV_W - 1):]

def peer(xn, w_pq, sub_keys1, sub_keys2, expert_u, expert_v):
    B, T, D = xn.shape
    dt = xn.dtype
    xt = xn.reshape(B * T, D)
    N = xt.shape[0]
    q = (xt @ w_pq).astype(jnp.float32).reshape(N, P_HEADS, 2, P_HALF)
    s1 = jnp.einsum('nhd,kd->nhk', q[:, :, 0], sub_keys1.astype(jnp.float32))
    s2 = jnp.einsum('nhd,kd->nhk', q[:, :, 1], sub_keys2.astype(jnp.float32))
    v1, i1 = lax.top_k(s1, P_TOPK)
    v2, i2 = lax.top_k(s2, P_TOPK)
    cand = (v1[..., :, None] + v2[..., None, :]).reshape(N, P_HEADS, P_TOPK * P_TOPK)
    cand_idx = (i1[..., :, None] * N_KEYS + i2[..., None, :]).reshape(N, P_HEADS, P_TOPK * P_TOPK)
    top_s, top_p = lax.top_k(cand, P_TOPK)
    idx = jnp.take_along_axis(cand_idx, top_p, axis=-1)
    g = jax.nn.softmax(top_s, axis=-1)
    n_blk = -(-N // P_BLOCK)
    pad = n_blk * P_BLOCK - N
    xb = jnp.pad(xt, ((0, pad), (0, 0))).reshape(n_blk, P_BLOCK, D)
    ib = jnp.pad(idx, ((0, pad), (0, 0), (0, 0))).reshape(n_blk, P_BLOCK, P_HEADS, P_TOPK)
    gb = jnp.pad(g, ((0, pad), (0, 0), (0, 0))).reshape(n_blk, P_BLOCK, P_HEADS, P_TOPK)

    def blk(args):
        xs, ids, gs = args
        u = expert_u[ids]
        a = jax.nn.gelu(jnp.einsum('pd,phkd->phk', xs, u).astype(jnp.float32), approximate=False)
        return jnp.einsum('phk,phkd->pd', (gs * a).astype(dt), expert_v[ids])

    out = lax.map(blk, (xb, ib, gb)).reshape(n_blk * P_BLOCK, D)[:N]
    return out.reshape(B, T, D)

def hybrid_layer(x, pos, s_ret, s_C, s_n, s_m, s_conv,
                 norm1_g, w_in, b_i, b_f, conv_w, conv_b, w_mq, w_mk, ret_norm_g, mlstm_norm_g,
                 w_br, w_bm, w_out, norm2_g, w_pq, sub_keys1, sub_keys2, expert_u, expert_v):
    B, T, _ = x.shape
    dt = x.dtype
    f32 = jnp.float32
    xn = rmsnorm(x, norm1_g)
    proj = xn @ w_in
    q_r, k_r, v_r, g_r, x_m, v_m, o_m, i_m, f_m, gate_r, gate_m = jnp.split(proj, _split_points(), axis=-1)
    q_r = rope(q_r.astype(f32).reshape(B, T, H_R, DK_R), pos) * (DK_R ** -0.5)
    k_r = rope(k_r.astype(f32).reshape(B, T, H_R, DK_R), pos)
    v_r = v_r.astype(f32).reshape(B, T, H_R, DV_R)
    y_r, ret_new = retention_chunked(q_r, k_r, v_r, s_ret.astype(f32))
    y_r = head_norm(y_r, ret_norm_g).reshape(B, T, V_R) * jax.nn.silu(g_r.astype(f32))
    br = y_r.astype(dt) @ w_br
    xc, conv_new = causal_conv(x_m, s_conv, conv_w, conv_b)
    xc = jax.nn.silu(xc.astype(f32)).reshape(B, T, H_M, DH_M)
    q_m = jnp.einsum('bthd,hde->bthe', xc, w_mq.astype(f32)) * (DH_M ** -0.5)
    k_m = jnp.einsum('bthd,hde->bthe', xc, w_mk.astype(f32))
    v_m = v_m.astype(f32).reshape(B, T, H_M, DH_M)
    i_pre = i_m.astype(f32) + b_i.astype(f32)
    logf = jax.nn.log_sigmoid(f_m.astype(f32) + b_f.astype(f32))
    h_m, C_new, n_new, m_new = mlstm_chunked(q_m, k_m, v_m, i_pre, logf,
                                             s_C.astype(f32), s_n.astype(f32), s_m.astype(f32))
    h_m = head_norm(h_m, mlstm_norm_g).reshape(B, T, W_M) * jax.nn.sigmoid(o_m.astype(f32))
    bm = h_m.astype(dt) @ w_bm
    merged = jax.nn.sigmoid(gate_r) * br + jax.nn.sigmoid(gate_m) * bm
    x = x + merged @ w_out
    x = x + peer(rmsnorm(x, norm2_g), w_pq, sub_keys1, sub_keys2, expert_u, expert_v)
    return x, ret_new, C_new, n_new, m_new, conv_new

def setup_inputs(seed: int = 0) -> dict:
    key = jax.random.key(seed)
    ks = jax.random.split(key, 32)
    f32 = jnp.float32

    def nrm(k, shape, scale):
        return jax.random.normal(k, shape, f32) * scale

    def gain(k, shape):
        return 1.0 + 0.01 * jax.random.normal(k, shape, f32)

    return {
        'x_prompt': nrm(ks[0], (BATCH, SEQ, D_MODEL), 1.0),
        'x_sample': nrm(ks[1], (DEC_BATCH, DEC_SEQ, D_MODEL), 1.0),
        'state_ret': nrm(ks[2], (DEPTH, DEC_BATCH, H_R, DK_R, DV_R), 2.0),
        'state_mlstm_C': nrm(ks[3], (DEPTH, DEC_BATCH, H_M, DH_M, DH_M), 0.5),
        'state_mlstm_n': nrm(ks[4], (DEPTH, DEC_BATCH, H_M, DH_M), 0.5),
        'state_mlstm_m': nrm(ks[5], (DEPTH, DEC_BATCH, H_M), 1.0),
        'state_conv': nrm(ks[6], (DEPTH, DEC_BATCH, CONV_W - 1, W_M), 1.0),
        'norm1_g': gain(ks[7], (DEPTH, D_MODEL)),
        'w_in': nrm(ks[8], (DEPTH, D_MODEL, IN_WIDTH), D_MODEL ** -0.5),
        'b_i': nrm(ks[9], (DEPTH, H_M), 0.1),
        'b_f': 3.0 + nrm(ks[10], (DEPTH, H_M), 0.5),
        'conv_w': nrm(ks[11], (DEPTH, CONV_W, W_M), 0.5),
        'conv_b': nrm(ks[12], (DEPTH, W_M), 0.02),
        'w_mq': nrm(ks[13], (DEPTH, H_M, DH_M, DH_M), DH_M ** -0.5),
        'w_mk': nrm(ks[14], (DEPTH, H_M, DH_M, DH_M), DH_M ** -0.5),
        'ret_norm_g': gain(ks[15], (DEPTH, H_R, DV_R)),
        'mlstm_norm_g': gain(ks[16], (DEPTH, H_M, DH_M)),
        'w_br': nrm(ks[17], (DEPTH, V_R, D_MODEL), V_R ** -0.5),
        'w_bm': nrm(ks[18], (DEPTH, W_M, D_MODEL), W_M ** -0.5),
        'w_out': nrm(ks[19], (DEPTH, D_MODEL, D_MODEL), D_MODEL ** -0.5),
        'norm2_g': gain(ks[20], (DEPTH, D_MODEL)),
        'w_pq': nrm(ks[21], (DEPTH, D_MODEL, P_HEADS * P_DKEY), D_MODEL ** -0.5),
        'sub_keys1': nrm(ks[22], (DEPTH, N_KEYS, P_HALF), P_HALF ** -0.5),
        'sub_keys2': nrm(ks[23], (DEPTH, N_KEYS, P_HALF), P_HALF ** -0.5),
        'expert_u': nrm(ks[24], (DEPTH, N_EXPERTS, D_MODEL), D_MODEL ** -0.5),
        'expert_v': nrm(ks[25], (DEPTH, N_EXPERTS, D_MODEL), P_HEADS ** -0.5),
        'norm_f_g': gain(ks[26], (D_MODEL,)),
    }

def reference(x_prompt, x_sample, state_ret, state_mlstm_C, state_mlstm_n, state_mlstm_m, state_conv,
              norm1_g, w_in, b_i, b_f, conv_w, conv_b, w_mq, w_mk, ret_norm_g, mlstm_norm_g,
              w_br, w_bm, w_out, norm2_g, w_pq, sub_keys1, sub_keys2, expert_u, expert_v, norm_f_g):
    f32 = jnp.float32
    Bp, Tp = x_prompt.shape[0], x_prompt.shape[1]
    Ts = x_sample.shape[1]
    pos_p = jnp.arange(Tp, dtype=f32)
    pos_s = PAST_LEN + jnp.arange(Ts, dtype=f32)
    hp, hs = x_prompt, x_sample
    ret_p, C_p, n_p, m_p, cv_p = [], [], [], [], []
    ret_s, C_s, n_s, m_s, cv_s = [], [], [], [], []
    for l in range(DEPTH):
        lw = (norm1_g[l], w_in[l], b_i[l], b_f[l], conv_w[l], conv_b[l], w_mq[l], w_mk[l],
              ret_norm_g[l], mlstm_norm_g[l], w_br[l], w_bm[l], w_out[l], norm2_g[l],
              w_pq[l], sub_keys1[l], sub_keys2[l], expert_u[l], expert_v[l])
        hp, r0, c0, n0, m0, v0 = hybrid_layer(
            hp, pos_p,
            jnp.zeros((Bp, H_R, DK_R, DV_R), f32), jnp.zeros((Bp, H_M, DH_M, DH_M), f32),
            jnp.zeros((Bp, H_M, DH_M), f32), jnp.zeros((Bp, H_M), f32),
            jnp.zeros((Bp, CONV_W - 1, W_M), x_prompt.dtype), *lw)
        hs, r1, c1, n1, m1, v1 = hybrid_layer(
            hs, pos_s, state_ret[l], state_mlstm_C[l], state_mlstm_n[l], state_mlstm_m[l], state_conv[l], *lw)
        ret_p.append(r0); C_p.append(c0); n_p.append(n0); m_p.append(m0); cv_p.append(v0)
        ret_s.append(r1); C_s.append(c1); n_s.append(n1); m_s.append(m1); cv_s.append(v1)
    y_prompt = rmsnorm(hp, norm_f_g)
    y_sample = rmsnorm(hs, norm_f_g)
    return (y_prompt, y_sample,
            jnp.stack(ret_p).astype(state_ret.dtype), jnp.stack(C_p).astype(state_mlstm_C.dtype),
            jnp.stack(n_p).astype(state_mlstm_n.dtype), jnp.stack(m_p).astype(state_mlstm_m.dtype),
            jnp.stack(cv_p).astype(state_conv.dtype),
            jnp.stack(ret_s).astype(state_ret.dtype), jnp.stack(C_s).astype(state_mlstm_C.dtype),
            jnp.stack(n_s).astype(state_mlstm_n.dtype), jnp.stack(m_s).astype(state_mlstm_m.dtype),
            jnp.stack(cv_s).astype(state_conv.dtype))


_drawn_inputs = setup_inputs


def setup_inputs(seed=0):
    import zlib

    import numpy as np

    out = dict(_drawn_inputs(seed))
    spreads = {}
    factors = {'ret_norm_g': 25.065, 'mlstm_norm_g': 28.388, 'norm2_g': 12.685, 'norm_f_g': 31.276}
    for name, (base, spread) in spreads.items():
        noise = np.random.default_rng([zlib.crc32(name.encode()), seed]).standard_normal(out[name].shape)
        drawn = base * np.exp(spread * noise) if base else spread * noise
        out[name] = __import__('jax').numpy.asarray(drawn.astype(out[name].dtype))
    for name, factor in factors.items():
        out[name] = (out[name] * factor).astype(out[name].dtype)
    return out
```

```python
import math

import numpy as np

import concourse.bass as bass
from concourse import mybir
from contextlib import ExitStack

F32 = mybir.dt.float32
U32 = mybir.dt.uint32
ACT = mybir.ActivationFunctionType
ALU = mybir.AluOpType
AX = mybir.AxisListType.X

P = 128
D = 1024
KD = D // P
SEQ = 512
NB = 8
TS = 8
NS = NB * TS
NCH = SEQ // P
NT = NCH + 1
TOK = SEQ + NS
HALF_TOK = TOK // 2
PAST = 4096
H = 4
DK = 128
DV = 256
DH = 256
CW = 4
QK_R = H * DK
V_R = H * DV
PH = 8
NKEY = 128
TOPK = 16
NCAND = TOPK * TOPK
NSLOT = PH * TOPK
EPS = 1e-6
NEG = -1.0e30
LOWEST = -3.0e38
GRP = 512
C_QKVG = 0
C_XM = 2 * QK_R + 2 * V_R
C_VM = C_XM + D
C_IF = C_XM + 3 * D
C_GR = C_IF + 2 * H
C_GM = C_GR + D
G_TILE = PH
G_SAMPLE = PH // 2
NGRP = NCH * G_TILE + G_SAMPLE


def _log_gamma():
    return np.log1p(-np.exp2(-5.0 - np.arange(H, dtype=np.float32))).astype(np.float32)


def _tables():
    t = {}
    lg = _log_gamma()
    half = DK // 2
    freqs = np.exp(np.float32(-math.log(10000.0)) * np.arange(half, dtype=np.float32) / np.float32(half)).astype(np.float32)
    pos = np.concatenate([np.arange(SEQ), np.tile(PAST + np.arange(TS), NB)]).astype(np.float32)
    ang = (pos[:, None] * freqs[None, :]).astype(np.float32)
    cs = np.zeros((NT * P, 2, half), np.float32)
    cs[:TOK, 0], cs[:TOK, 1] = np.cos(ang), np.sin(ang)
    t["rope"] = cs.reshape(NT, P, 2 * half).transpose(1, 0, 2).reshape(P, -1)
    i = np.arange(P, dtype=np.float32)
    r = np.arange(NS)
    same = (r[:, None] // TS) == (r[None, :] // TS)
    scale = np.float32(DK ** -0.5)

    def pad(a):
        out = np.zeros((P,) + a.shape[1:], np.float32)
        out[:a.shape[0]] = a
        return out.reshape(P, -1)

    diff = i[None, :] - i[:, None]
    dm = np.where(diff >= 0, np.exp(lg[:, None, None] * np.maximum(diff, 0)), 0) * scale
    t["ret_mask_p"] = dm.transpose(1, 0, 2).reshape(P, -1)
    sdiff = (r[None, :] - r[:, None]).astype(np.float32)
    sok = same & (sdiff >= 0)
    sm = np.where(sok, np.exp(lg[:, None, None] * np.maximum(sdiff, 0)), 0) * scale
    t["ret_mask_s"] = pad(sm.transpose(1, 0, 2))
    t["ret_qdec_p"] = np.broadcast_to((np.exp(lg[:, None] * (i + 1)) * scale).reshape(1, -1), (P, H * P))
    t["ret_qdec_s"] = np.broadcast_to((np.exp(lg[:, None] * (r % TS + 1)) * scale).reshape(1, -1), (P, H * NS))
    t["ret_kdec_p"] = np.exp(lg[None, :] * (P - 1 - i)[:, None])
    t["ret_kdec_s"] = pad(np.exp(lg[None, :] * (TS - 1 - r % TS)[:, None]))
    t["batch_cols"] = np.broadcast_to((r[None, :] // TS == np.arange(NB)[:, None]).astype(np.float32).reshape(1, -1), (P, NB * NS))
    t["batch_rows"] = pad((r[:, None] // TS == np.arange(NB)[None, :]).astype(np.float32))
    t["last_rows"] = pad((r[:, None] == np.arange(NB)[None, :] * TS + TS - 1).astype(np.float32))
    t["tri_p"] = (diff >= 0).astype(np.float32)
    t["tri_s"] = pad(sok.astype(np.float32))
    t["mask_ts_p"] = np.where(diff.T >= 0, 0, NEG)
    t["mask_ts_s"] = pad(np.where(sok.T, 0, NEG))
    t["mask_st_p"] = np.where(diff >= 0, 0, NEG)
    t["mask_st_s"] = pad(np.where(sok, 0, NEG))
    t["pick_p"] = (np.arange(P)[:, None] == P - 1).astype(np.float32) * np.ones((1, P), np.float32)
    t["pick_s"] = pad((r[:, None] == (r[None, :] // TS) * TS + TS - 1).astype(np.float32))
    t["ones"] = np.ones((P, P))
    t["ident"] = np.eye(P)
    t["fold2"] = np.concatenate([np.concatenate([np.eye(NS), np.eye(NS)], 0), np.zeros((P, P - NS))], 1)
    t["iota16"] = np.broadcast_to(np.arange(TOPK, dtype=np.float32)[None, :], (P, TOPK))
    where, at, parts = {}, 0, []
    for k, v in t.items():
        v = np.ascontiguousarray(v, dtype=np.float32)
        where[k] = (at, v.shape[1])
        at += v.shape[1]
        parts.append(v)
    return where, np.concatenate(parts, 1)


_WHERE, _TABLES = _tables()
NTAB = _TABLES.shape[1]

COLS = ["norm1_g", "norm2_g", "ret_norm_g", "mlstm_norm_g", "conv_b", "conv_w0", "conv_w1", "conv_w2", "conv_w3"]


class Arena:

    def __init__(self, tensor, words):
        self.tensor, self.words, self.top = tensor, words, 0

    def take(self, *shape, at=None):
        n = int(np.prod(shape))
        a = self.top if at is None else at
        if at is None:
            self.top += n
        assert a + n <= self.words, (a, n, self.words)
        v = self.tensor[:, a:a + n]
        if len(shape) == 1:
            return v
        names = "abcd"[:len(shape)]
        return v.rearrange("p (" + " ".join(names) + ") -> p " + " ".join(names),
                           **{k: s for k, s in zip(names[1:], shape[1:])})


class Chain:

    def __init__(self, eng, sem):
        self.eng, self.sem, self.n = eng, sem, 0

    def then(self, ins):
        self.n += 1
        ins.then_inc(self.sem, 1)
        self.eng.wait_ge(self.sem, self.n)


def rows(c):
    return P if c < NCH else NS


def bc(ap, *shape):
    return ap.unsqueeze(len(shape) - 1).to_broadcast(list(shape))


def mid(ap, n, *shape):
    return ap.unsqueeze(1).to_broadcast(list(shape))


def program(nc, I, O):
    with ExitStack() as ctx:
        WORDS = 52480
        sbuf = ctx.enter_context(nc.sbuf_tensor("arena", [P, WORDS], F32))
        A = Arena(sbuf, WORDS)
        bank = [ctx.enter_context(nc.psum_tensor(f"bank{i}", [P, GRP], F32)) for i in range(8)]

        tab = A.take(NTAB)
        T = {k: tab[:, a:a + n] for k, (a, n) in _WHERE.items()}
        cols = A.take(len(COLS), KD)
        col = {k: cols[:, i, :] for i, k in enumerate(COLS)}
        xnT = A.take(KD, TOK)
        yrT = A.take(KD, TOK)
        BASE = A.top
        held = []

        def sem(name):
            held.append(nc.alloc_semaphore(name=name))
            return held[-1]

        def give_back():
            with nc.Block() as block:
                @block.gpsimd
                def _(pool):
                    for s in held:
                        pool.sem_clear(s)
            for s in held:
                nc.release_semaphore(s)
            held.clear()

        env = dict(nc=nc, I=I, O=O, A=A, bank=bank, T=T, tab=tab, cols=cols, col=col, xnT=xnT, yrT=yrT, sem=sem)
        proj = A.take(NT, 2 * QK_R + 2 * V_R)
        norm_and_retention_projection(env, proj)
        retention(env, proj)
        A.top = BASE
        v = A.take(NT, H, DH + 1)
        o = A.take(NT, D)
        kT = A.take(KD, TOK)
        qT = A.take(KD, TOK)
        gates = A.take(NT, 2 * H)
        MID = A.top
        mlstm_projection(env, v, o, kT, qT, gates)
        A.top = MID
        mlstm(env, v, o, kT, qT, gates)
        hmT = qT
        give_back()
        A.top = BASE
        x1 = A.take(NT, D)
        xn2 = A.take(NT, D)
        assert A.top <= BASE + NT * H * (DH + 1) + NT * D
        A.top = MID
        env["kT_place"] = kT.rearrange("p k t -> p (k t)")
        xn2T = merge_and_norm(env, hmT, x1, xn2)
        A.top = BASE + 2 * NT * D
        table = A.take(NGRP, TOPK)
        gate = A.take(NGRP, TOPK)
        route(env, x1, xn2, xn2T, table, gate)
        A.top = BASE + 2 * NT * D + 2 * NGRP * TOPK
        experts(env, x1, xn2, table, gate)


def transpose_tile(pe, src, ident, banks, n, last_sem, before=None):
    for half in range(2):
        if before:
            before(half)
        for j in range(4):
            k = half * 4 + j
            ins = pe.transpose(banks[half][:, j * P:j * P + n], src[0:n, k * P:(k + 1) * P], ident[0:n, 0:n])
        ins.then_inc(last_sem, 1)


def quarter(b, n):
    return b[:, :].rearrange("p (k t) -> p k t", k=4)[:, :, 0:n]


def norm_and_retention_projection(env, proj):
    nc, I, A, T, bank, sem = (env[k] for k in ("nc", "I", "A", "T", "bank", "sem"))
    xnT, col = env["xnT"], env["col"]
    x = A.take(NT, D)
    junk = A.take(D)
    ms = A.take(NT, 1)
    NW = 2
    ring = A.take(NW, KD, GRP)
    NG = proj.shape[2] // GRP
    tables, loaded = sem("p1_tables"), sem("p1_x_loaded")
    weights = [sem(f"p1_weights{i}") for i in range(NW)]
    squares, roots, normed = sem("p1_squares"), sem("p1_roots"), sem("p1_normed")
    turned, kept = sem("p1_turned"), sem("p1_kept")
    product, copied, own = sem("p1_product"), sem("p1_copied"), sem("p1_own")
    w_in = I["w_in"].rearrange("(k p) c -> p k c", p=P)

    with nc.Block() as block:
        @block.sync
        def _(sp):
            sp.dma_start(x[:, 0:NCH, :], I["x_prompt"].rearrange("(t p) d -> p t d", p=P)).then_inc(loaded, 16)
            sp.dma_start(x[0:NS, NCH, :], I["x_sample"]).then_inc(loaded, 16)
            sp.dma_start(env["tab"], I["tables"]).then_inc(tables, 16)
            sp.dma_start(env["cols"].rearrange("p a b -> p (a b)"), I["cols"]).then_inc(tables, 16)
            for g in range(NW):
                sp.dma_start(ring[:, g], w_in[:, :, g * GRP:(g + 1) * GRP]).then_inc(weights[g], 16)
            with sp.Fori(1, NG // NW) as r:
                for g in range(NW):
                    sp.wait_ge(product, NT * (NW * (r - 1) + g + 1))
                    sp.dma_start(ring[:, g], w_in[:, :, bass.ds((NW * r + g) * GRP, GRP)]).then_inc(weights[g], 16)

        @block.scalar
        def _(act):
            act.wait_ge(loaded, 32)
            for c in range(NT):
                n = rows(c)
                if c:
                    act.wait_ge(squares, c)
                act.activation(junk[0:n, :], x[0:n, c, :], ACT.Square, accum_out=ms[0:n, c, :]).then_inc(squares, 1)
            act.wait_ge(squares, NT)
            for c in range(NT):
                n = rows(c)
                act.activation(ms[0:n, c, :], ms[0:n, c, :], ACT.Sqrt, bias=EPS, scale=1.0 / D).then_inc(roots, 1)
            with act.Fori(0, NG) as g:
                for c in range(NT):
                    n = rows(c)
                    act.wait_ge(product, NT * g + (c + 1))
                    act.activation(proj[0:n, c, bass.ds(g * GRP, GRP)], bank[c][0:n, :], ACT.Copy).then_inc(copied, 1)

        @block.vector
        def _(dve):
            chain = Chain(dve, own)
            for c in range(NT):
                n = rows(c)
                dve.wait_ge(roots, c + 1)
                chain.then(dve.reciprocal(ms[0:n, c, :], ms[0:n, c, :]))
                dve.tensor_scalar(x[0:n, c, :], x[0:n, c, :], ms[0:n, c, :], None, ALU.mult).then_inc(normed, 1)
            dve.wait_ge(tables, 32)
            for c in range(NT):
                n = rows(c)
                for half in range(2):
                    dve.wait_ge(turned, 2 * c + half + 1)
                    k = 4 * half
                    dve.tensor_tensor(xnT[:, k:k + 4, c * P:c * P + n], quarter(bank[6 + half], n),
                                      bc(col["norm1_g"][:, k:k + 4], P, 4, n), ALU.mult).then_inc(kept, 1)

        @block.tensor
        def _(pe):
            pe.wait_ge(tables, 32)
            for c in range(NT):
                pe.wait_ge(normed, c + 1)

                def free(half, c=c):
                    if c:
                        pe.wait_ge(kept, 2 * (c - 1) + half + 1)
                transpose_tile(pe, x[:, c, :], T["ident"], bank[6:8], rows(c), turned, free)
            pe.wait_ge(kept, 2 * NT)
            project_groups(pe, xnT, ring, weights, bank, product, copied, NG, NW)


def project_groups(pe, xT, ring, weights, bank, product, copied, NG, NW):
    def body(r, first):
        for s in range(NW):
            pe.wait_ge(weights[s], 16 * (r + 1))
            for c in range(NT):
                n = rows(c)
                if not (first and s == 0):
                    pe.wait_ge(copied, NT * (NW * r + s - 1) + c + 1)
                for k in range(KD):
                    ins = pe.matmul(bank[c][0:n, :], xT[:, k, c * P:c * P + n], ring[:, s, k, :], start=k == 0, stop=k == KD - 1)
                ins.then_inc(product, 1)
    body(0, True)
    if NG > NW:
        with pe.Fori(1, NG // NW) as r:
            body(r, False)


def retention(env, proj):
    nc, I, O, A, T, bank, sem = (env[k] for k in ("nc", "I", "O", "A", "T", "bank", "sem"))
    yrT, col = env["yrT"], env["col"]
    top = A.top
    A.top = top - (NT * D + D + NT + 2 * KD * GRP)
    rr = A.take(2 * H, DK)
    part = A.take(4, 2 * H, DK // 2)
    qT, kT, qdT = A.take(H, P), A.take(H, P), A.take(H, P)
    kd = A.take(H, DK)
    prob = A.take(H, P)
    S = A.take(H, DV)
    y = A.take(H, DV)
    stats, mv, rstd = A.take(H, 6), A.take(H, 2), A.take(H)
    SS = A.take(H, NB, DV)
    qz = A.take(H, NB, NS)
    kz = A.take(H, NB, DK)
    gamma = np.exp(_log_gamma())
    cdec = [float(np.exp(_log_gamma()[h] * L)) for L in (P, TS) for h in range(H)]

    states, silu = sem("p2_states"), sem("p2_silu")
    own, rotated = sem("p2_own"), sem("p2_rotated")
    turned, q_out, k_out, qd_out = sem("p2_turned"), sem("p2_q_out"), sem("p2_k_out"), sem("p2_qd_out")
    scores, probs, ydone, kv, kd_out = sem("p2_scores"), sem("p2_probs"), sem("p2_y"), sem("p2_kv"), sem("p2_kd")
    new_state, var, root, yn, yturned, ykept = (sem("p2_" + n) for n in ("new_state", "var", "root", "ynormed", "yturned", "ykept"))
    masked, stored = sem("p2_masked"), sem("p2_stored")
    UNITS = 2 * H

    with nc.Block() as block:
        @block.sync
        def _(sp):
            for h in range(H):
                sp.dma_start(SS[:, h], I["state_ret"].rearrange("b h k v -> h k b v")[h]).then_inc(states, 16)
            sp.wait_ge(new_state, NCH * H)
            sp.dma_start(O["ret_p"].rearrange("h k v -> k h v"), S).then_inc(stored, 16)
            for h in range(H):
                sp.wait_ge(new_state, NCH * H + NB * (h + 1))
                sp.dma_start(O["ret_s"].rearrange("b h k v -> h k b v")[h], SS[:, h]).then_inc(stored, 16)
            sp.wait_ge(stored, 16 * (H + 1))

        @block.scalar
        def _(act):
            for c in range(NT):
                n = rows(c)
                g = proj[0:n, c, 2 * QK_R + V_R:]
                act.activation(g, g, ACT.Silu).then_inc(silu, 1)
            for c in range(NT):
                n = rows(c)
                act.wait_ge(turned, 2 * c + 1)
                if c:
                    act.wait_ge(scores, c)
                    act.wait_ge(qd_out, c)
                act.activation(qT[:, :, 0:n], quarter(bank[0], n), ACT.Copy).then_inc(q_out, 1)
                act.wait_ge(turned, 2 * c + 2)
                act.activation(kT[:, :, 0:n], quarter(bank[1], n), ACT.Copy).then_inc(k_out, 1)
                act.wait_ge(var, c + 1)
                act.activation(rstd[0:n, :], mv[0:n, :, 1], ACT.Sqrt, bias=EPS).then_inc(root, 1)

        @block.vector
        def _(dve):
            chain = Chain(dve, own)
            for c in range(NT):
                n = rows(c)
                sample = c == NCH
                k_ = "s" if sample else "p"
                qk = proj[0:n, c, 0:2 * QK_R].rearrange("p (h two d) -> p h two d", two=2, d=DK // 2)
                cs = T["rope"].rearrange("p (t two d) -> p t two d", t=NT, two=2)[0:n, c]
                for i, (x, f) in enumerate(((0, 0), (1, 1), (0, 1), (1, 0))):
                    ins = dve.tensor_tensor(part[0:n, i], qk[:, :, x, :],
                                            mid(cs[:, f, :], 2 * H, n, 2 * H, DK // 2), ALU.mult)
                chain.then(ins)
                if c:
                    dve.wait_ge(turned, 2 * c)
                dve.tensor_tensor(rr[0:n, :, 0:DK // 2], part[0:n, 0], part[0:n, 1], ALU.subtract)
                dve.tensor_tensor(rr[0:n, :, DK // 2:], part[0:n, 2], part[0:n, 3], ALU.add).then_inc(rotated, 1)
                dve.wait_ge(rotated, c + 1)
                if c:
                    dve.wait_ge(kv, c)
                dve.tensor_tensor(kd[0:n], rr[0:n, H:2 * H], bc(T["ret_kdec_" + k_][0:n], n, H, DK), ALU.mult).then_inc(kd_out, 1)
                dve.wait_ge(q_out, c + 1)
                dve.tensor_tensor(qdT[:, :, 0:n], qT[:, :, 0:n],
                                  T["ret_qdec_" + k_].rearrange("p (h t) -> p h t", h=H), ALU.mult).then_inc(qd_out, 1)
                if sample:
                    dve.wait_ge(qd_out, c + 1)
                    dve.wait_ge(kd_out, c + 1)
                    for h in range(H):
                        dve.tensor_tensor(qz[:, h], mid(qdT[:, h, 0:n], NB, P, NB, n),
                                          T["batch_cols"].rearrange("p (b t) -> p b t", b=NB), ALU.mult).then_inc(masked, 1)
                    for h in range(H):
                        dve.tensor_tensor(kz[0:n, h], mid(kd[0:n, h, :], NB, n, NB, DK),
                                          bc(T["batch_rows"][0:n], n, NB, DK), ALU.mult).then_inc(masked, 1)
                dve.wait_ge(scores, c + 1)
                if c:
                    dve.wait_ge(ydone, c)
                dve.tensor_tensor(prob[0:n, :, 0:n], quarter(bank[2], n)[0:n],
                                  T["ret_mask_" + k_].rearrange("p (h t) -> p h t", h=H)[0:n], ALU.mult).then_inc(probs, 1)
                if not sample:
                    dve.wait_ge(kv, c + 1)
                    dve.wait_ge(ydone, c + 1)
                    for h in range(H):
                        src = bank[5 + h // 2][:, (h % 2) * DV:(h % 2 + 1) * DV]
                        if c == 0:
                            dve.tensor_copy(S[:, h], src).then_inc(new_state, 1)
                        else:
                            dve.scalar_tensor_tensor(out=S[:, h], in0=S[:, h], scalar=cdec[h], in1=src,
                                                     op0=ALU.mult, op1=ALU.add).then_inc(new_state, 1)
                else:
                    dve.wait_ge(ydone, c + 1)
                    for u in range(UNITS):
                        dve.wait_ge(kv, NCH + u + 1)
                        for j in range(4):
                            h, b = u // 2, (u % 2) * 4 + j
                            src = bank[5 + j // 2][:, (j % 2) * DV:(j % 2 + 1) * DV]
                            dve.scalar_tensor_tensor(out=SS[:, h, b], in0=SS[:, h, b], scalar=cdec[H + h], in1=src,
                                                     op0=ALU.mult, op1=ALU.add).then_inc(new_state, 1)
                for h in range(H):
                    ins = dve.bn_stats(stats[0:n, h], bank[3 + h // 2][0:n, (h % 2) * DV:(h % 2 + 1) * DV])
                chain.then(ins)
                for h in range(H):
                    ins = dve.bn_aggr(mv[0:n, h], stats[0:n, h])
                ins.then_inc(var, 1)
                dve.wait_ge(root, c + 1)
                chain.then(dve.reciprocal(rstd[0:n, :], rstd[0:n, :]))
                if c:
                    dve.wait_ge(yturned, 2 * c)
                for h in range(H):
                    ins = dve.tensor_scalar(y[0:n, h], bank[3 + h // 2][0:n, (h % 2) * DV:(h % 2 + 1) * DV],
                                            mv[0:n, h, 0:1], rstd[0:n, h:h + 1], ALU.subtract, ALU.mult)
                chain.then(ins)
                dve.wait_ge(silu, NT)
                dve.tensor_tensor(y[0:n].rearrange("p h v -> p (h v)"), y[0:n].rearrange("p h v -> p (h v)"),
                                  proj[0:n, c, 2 * QK_R + V_R:], ALU.mult).then_inc(yn, 1)
                for half in range(2):
                    dve.wait_ge(yturned, 2 * c + half + 1)
                    k = 4 * half
                    dve.tensor_tensor(yrT[:, k:k + 4, c * P:c * P + n], quarter(bank[7], n),
                                      bc(col["ret_norm_g"][:, k:k + 4], P, 4, n), ALU.mult).then_inc(ykept, 1)

        @block.tensor
        def _(pe):
            for c in range(NT):
                n = rows(c)
                sample = c == NCH
                pe.wait_ge(rotated, c + 1)
                for side in range(2):
                    if c:
                        pe.wait_ge(qd_out, c)
                        pe.wait_ge(k_out, c)
                    for h in range(H):
                        ins = pe.transpose(bank[side][:, h * P:h * P + n], rr[0:n, side * H + h, :], T["ident"][0:n, 0:n])
                    ins.then_inc(turned, 1)
                pe.wait_ge(q_out, c + 1)
                pe.wait_ge(k_out, c + 1)
                if c:
                    pe.wait_ge(probs, c)
                for h in range(H):
                    ins = pe.matmul(bank[2][0:n, h * P:h * P + n], kT[:, h, 0:n], qT[:, h, 0:n], start=True, stop=True)
                ins.then_inc(scores, 1)
                pe.wait_ge(probs, c + 1)
                pe.wait_ge(qd_out, c + 1)
                if c:
                    pe.wait_ge(yn, c)
                    pe.wait_ge(new_state, c * H)
                if sample:
                    pe.wait_ge(masked, 2 * H)
                    pe.wait_ge(states, 16 * H)
                for h in range(H):
                    out = bank[3 + h // 2][0:n, (h % 2) * DV:(h % 2 + 1) * DV]
                    vh = proj[0:n, c, 2 * QK_R + h * DV:2 * QK_R + (h + 1) * DV]
                    ins = pe.matmul(out, prob[0:n, h, 0:n], vh, start=True, stop=c == 0)
                    if sample:
                        for b in range(NB):
                            ins = pe.matmul(out, qz[:, h, b], SS[:, h, b], start=False, stop=b == NB - 1)
                    elif c:
                        ins = pe.matmul(out, qdT[:, h, 0:n], S[:, h], start=False, stop=True)
                ins.then_inc(ydone, 1)
                pe.wait_ge(kd_out, c + 1)
                if not sample:
                    for h in range(H):
                        ins = pe.matmul(bank[5 + h // 2][:, (h % 2) * DV:(h % 2 + 1) * DV], kd[0:n, h],
                                        proj[0:n, c, 2 * QK_R + h * DV:2 * QK_R + (h + 1) * DV], start=True, stop=True)
                    ins.then_inc(kv, 1)
                else:
                    for u in range(UNITS):
                        pe.wait_ge(new_state, NCH * H + 4 * u)
                        for j in range(4):
                            h, b = u // 2, (u % 2) * 4 + j
                            ins = pe.matmul(bank[5 + j // 2][:, (j % 2) * DV:(j % 2 + 1) * DV], kz[0:n, h, b],
                                            proj[0:n, c, 2 * QK_R + h * DV:2 * QK_R + (h + 1) * DV], start=True, stop=True)
                        ins.then_inc(kv, 1)
                pe.wait_ge(yn, c + 1)
                for half in range(2):
                    if c or half:
                        pe.wait_ge(ykept, 2 * c + half)
                    for j in range(4):
                        k = half * 4 + j
                        ins = pe.transpose(bank[7][:, j * P:j * P + n], y[0:n].rearrange("p h v -> p (h v)")[:, k * P:(k + 1) * P],
                                           T["ident"][0:n, 0:n])
                    ins.then_inc(yturned, 1)


def token_tiles_of(half):
    if half == 0:
        return [(0, HALF_TOK, False)]
    return [(HALF_TOK, SEQ - HALF_TOK, False), (SEQ, NS, True)]


def mlstm_projection(env, v, o, kT, qT, gates):
    nc, I, O, A, T, bank, sem = (env[k] for k in ("nc", "I", "O", "A", "T", "bank", "sem"))
    xnT, col = env["xnT"], env["col"]
    PAD = CW - 1
    xm = A.take(KD, PAD + SEQ)
    xs = A.take(KD, NB * (PAD + TS)).rearrange("p k (b t) -> p k b t", b=NB)
    xcT = A.take(KD, TOK)
    NW = 2
    ring = A.take(NW, KD, GRP)
    wif = A.take(KD, 2 * H)
    bias = A.take(2 * H)
    past = A.take(D)
    tails = A.take(KD, (NB + 1) * PAD)
    tail_rows = past
    NTAIL = (NB + 1) * PAD
    small, weights = sem("p3_small"), [sem(f"p3_weights{i}") for i in range(NW)]
    past_turned, past_in, cleared = sem("p3_past_turned"), sem("p3_past_in"), sem("p3_cleared")
    xm_done, xm_copied = sem("p3_xm_done"), sem("p3_xm_copied")
    product, copied = sem("p3_product"), sem("p3_copied")
    if_done, if_kept = sem("p3_if_done"), sem("p3_if_kept")
    own, conv, act_out = sem("p3_own"), sem("p3_conv"), sem("p3_silu")
    tail_in, tail_turned, tail_out = sem("p3_tail_in"), sem("p3_tail_turned"), sem("p3_tail_out")
    q_done, k_done, q_kept, k_kept, stored = (sem("p3_" + n) for n in ("q_done", "k_done", "q_kept", "k_kept", "stored"))
    w_in = I["w_in"].rearrange("(k p) c -> p k c", p=P)
    NG = 3 * D // GRP
    XG = D // GRP
    wq = ring[:, 0].rearrange("p k c -> p (k c)")[:, 0:KD * DH].rearrange("p (k e) -> p k e", k=KD)
    wk = ring[:, 1].rearrange("p k c -> p (k c)")[:, 0:KD * DH].rearrange("p (k e) -> p k e", k=KD)

    with nc.Block() as block:
        @block.sync
        def _(sp):
            for g in range(NW):
                sp.dma_start(ring[:, g], w_in[:, :, C_XM + g * GRP:C_XM + (g + 1) * GRP]).then_inc(weights[g], 16)
            sp.dma_start(past[0:NB * PAD, :], I["state_conv"]).then_inc(small, 16)
            sp.dma_start(wif, w_in[:, :, C_IF:C_IF + 2 * H]).then_inc(small, 16)
            sp.dma_start(bias, I["bias"].broadcast_to([P, 2 * H])).then_inc(small, 16)
            for g in range(NW):
                sp.wait_ge(xm_done, 8 * (g + 1))
                sp.dma_start(ring[:, g], w_in[:, :, C_VM + g * GRP:C_VM + (g + 1) * GRP]).then_inc(weights[g], 16)
            for g in range(NW):
                sp.wait_ge(product, NT * (g + 1))
                sp.dma_start(ring[:, g], w_in[:, :, C_VM + (NW + g) * GRP:C_VM + (NW + g + 1) * GRP]).then_inc(weights[g], 16)
            sp.wait_ge(product, NT * 3)
            sp.dma_start(wq, I["w_mq"].rearrange("h (k p) e -> p (h k) e", p=P)).then_inc(weights[0], 16)
            sp.wait_ge(product, NT * 4)
            sp.dma_start(wk, I["w_mk"].rearrange("h (k p) e -> p (h k) e", p=P)).then_inc(weights[1], 16)
            sp.wait_ge(tail_out, 2)
            sp.dma_start(O["conv_p"], tail_rows[0:PAD, :]).then_inc(stored, 16)
            sp.dma_start(O["conv_s"], tail_rows[PAD:NTAIL, :]).then_inc(stored, 16)
            sp.wait_ge(stored, 32)

        @block.scalar
        def _(act):
            act.wait_ge(cleared, 1)
            for j in range(KD):
                for half in range(2):
                    act.wait_ge(xm_done, 2 * j + half + 1)
                    for t0, m, sample in token_tiles_of(half):
                        src = bank[2 * (j % 2) + half][:, t0 - half * HALF_TOK:t0 - half * HALF_TOK + m]
                        if sample:
                            act.activation(xs[:, j, :, PAD:], src.rearrange("p (b t) -> p b t", b=NB), ACT.Copy).then_inc(xm_copied, 1)
                        else:
                            act.activation(xm[:, j, PAD + t0:PAD + t0 + m], src, ACT.Copy).then_inc(xm_copied, 1)
            for g in range(NG - XG):
                for c in range(NT):
                    n = rows(c)
                    act.wait_ge(product, NT * g + c + 1)
                    if g < XG:
                        act.activation(v[0:n, c, 2 * g:2 * g + 2, 0:DH], bank[c][0:n, :].rearrange("p (h e) -> p h e", h=2),
                                       ACT.Copy).then_inc(copied, 1)
                    else:
                        act.activation(o[0:n, c, (g - XG) * GRP:(g - XG + 1) * GRP], bank[c][0:n, :], ACT.Sigmoid).then_inc(copied, 1)
            act.wait_ge(conv, 1)
            act.activation(xcT.rearrange("p k t -> p (k t)"), xcT.rearrange("p k t -> p (k t)"), ACT.Silu).then_inc(act_out, 1)
            for u in range(2 * KD):
                k, half = u // 2, u % 2
                act.wait_ge(q_done, u + 1)
                act.activation(qT[:, k, half * HALF_TOK:(half + 1) * HALF_TOK], bank[half][:, 0:HALF_TOK], ACT.Copy,
                               scale=DH ** -0.5).then_inc(q_kept, 1)

        @block.vector
        def _(dve):
            chain = Chain(dve, own)
            dve.memset(gates.rearrange("p c g -> p (c g)"), 0.0)
            dve.memset(v[:, :, :, DH], 1.0)
            dve.memset(xm[:, :, 0:PAD], 0.0).then_inc(cleared, 1)
            dve.wait_ge(past_turned, 1)
            dve.tensor_copy(xs[:, :, :, 0:PAD],
                            bank[5][:, 0:KD * NB * PAD].rearrange("p (k b t) -> p k b t", k=KD, b=NB)).then_inc(past_in, 1)
            dve.wait_ge(past_in, 1)
            dve.wait_ge(cleared, 1)
            for j in range(KD):
                dve.wait_ge(xm_copied, 3 * (j + 1))
                out_p = xcT[:, j, 0:SEQ]
                out_s = xcT[:, j, SEQ:].rearrange("p (b t) -> p b t", b=NB)
                for i in range(CW):
                    w = col[f"conv_w{i}"][:, j:j + 1]
                    for out, src in ((out_p, xm[:, j, i:i + SEQ]), (out_s, xs[:, j, :, i:i + TS])):
                        if i == 0:
                            ins = dve.tensor_scalar(out, src, w, col["conv_b"][:, j:j + 1], ALU.mult, ALU.add)
                        else:
                            ins = dve.scalar_tensor_tensor(out=out, in0=src, scalar=w, in1=out, op0=ALU.mult, op1=ALU.add)
                    if j == KD - 1 and i == CW - 1:
                        ins.then_inc(conv, 1)
                    else:
                        chain.then(ins)
            tv = tails.rearrange("p k (b t) -> p k b t", t=PAD)
            dve.tensor_copy(tv[:, :, 0, :], xm[:, :, SEQ:SEQ + PAD])
            dve.tensor_copy(tv[:, :, 1:, :], xs[:, :, :, TS:TS + PAD]).then_inc(tail_in, 1)
            dve.wait_ge(if_done, 1)
            dve.tensor_tensor(gates[:, 0:NCH, :], bank[7][:, 0:NCH * 2 * H].rearrange("p (c g) -> p c g", c=NCH),
                              mid(bias, NCH, P, NCH, 2 * H), ALU.add)
            dve.tensor_tensor(gates[0:NS, NCH, :], bank[7][0:NS, NCH * 2 * H:NT * 2 * H], bias[0:NS], ALU.add).then_inc(if_kept, 1)
            for half in range(2):
                dve.wait_ge(tail_turned, half + 1)
                dve.tensor_copy(tail_rows[0:NTAIL, half * GRP:(half + 1) * GRP], bank[5 + half][0:NTAIL, :]).then_inc(tail_out, 1)
            for u in range(2 * KD):
                k, half = u // 2, u % 2
                dve.wait_ge(k_done, u + 1)
                dve.tensor_copy(kT[:, k, half * HALF_TOK:(half + 1) * HALF_TOK], bank[2 + half][:, 0:HALF_TOK]).then_inc(k_kept, 1)

        @block.tensor
        def _(pe):
            pe.wait_ge(small, 48)
            n = NB * PAD
            for k in range(KD):
                ins = pe.transpose(bank[5][:, k * n:(k + 1) * n], past[0:n, k * P:(k + 1) * P], T["ident"][0:n, 0:n])
            ins.then_inc(past_turned, 1)
            for j in range(KD):
                if j % 4 == 0:
                    pe.wait_ge(weights[j // 4], 16)
                for half in range(2):
                    if j >= 2:
                        pe.wait_ge(xm_copied, 3 * (j - 2) + (1, 3)[half])
                    for k in range(KD):
                        ins = pe.matmul(bank[2 * (j % 2) + half][:, 0:HALF_TOK], ring[:, j // 4, k, (j % 4) * P:(j % 4 + 1) * P],
                                        xnT[:, k, half * HALF_TOK:(half + 1) * HALF_TOK], start=k == 0, stop=k == KD - 1)
                    ins.then_inc(xm_done, 1)
            pe.wait_ge(xm_copied, 3 * KD)
            for c in range(NT):
                m = rows(c)
                for k in range(KD):
                    ins = pe.matmul(bank[7][0:m, c * 2 * H:(c + 1) * 2 * H], xnT[:, k, c * P:c * P + m], wif[:, k, :],
                                    start=k == 0, stop=k == KD - 1)
            ins.then_inc(if_done, 1)
            for g in range(NG - XG):
                pe.wait_ge(weights[g % NW], 16 * (g // NW + 2))
                for c in range(NT):
                    m = rows(c)
                    if g:
                        pe.wait_ge(copied, NT * (g - 1) + c + 1)
                    for k in range(KD):
                        ins = pe.matmul(bank[c][0:m, :], xnT[:, k, c * P:c * P + m], ring[:, g % NW, k, :], start=k == 0, stop=k == KD - 1)
                    ins.then_inc(product, 1)
            pe.wait_ge(past_in, 1)
            pe.wait_ge(tail_in, 1)
            for half in range(2):
                for j in range(4):
                    ins = pe.transpose(bank[5 + half][0:NTAIL, j * P:(j + 1) * P], tails[:, half * 4 + j, :], T["ident"])
                ins.then_inc(tail_turned, 1)
            pe.wait_ge(act_out, 1)
            pe.wait_ge(copied, NT * (NG - XG))
            for g in range(2):
                pe.wait_ge(weights[g], 16 * 4)
            for u in range(2 * KD):
                k, half = u // 2, u % 2
                h, e = k // 2, k % 2
                for w, b0, done, kept in ((wq, 0, q_done, q_kept), (wk, 2, k_done, k_kept)):
                    if u >= 2:
                        pe.wait_ge(kept, u - 1)
                    for d in range(2):
                        ins = pe.matmul(bank[b0 + half][:, 0:HALF_TOK], w[:, 2 * h + d, e * P:(e + 1) * P],
                                        xcT[:, 2 * h + d, half * HALF_TOK:(half + 1) * HALF_TOK], start=d == 0, stop=d == 1)
                    ins.then_inc(done, 1)


def mlstm(env, v, o, kT, qT, gates):
    nc, I, O, A, T, bank, sem = (env[k] for k in ("nc", "I", "O", "A", "T", "bank", "sem"))
    col = env["col"]
    NE = DH + 1
    lf, a, b = A.take(NT, H), A.take(NT, H), A.take(NT, H)
    sp_ = A.take(NT, H)
    m_prev = A.take(2, H)
    m_last = A.take(2, H)
    top_, mb, u, w_prev, floor_ = A.take(H), A.take(2 * H), A.take(H), A.take(H), A.take(H)
    expo, wkd = A.take(2 * H), A.take(2 * H)
    den = A.take(H)
    stats, mv, rstd = A.take(H, 6), A.take(H, 2), A.take(H)
    dA, dM, dW = A.take(H, P), A.take(H, P), A.take(H, P)
    tmp, prob = A.take(H, P), A.take(H, P)
    qh, kw, yb = A.take(H, 2, P), A.take(H, DH), A.take(H, NE)
    Cp = A.take(H, 2, NE)
    Cs = A.take(2, NB, 2 * NE).rearrange("p s b (e n) -> p s b e n", e=2)
    qz = A.take(2, NB, NS)
    n_rows = A.take(DH)
    nT_in, nT_out = A.take(2, NB * H), A.take(2, H + NB * H)
    decm, decB = A.take(NB, H), A.take(NB, H)
    kz = A.take(NB, DH, at=0)
    names = ("small loads0 loads1 stored stored_h0 stored_h1 absolute lf_in lf_done b_done a_done own act_own diagA bcA mx diagM "
             "w_en diagW picked bcM bcW scores kturned expo wkd masked dwT probs qh kw y ycopied kv C_new var root ydone "
             "yturned hm qz kz decm dec_done dec_in n_turned n_in n_out n_out_turned n_out_rows n_col ml").split()
    S = {x: sem("p4_" + x) for x in names}
    C_dram = I["state_C"].rearrange("b h (e p) v -> h p b e v", p=P)
    C_out = O["C_s"].rearrange("b h (e p) v -> h p b e v", p=P)
    qTv = qT.rearrange("p (h e) t -> p h e t", h=H)

    with nc.Block() as block:
        @block.sync
        def _(sp):
            def load(h):
                for e in range(2):
                    sp.dma_start(Cs[:, h % 2, :, e, 0:DH], C_dram[h][:, :, e, :]).then_inc(S[f"loads{h % 2}"], 16)
            sp.dma_start(n_rows[0:NB * H, :], I["state_n"]).then_inc(S["small"], 16)
            for s in range(NB):
                sp.dma_start(m_prev[s * TS:(s + 1) * TS, 1, :], I["state_m"][s:s + 1, :].broadcast_to([TS, H])).then_inc(S["small"], 16)
            load(0)
            load(1)
            sp.wait_ge(S["C_new"], NCH * 2 * H)
            for e in range(2):
                sp.dma_start(O["C_p"].rearrange("h (e p) v -> e p h v", p=P)[e], Cp[:, :, e, 0:DH]).then_inc(S["stored"], 16)
            for h in range(H):
                sp.wait_ge(S["n_col"], h + 1)
                for e in range(2):
                    sp.dma_start(C_out[h][:, :, e, :], Cs[:, h % 2, :, e, 0:DH]).then_inc(S[f"stored_h{h % 2}"], 16)
                if h + 2 < H:
                    sp.wait_ge(S[f"stored_h{h % 2}"], 32 * (h // 2 + 1))
                    load(h + 2)
            sp.wait_ge(S["n_out_rows"], 1)
            sp.dma_start(O["n_p"], n_rows[0:H, :]).then_inc(S["stored"], 16)
            sp.dma_start(O["n_s"], n_rows[H:H + NB * H, :]).then_inc(S["stored"], 16)
            sp.dma_start(O["m_p"], m_last[0:1, 0, :]).then_inc(S["stored"], 16)
            sp.dma_start(O["m_s"], m_last[0:NS:TS, 1, :]).then_inc(S["stored"], 16)
            sp.wait_ge(S["stored"], 16 * 6)
            for i in range(2):
                sp.wait_ge(S[f"stored_h{i}"], 64)

        @block.scalar
        def _(act):
            z = gates[:, :, H:2 * H]
            chain = Chain(act, S["act_own"])
            chain.then(act.activation(sp_, z, ACT.Abs))
            chain.then(act.activation(sp_, sp_, ACT.Exp, scale=-1.0))
            act.activation(sp_, sp_, ACT.Ln, bias=1.0).then_inc(S["absolute"], 1)
            for c in range(NT):
                n = rows(c)
                act.wait_ge(S["mx"], c + 1)
                act.activation(w_prev[0:n], u[0:n], ACT.Exp)
                act.activation(floor_[0:n], mb[0:n, H:2 * H], ACT.Exp, scale=-1.0).then_inc(S["w_en"], 1)
                act.wait_ge(S["expo"], c + 1)
                act.activation(wkd[0:n], expo[0:n], ACT.Exp).then_inc(S["wkd"], 1)
                act.wait_ge(S["masked"], c + 1)
                for h in range(H):
                    act.activation(tmp[0:n, h, 0:n], tmp[0:n, h, 0:n], ACT.Exp, bias=a[0:n, c, h:h + 1]).then_inc(S["dwT"], 1)
                if c:
                    act.wait_ge(S["ydone"], c)
                for h in range(H):
                    act.wait_ge(S["y"], H * c + h + 1)
                    act.activation(yb[0:n, h], bank[6 + h % 2][0:n, 0:NE], ACT.Copy).then_inc(S["ycopied"], 1)
                act.wait_ge(S["var"], c + 1)
                act.activation(rstd[0:n, :], mv[0:n, :, 1], ACT.Sqrt, bias=EPS).then_inc(S["root"], 1)

        @block.vector
        def _(dve):
            chain = Chain(dve, S["own"])
            dve.memset(m_prev[:, 0, :], 0.0)
            dve.wait_ge(S["absolute"], 1)
            dve.scalar_tensor_tensor(out=lf, in0=gates[:, :, H:2 * H], scalar=0.0, in1=sp_, op0=ALU.min,
                                     op1=ALU.subtract).then_inc(S["lf_done"], 1)
            dve.wait_ge(S["small"], 16 * (NB + 1))
            dve.wait_ge(S["n_turned"], 1)
            dve.tensor_copy(nT_in, bank[3][:, 0:2 * NB * H].rearrange("p (e n) -> p e n", e=2)).then_inc(S["n_in"], 1)
            dve.wait_ge(S["b_done"], 1)
            dve.tensor_copy(b[:, 0:NCH, :], bank[0][:, 0:NCH * H].rearrange("p (c h) -> p c h", c=NCH))
            dve.tensor_copy(b[0:NS, NCH, :], bank[0][0:NS, NCH * H:NT * H]).then_inc(S["own"], 1)
            chain.n += 1
            dve.wait_ge(S["own"], chain.n)
            dve.tensor_tensor(a[:, 0:NCH, :], gates[:, 0:NCH, 0:H], b[:, 0:NCH, :], ALU.subtract)
            chain.then(dve.tensor_tensor(a[0:NS, NCH, :], gates[0:NS, NCH, 0:H], b[0:NS, NCH, :], ALU.subtract))
            for c in range(NT):
                n = rows(c)
                sample = c == NCH
                k_ = "s" if sample else "p"
                mp = m_prev[0:n, 1 if sample else 0, :]
                ident = mid(T["ident"][0:n, 0:n], H, n, H, n)
                if c:
                    dve.wait_ge(S["bcA"], c)
                dve.tensor_tensor(dA[0:n, :, 0:n], ident, bc(a[0:n, c, :], n, H, n), ALU.mult).then_inc(S["diagA"], 1)
                dve.wait_ge(S["bcA"], c + 1)
                if c:
                    dve.wait_ge(S["probs"], c)
                chain.then(dve.tensor_tensor(tmp[0:n, :, 0:n], quarter(bank[1], n)[0:n],
                                             mid(T["mask_ts_" + k_][0:n, 0:n], H, n, H, n), ALU.add))
                chain.then(dve.tensor_reduce(top_[0:n], tmp[0:n, :, 0:n], AX, ALU.max))
                if c:
                    dve.wait_ge(S["picked"], c)
                chain.then(dve.tensor_tensor(mb[0:n, 0:H], top_[0:n], mp, ALU.max))
                dve.tensor_tensor(mb[0:n, H:2 * H], mb[0:n, 0:H], b[0:n, c, :], ALU.add)
                dve.tensor_tensor(u[0:n], mp, mb[0:n, 0:H], ALU.subtract).then_inc(S["mx"], 1)
                if c:
                    dve.wait_ge(S["bcM"], c)
                    dve.wait_ge(S["bcW"], c)
                dve.tensor_tensor(dM[0:n, :, 0:n], ident, bc(mb[0:n, 0:H], n, H, n), ALU.mult).then_inc(S["diagM"], 1)
                dve.wait_ge(S["w_en"], c + 1)
                dve.tensor_tensor(dW[0:n, :, 0:n], ident, bc(w_prev[0:n], n, H, n), ALU.mult).then_inc(S["diagW"], 1)
                dve.wait_ge(S["picked"], c + 1)
                dve.tensor_tensor(expo[0:n, 0:H], a[0:n, c, :], bank[0][0:n, 32:32 + H], ALU.subtract)
                dve.tensor_tensor(expo[0:n, H:2 * H], mp, bank[0][0:n, 32:32 + H], ALU.subtract).then_inc(S["expo"], 1)
                dve.tensor_copy(m_last[0:n, 1 if sample else 0, :], bank[0][0:n, 32 + H:32 + 2 * H])
                if not sample:
                    dve.wait_ge(S["expo"], c + 1)
                    dve.tensor_copy(mp, bank[0][0:n, 32 + H:32 + 2 * H]).then_inc(S["ml"], 1)
                dve.wait_ge(S["bcM"], c + 1)
                dve.tensor_tensor(tmp[0:n, :, 0:n], mid(T["mask_st_" + k_][0:n, 0:n], H, n, H, n), quarter(bank[1], n)[0:n],
                                  ALU.subtract).then_inc(S["masked"], 1)
                dve.wait_ge(S["bcW"], c + 1)
                if c:
                    dve.wait_ge(S["y"], H * c)
                for e in range(2):
                    ins = dve.tensor_tensor(qh[:, :, e, 0:n], qTv[:, :, e, c * P:c * P + n], quarter(bank[2], n), ALU.mult)
                ins.then_inc(S["qh"], 1)
                dve.wait_ge(S["wkd"], c + 1)
                if c:
                    dve.wait_ge(S["kv"], 2 * H * c)
                for half in range(2):
                    dve.wait_ge(S["kturned"], 2 * c + half + 1)
                    dve.tensor_tensor(kw[0:n, 2 * half:2 * half + 2], bank[4 + half][0:n, :].rearrange("p (h e) -> p h e", h=2),
                                      bc(wkd[0:n, 2 * half:2 * half + 2], n, 2, DH), ALU.mult).then_inc(S["kw"], 1)
                dve.wait_ge(S["scores"], c + 1)
                dve.wait_ge(S["dwT"], H * (c + 1))
                dve.tensor_tensor(prob[0:n, :, 0:n], quarter(bank[3], n)[0:n], tmp[0:n, :, 0:n], ALU.mult).then_inc(S["probs"], 1)
                if not sample:
                    dve.wait_ge(S["y"], H * (c + 1))
                    for h in range(H):
                        for e in range(2):
                            dve.wait_ge(S["kv"], 2 * H * c + 2 * h + e + 1)
                            if c == 0:
                                dve.tensor_copy(Cp[:, h, e], bank[4 + e][:, 0:NE]).then_inc(S["C_new"], 1)
                            else:
                                dve.scalar_tensor_tensor(out=Cp[:, h, e], in0=Cp[:, h, e], scalar=wkd[:, H + h:H + h + 1],
                                                         in1=bank[4 + e][:, 0:NE], op0=ALU.mult, op1=ALU.add).then_inc(S["C_new"], 1)
                else:
                    dve.tensor_tensor(decm[0:n], bc(T["last_rows"][0:n], n, NB, H), mid(wkd[0:n, H:2 * H], NB, n, NB, H),
                                      ALU.mult).then_inc(S["decm"], 1)
                    dve.wait_ge(S["dec_done"], 1)
                    chain.then(dve.tensor_copy(decB.rearrange("p b h -> p (b h)"), bank[0][:, 64:64 + NB * H]))
                    dve.wait_ge(S["C_new"], NCH * 2 * H)
                    dve.wait_ge(S["n_in"], 1)
                    dve.tensor_copy(nT_out[:, :, 0:H], Cp[:, :, :, DH].rearrange("p h e -> p e h"))
                    n_in_v = nT_in.rearrange("p e (b h) -> p e b h", b=NB)
                    n_out_v = nT_out[:, :, H:].rearrange("p e (b h) -> p e b h", b=NB)
                    for h in range(H):
                        dve.wait_ge(S[f"loads{h % 2}"], 32 * (h // 2 + 1))
                        dve.tensor_copy(Cs[:, h % 2, :, :, DH].rearrange("p b e -> p e b"), n_in_v[:, :, :, h])
                        if h:
                            dve.wait_ge(S["y"], H * NCH + h)
                        dve.tensor_tensor(qz, qh[:, h, :, 0:n].unsqueeze(2).to_broadcast([P, 2, NB, n]),
                                          T["batch_cols"].rearrange("p (b t) -> p b t", b=NB).unsqueeze(1).to_broadcast([P, 2, NB, n]),
                                          ALU.mult).then_inc(S["qz"], 1)
                        dve.tensor_tensor(kz[0:n], mid(kw[0:n, h, :], NB, n, NB, DH), bc(T["batch_rows"][0:n], n, NB, DH),
                                          ALU.mult).then_inc(S["kz"], 1)
                        dve.wait_ge(S["y"], H * NCH + h + 1)
                        for s in range(NB):
                            for e in range(2):
                                dve.wait_ge(S["kv"], 2 * H * NCH + 2 * NB * h + 2 * s + e + 1)
                                dve.scalar_tensor_tensor(out=Cs[:, h % 2, s, e], in0=Cs[:, h % 2, s, e],
                                                         scalar=decB[:, s, h:h + 1], in1=bank[4 + e][:, 0:NE],
                                                         op0=ALU.mult, op1=ALU.add).then_inc(S["C_new"], 1)
                        dve.wait_ge(S["C_new"], 2 * H * NCH + 2 * NB * (h + 1))
                        dve.tensor_copy(n_out_v[:, :, :, h], Cs[:, h % 2, :, :, DH].rearrange("p b e -> p e b")).then_inc(S["n_col"], 1)
                    dve.wait_ge(S["n_out_turned"], 1)
                    dve.tensor_copy(n_rows[0:H + NB * H, :], bank[3][0:H + NB * H, 0:DH]).then_inc(S["n_out_rows"], 1)
                dve.wait_ge(S["ycopied"], H * (c + 1))
                chain.then(dve.scalar_tensor_tensor(out=den[0:n], in0=yb[0:n, :, DH], scalar=-1.0, in1=yb[0:n, :, DH],
                                                    op0=ALU.mult, op1=ALU.max))
                chain.then(dve.tensor_tensor(den[0:n], den[0:n], floor_[0:n], ALU.max))
                chain.then(dve.reciprocal(den[0:n], den[0:n]))
                chain.then(dve.tensor_tensor(yb[0:n, :, 0:DH], yb[0:n, :, 0:DH], bc(den[0:n], n, H, DH), ALU.mult))
                for h in range(H):
                    ins = dve.bn_stats(stats[0:n, h], yb[0:n, h, 0:DH])
                chain.then(ins)
                for h in range(H):
                    ins = dve.bn_aggr(mv[0:n, h], stats[0:n, h])
                ins.then_inc(S["var"], 1)
                dve.wait_ge(S["root"], c + 1)
                chain.then(dve.reciprocal(rstd[0:n, :], rstd[0:n, :]))
                for h in range(H):
                    ins = dve.tensor_scalar(yb[0:n, h, 0:DH], yb[0:n, h, 0:DH], mv[0:n, h, 0:1], rstd[0:n, h:h + 1],
                                            ALU.subtract, ALU.mult)
                chain.then(ins)
                oc = o[0:n, c, :].rearrange("p (h e) -> p h e", h=H)
                dve.tensor_tensor(oc, yb[0:n, :, 0:DH], oc, ALU.mult).then_inc(S["ydone"], 1)
                for half in range(2):
                    dve.wait_ge(S["yturned"], 2 * c + half + 1)
                    k = 4 * half
                    dve.tensor_tensor(qT[:, k:k + 4, c * P:c * P + n], quarter(bank[1 + half], n),
                                      bc(col["mlstm_norm_g"][:, k:k + 4], P, 4, n), ALU.mult).then_inc(S["hm"], 1)

        @block.tensor
        def _(pe):
            pe.wait_ge(S["small"], 16 * (NB + 1))
            for e in range(2):
                ins = pe.transpose(bank[3][:, e * NB * H:(e + 1) * NB * H], n_rows[0:NB * H, e * P:(e + 1) * P],
                                   T["ident"][0:NB * H, 0:NB * H])
            ins.then_inc(S["n_turned"], 1)
            pe.wait_ge(S["lf_done"], 1)
            for c in range(NT):
                n = rows(c)
                ins = pe.matmul(bank[0][0:n, c * H:(c + 1) * H], T["tri_s" if c == NCH else "tri_p"][0:n, 0:n], lf[0:n, c, :],
                                start=True, stop=True)
            ins.then_inc(S["b_done"], 1)
            pe.wait_ge(S["n_in"], 1)
            for c in range(NT):
                n = rows(c)
                sample = c == NCH
                tok = slice(c * P, c * P + n)
                pe.wait_ge(S["diagA"], c + 1)
                if c:
                    pe.wait_ge(S["hm"], 2 * c)
                pe.matmul(quarter(bank[1], n)[0:n], T["ones"][0:n, 0:n], dA[0:n, :, 0:n], start=True, stop=True).then_inc(S["bcA"], 1)
                if c:
                    pe.wait_ge(S["probs"], c)
                for h in range(H):
                    for e in range(2):
                        ins = pe.matmul(bank[3][0:n, h * P:h * P + n], kT[:, 2 * h + e, tok], qT[:, 2 * h + e, tok],
                                        start=e == 0, stop=e == 1)
                ins.then_inc(S["scores"], 1)
                if c:
                    pe.wait_ge(S["C_new"], 2 * H * c)
                for half in range(2):
                    for j in range(4):
                        ins = pe.transpose(bank[4 + half][0:n, j * P:(j + 1) * P], kT[:, 4 * half + j, tok], T["ident"])
                    ins.then_inc(S["kturned"], 1)
                pe.wait_ge(S["mx"], c + 1)
                if c:
                    pe.wait_ge(S["ml"], c)
                pe.matmul(bank[0][0:n, 32:32 + 2 * H], T["pick_s" if sample else "pick_p"][0:n, 0:n], mb[0:n, :],
                          start=True, stop=True).then_inc(S["picked"], 1)
                pe.wait_ge(S["diagM"], c + 1)
                pe.matmul(quarter(bank[1], n)[0:n], T["ones"][0:n, 0:n], dM[0:n, :, 0:n], start=True, stop=True).then_inc(S["bcM"], 1)
                pe.wait_ge(S["diagW"], c + 1)
                pe.matmul(quarter(bank[2], n), T["ones"][0:n, :], dW[0:n, :, 0:n], start=True, stop=True).then_inc(S["bcW"], 1)
                pe.wait_ge(S["probs"], c + 1)
                pe.wait_ge(S["qh"], c + 1)
                if sample:
                    pe.wait_ge(S["decm"], 1)
                    pe.matmul(bank[0][:, 64:64 + NB * H], T["ones"][0:n, :], decm[0:n].rearrange("p b h -> p (b h)"),
                              start=True, stop=True).then_inc(S["dec_done"], 1)
                for h in range(H):
                    out = bank[6 + h % 2][0:n, 0:NE]
                    if c or h >= 2:
                        pe.wait_ge(S["ycopied"], H * c + h - 1)
                    if sample:
                        pe.wait_ge(S["qz"], h + 1)
                    ins = pe.matmul(out, prob[0:n, h, 0:n], v[0:n, c, h, :], start=True, stop=c == 0)
                    if sample:
                        for s in range(NB):
                            for e in range(2):
                                ins = pe.matmul(out, qz[:, e, s], Cs[:, h % 2, s, e], start=False, stop=s == NB - 1 and e == 1)
                    elif c:
                        for e in range(2):
                            ins = pe.matmul(out, qh[:, h, e, 0:n], Cp[:, h, e], start=False, stop=e == 1)
                    ins.then_inc(S["y"], 1)
                    if sample:
                        pe.wait_ge(S["kz"], h + 1)
                        for s in range(NB):
                            for e in range(2):
                                i = 2 * NB * h + 2 * s + e
                                pe.wait_ge(S["kw"], 2 * NT)
                                if i >= 2:
                                    pe.wait_ge(S["C_new"], 2 * H * NCH + i - 1)
                                pe.matmul(bank[4 + e][:, 0:NE], kz[0:n, s, e * P:(e + 1) * P], v[0:n, c, h, :],
                                          start=True, stop=True).then_inc(S["kv"], 1)
                if not sample:
                    pe.wait_ge(S["kw"], 2 * (c + 1))
                    for h in range(H):
                        for e in range(2):
                            if h:
                                pe.wait_ge(S["C_new"], 2 * H * c + 2 * h + e - 1)
                            pe.matmul(bank[4 + e][:, 0:NE], kw[0:n, h, e * P:(e + 1) * P], v[0:n, c, h, :],
                                      start=True, stop=True).then_inc(S["kv"], 1)
                else:
                    pe.wait_ge(S["n_col"], H)
                    for e in range(2):
                        ins = pe.transpose(bank[3][0:H + NB * H, e * P:(e + 1) * P], nT_out[:, e, :], T["ident"])
                    ins.then_inc(S["n_out_turned"], 1)
                pe.wait_ge(S["ydone"], c + 1)
                for half in range(2):
                    for j in range(4):
                        k = 4 * half + j
                        ins = pe.transpose(bank[1 + half][:, j * P:j * P + n], o[0:n, c, k * P:(k + 1) * P], T["ident"][0:n, 0:n])
                    ins.then_inc(S["yturned"], 1)


def merge_and_norm(env, hmT, x1, xn2):
    nc, I, A, T, bank, sem = (env[k] for k in ("nc", "I", "A", "T", "bank", "sem"))
    xnT, yrT = env["xnT"], env["yrT"]
    NG = D // GRP
    KINDS = 4
    ring = A.take(KINDS - 1, KD, GRP)
    slots = [ring[:, i] for i in range(KINDS - 1)] + [env["kT_place"][:, 0:KD * GRP].rearrange("p (k c) -> p k c", k=KD)]
    merged = A.take(NT, D)
    other = A.take(2, GRP)
    junk = other.rearrange("p a b -> p (a b)")
    ms = A.take(NT, 1)
    g_row = slots[2].rearrange("p k c -> p (k c)")[:, 0:D]
    mT = xnT
    xn2T = yrT
    w_in = I["w_in"].rearrange("(k p) c -> p k c", p=P)
    w_of = [w_in[:, :, C_GR:C_GR + D], I["w_br"].rearrange("(k p) c -> p k c", p=P),
            w_in[:, :, C_GM:C_GM + D], I["w_bm"].rearrange("(k p) c -> p k c", p=P)]
    xin, row = sem("p5_x"), sem("p5_row")
    weights = [sem(f"p5_weights{i}") for i in range(KINDS)]
    product = sem("p5_product")
    sig, merge, own = sem("p5_sigmoids"), sem("p5_merged"), sem("p5_own")
    turned, mT_in, out_done, x1_in = sem("p5_turned"), sem("p5_mT"), sem("p5_out"), sem("p5_x1")
    squares, roots, normed, turned2, xn2T_in = (sem("p5_" + n) for n in ("squares", "roots", "normed", "turned2", "xn2T"))

    with nc.Block() as block:
        @block.sync
        def _(sp):
            for k in range(KINDS):
                sp.dma_start(slots[k], w_of[k][:, :, 0:GRP]).then_inc(weights[k], 16)
            sp.dma_start(x1[:, 0:NCH, :], I["x_prompt"].rearrange("(t p) d -> p t d", p=P)).then_inc(xin, 16)
            sp.dma_start(x1[0:NS, NCH, :], I["x_sample"]).then_inc(xin, 16)
            for k in range(KINDS):
                sp.wait_ge(product, KINDS * (NT - 1) + k + 1)
                sp.dma_start(slots[k], w_of[k][:, :, GRP:2 * GRP]).then_inc(weights[k], 16)
            w_out = I["w_out"].rearrange("(k p) c -> p k c", p=P)
            for g in range(NG):
                sp.wait_ge(product, KINDS * (2 * NT - 1) + g + 1)
                sp.dma_start(slots[g], w_out[:, :, g * GRP:(g + 1) * GRP]).then_inc(weights[g], 16)
            sp.wait_ge(product, KINDS * 2 * NT)
            sp.dma_start(g_row, I["norm2_row"].broadcast_to([P, D])).then_inc(row, 16)

        @block.scalar
        def _(act):
            for i in range(NG * NT):
                g, c = i // NT, i % NT
                n = rows(c)
                act.wait_ge(product, KINDS * i + 1)
                act.activation(merged[0:n, c, g * GRP:(g + 1) * GRP], bank[4 * (i % 2)][0:n, :], ACT.Sigmoid).then_inc(sig, 1)
                act.wait_ge(product, KINDS * i + 3)
                if i >= 2:
                    act.wait_ge(merge, i - 1)
                act.activation(other[0:n, i % 2], bank[4 * (i % 2) + 2][0:n, :], ACT.Sigmoid).then_inc(sig, 1)
            for c in range(NT):
                n = rows(c)
                for half in range(2):
                    act.wait_ge(turned, 2 * c + half + 1)
                    act.activation(mT[:, 4 * half:4 * half + 4, c * P:c * P + n], quarter(bank[half], n), ACT.Copy).then_inc(mT_in, 1)
            for c in range(NT):
                n = rows(c)
                act.wait_ge(x1_in, NG * (c + 1))
                if c:
                    act.wait_ge(squares, c)
                act.activation(junk[0:n, :], x1[0:n, c, :], ACT.Square, accum_out=ms[0:n, c, :]).then_inc(squares, 1)
            act.wait_ge(squares, NT)
            for c in range(NT):
                n = rows(c)
                act.activation(ms[0:n, c, :], ms[0:n, c, :], ACT.Sqrt, bias=EPS, scale=1.0 / D).then_inc(roots, 1)
            for c in range(NT):
                n = rows(c)
                for half in range(2):
                    act.wait_ge(turned2, 2 * c + half + 1)
                    act.activation(xn2T[:, 4 * half:4 * half + 4, c * P:c * P + n], quarter(bank[6 + half], n), ACT.Copy).then_inc(xn2T_in, 1)

        @block.vector
        def _(dve):
            chain = Chain(dve, own)
            dve.memset(x1[NS:P, NCH, :], 0.0)
            for i in range(NG * NT):
                g, c = i // NT, i % NT
                n = rows(c)
                m, b0 = merged[0:n, c, g * GRP:(g + 1) * GRP], 4 * (i % 2)
                dve.wait_ge(product, KINDS * i + 4)
                dve.wait_ge(sig, 2 * i + 2)
                dve.tensor_tensor(m, m, bank[b0 + 1][0:n, :], ALU.mult)
                chain.then(dve.tensor_tensor(other[0:n, i % 2], other[0:n, i % 2], bank[b0 + 3][0:n, :], ALU.mult))
                dve.tensor_tensor(m, m, other[0:n, i % 2], ALU.add).then_inc(merge, 1)
            dve.wait_ge(xin, 32)
            for c in range(NT):
                n = rows(c)
                for g in range(NG):
                    dve.wait_ge(out_done, NG * c + g + 1)
                    x = x1[0:n, c, g * GRP:(g + 1) * GRP]
                    dve.tensor_tensor(x, x, bank[2 + (NG * c + g) % 4][0:n, :], ALU.add).then_inc(x1_in, 1)
            dve.wait_ge(row, 16)
            for c in range(NT):
                n = rows(c)
                dve.wait_ge(roots, c + 1)
                chain.then(dve.reciprocal(ms[0:n, c, :], ms[0:n, c, :]))
                dve.scalar_tensor_tensor(out=xn2[0:n, c, :], in0=x1[0:n, c, :], scalar=ms[0:n, c, :], in1=g_row[0:n, :],
                                         op0=ALU.mult, op1=ALU.mult).then_inc(normed, 1)

        @block.tensor
        def _(pe):
            lhs = [xnT, yrT, xnT, hmT]
            for i in range(NG * NT):
                g, c = i // NT, i % NT
                n = rows(c)
                if i >= 2:
                    pe.wait_ge(merge, i - 1)
                for k in range(KINDS):
                    pe.wait_ge(weights[k], 16 * (g + 1))
                    for d in range(KD):
                        ins = pe.matmul(bank[4 * (i % 2) + k][0:n, :], lhs[k][:, d, c * P:c * P + n], slots[k][:, d, :],
                                        start=d == 0, stop=d == KD - 1)
                    ins.then_inc(product, 1)
            pe.wait_ge(merge, NG * NT)
            for c in range(NT):
                def free(half, c=c):
                    if c:
                        pe.wait_ge(mT_in, 2 * (c - 1) + half + 1)
                transpose_tile(pe, merged[:, c, :], T["ident"], bank[0:2], rows(c), turned, free)
            for g in range(NG):
                pe.wait_ge(weights[g], 16 * 3)
            for c in range(NT):
                n = rows(c)
                pe.wait_ge(mT_in, 2 * (c + 1))
                for g in range(NG):
                    i = NG * c + g
                    if i >= 4:
                        pe.wait_ge(x1_in, i - 3)
                    for d in range(KD):
                        ins = pe.matmul(bank[2 + i % 4][0:n, :], mT[:, d, c * P:c * P + n], slots[g][:, d, :],
                                        start=d == 0, stop=d == KD - 1)
                    ins.then_inc(out_done, 1)
            for c in range(NT):
                pe.wait_ge(normed, c + 1)

                def free2(half, c=c):
                    if c:
                        pe.wait_ge(xn2T_in, 2 * (c - 1) + half + 1)
                transpose_tile(pe, xn2[:, c, :], T["ident"], bank[6:8], rows(c), turned2, free2)
    return xn2T


def route(env, x1, xn2, xn2T, table, gate):
    nc, I, A, T, bank, sem = (env[k] for k in ("nc", "I", "A", "T", "bank", "sem"))
    NQ = 2 * PH
    NW = 2
    GQ = GRP // P
    keys = A.take(2, NKEY)
    qpT = A.take(NQ, TOK)
    ring = A.take(NW, KD, GRP)
    s = A.take(NQ, NKEY)
    rest = ring[:, 0].rearrange("p k c -> p (k c)")[:, 0:NQ * NKEY].rearrange("p (q k) -> p q k", q=NQ)
    cand = ring[:, 0].rearrange("p k c -> p (k c)")[:, NQ * NKEY:2 * NQ * NKEY].rearrange("p (h k) -> p h k", h=PH)
    cand_rest = ring[:, 1].rearrange("p k c -> p (k c)")[:, 0:PH * NCAND].rearrange("p (h k) -> p h k", h=PH)
    onehot = ring[:, 1].rearrange("p k c -> p (k c)")[:, PH * NCAND:2 * PH * NCAND].rearrange("p (h k a) -> p h k a", h=PH, k=TOPK)
    vals, picks, picks_f = A.take(NQ, TOPK), A.take(NQ, TOPK), A.take(NQ, TOPK)
    top_s, top_p = A.take(PH, TOPK), A.take(PH, TOPK)
    at, at_f, found = A.take(2, PH * TOPK), A.take(2, PH, TOPK), A.take(2, PH, TOPK)
    w, total = A.take(PH, TOPK), A.take(PH)
    numbers = A.take(PH, TOPK)
    names = "keys own product kept scores s_in tops expos w_done sample moved".split()
    S = {x: sem("p6_" + x) for x in names}
    weights = [sem(f"p6_weights{i}") for i in range(NW)]
    w_pq = I["w_pq"].rearrange("(k p) c -> p k c", p=P)
    NG = NQ // GQ

    with nc.Block() as block:
        @block.sync
        def _(sp):
            for g in range(NW):
                sp.dma_start(ring[:, g], w_pq[:, :, g * GRP:(g + 1) * GRP]).then_inc(weights[g], 16)
            sp.dma_start(keys[:, 0], I["keys1"]).then_inc(S["keys"], 16)
            sp.dma_start(keys[:, 1], I["keys2"]).then_inc(S["keys"], 16)
            for g in range(NW):
                sp.wait_ge(S["product"], 2 * GQ * (g + 1))
                sp.dma_start(ring[:, g], w_pq[:, :, (NW + g) * GRP:(NW + g + 1) * GRP]).then_inc(weights[g], 16)
            sp.wait_ge(S["sample"], 1)
            g0 = NCH * G_TILE
            for half in range(2):
                dst = slice(half * NS, (half + 1) * NS)
                sp.dma_start(table[dst, g0:, :].bitcast(U32), numbers[0:NS, half * G_SAMPLE:(half + 1) * G_SAMPLE, :].bitcast(U32)).then_inc(S["moved"], 16)
                sp.dma_start(gate[dst, g0:, :], w[0:NS, half * G_SAMPLE:(half + 1) * G_SAMPLE, :]).then_inc(S["moved"], 16)
            sp.dma_start(xn2[NS:P, NCH, :], xn2[0:NS, NCH, :]).then_inc(S["moved"], 16)
            sp.wait_ge(S["moved"], 16 * 5)

        @block.scalar
        def _(act):
            for q in range(NQ):
                for half in range(2):
                    act.wait_ge(S["product"], 2 * q + half + 1)
                    act.activation(qpT[:, q, half * HALF_TOK:(half + 1) * HALF_TOK], bank[4 + 2 * (q % 2) + half][:, 0:HALF_TOK],
                                   ACT.Copy).then_inc(S["kept"], 1)
            for c in range(NT):
                n = rows(c)
                if c:
                    act.wait_ge(S["tops"], c)
                for j in range(4):
                    act.wait_ge(S["scores"], 4 * c + j + 1)
                    act.activation(s[0:n, 4 * j:4 * j + 4, :], bank[j][0:n, :].rearrange("p (q k) -> p q k", q=4),
                                   ACT.Copy).then_inc(S["s_in"], 1)
                act.wait_ge(S["expos"], c + 1)
                act.activation(w[0:n], w[0:n], ACT.Exp).then_inc(S["w_done"], 1)

        @block.vector
        def _(dve):
            chain = Chain(dve, S["own"])
            pk, tp = picks.bitcast(U32), top_p.bitcast(U32)

            def top16(n, count, values, places, left, out_v, out_i, last=None):
                for q in range(count):
                    ins = dve.max(out_v[0:n, q, 0:8], values[0:n, q, :])
                chain.then(ins)
                for q in range(count):
                    dve.max_index(out_i[0:n, q, 0:8], out_v[0:n, q, 0:8], values[0:n, q, :])
                    ins = dve.match_replace(left[0:n, q, :], out_v[0:n, q, 0:8], values[0:n, q, :], LOWEST)
                chain.then(ins)
                for q in range(count):
                    ins = dve.max(out_v[0:n, q, 8:16], left[0:n, q, :])
                chain.then(ins)
                for q in range(count):
                    ins = dve.max_index(out_i[0:n, q, 8:16], out_v[0:n, q, 8:16], left[0:n, q, :])
                return ins

            dve.wait_ge(S["product"], 2 * NQ)
            for c in range(NT):
                n = rows(c)
                sample = c == NCH
                dve.wait_ge(S["s_in"], 4 * (c + 1))
                top16(n, NQ, s, None, rest, vals, pk).then_inc(S["tops"], 1)
                dve.wait_ge(S["tops"], c + 1)
                v4 = vals[0:n].rearrange("p (h two) k -> p h two k", two=2)
                dve.tensor_copy(picks_f[0:n], pk[0:n])
                chain.then(dve.tensor_tensor(cand[0:n].rearrange("p h (i j) -> p h i j", i=TOPK),
                                             v4[:, :, 0, :].unsqueeze(3).to_broadcast([n, PH, TOPK, TOPK]),
                                             v4[:, :, 1, :].unsqueeze(2).to_broadcast([n, PH, TOPK, TOPK]), ALU.add))
                chain.then(top16(n, PH, cand, None, cand_rest, top_s, tp))
                atu = at.bitcast(U32)
                flat = tp[0:n].rearrange("p h k -> p (h k)")
                dve.tensor_single_scalar(atu[0:n, 0], flat, 4, ALU.logical_shift_right)
                chain.then(dve.tensor_single_scalar(atu[0:n, 1], flat, 15, ALU.bitwise_and))
                if c:
                    dve.wait_ge(S["w_done"], c)
                dve.tensor_tensor(w[0:n], top_s[0:n], top_s[0:n, :, 0:1].to_broadcast([n, PH, TOPK]), ALU.subtract).then_inc(S["expos"], 1)
                chain.then(dve.tensor_copy(at_f[0:n].rearrange("p t h k -> p t (h k)"), atu[0:n]))
                pf = picks_f[0:n].rearrange("p (h two) k -> p h two k", two=2)
                for t in range(2):
                    chain.then(dve.tensor_tensor(onehot[0:n], at_f[0:n, t].unsqueeze(3).to_broadcast([n, PH, TOPK, TOPK]),
                                                 T["iota16"][0:n].unsqueeze(1).unsqueeze(1).to_broadcast([n, PH, TOPK, TOPK]),
                                                 ALU.is_equal))
                    chain.then(dve.tensor_tensor(onehot[0:n], onehot[0:n],
                                                 pf[:, :, t, :].unsqueeze(2).to_broadcast([n, PH, TOPK, TOPK]), ALU.mult))
                    chain.then(dve.tensor_reduce(found[0:n, t], onehot[0:n], AX, ALU.add))
                e_out = numbers[0:n] if sample else table[:, c * G_TILE:(c + 1) * G_TILE, :]
                g_out = w[0:n] if sample else gate[:, c * G_TILE:(c + 1) * G_TILE, :]
                dve.scalar_tensor_tensor(out=e_out.bitcast(U32), in0=found[0:n, 0], scalar=float(NKEY), in1=found[0:n, 1],
                                         op0=ALU.mult, op1=ALU.add)
                dve.wait_ge(S["w_done"], c + 1)
                chain.then(dve.tensor_reduce(total[0:n], w[0:n], AX, ALU.add))
                chain.then(dve.reciprocal(total[0:n], total[0:n]))
                ins = dve.tensor_tensor(g_out, w[0:n], bc(total[0:n], n, PH, TOPK), ALU.mult)
                if sample:
                    ins.then_inc(S["sample"], 1)
                else:
                    chain.then(ins)

        @block.tensor
        def _(pe):
            for q in range(NQ):
                g = q // GQ
                pe.wait_ge(weights[g % NW], 16 * (g // NW + 1))
                for half in range(2):
                    if q >= 2:
                        pe.wait_ge(S["kept"], 2 * (q - 2) + half + 1)
                    for d in range(KD):
                        ins = pe.matmul(bank[4 + 2 * (q % 2) + half][:, 0:HALF_TOK], ring[:, g % NW, d, (q % GQ) * P:(q % GQ + 1) * P],
                                        xn2T[:, d, half * HALF_TOK:(half + 1) * HALF_TOK], start=d == 0, stop=d == KD - 1)
                    ins.then_inc(S["product"], 1)
            pe.wait_ge(S["kept"], 2 * NQ)
            pe.wait_ge(S["keys"], 32)
            for c in range(NT):
                n = rows(c)
                for j in range(4):
                    if c:
                        pe.wait_ge(S["s_in"], 4 * (c - 1) + j + 1)
                    for i in range(4):
                        q = 4 * j + i
                        ins = pe.matmul(bank[j][0:n, i * P:(i + 1) * P], qpT[:, q, c * P:c * P + n], keys[:, q % 2],
                                        start=True, stop=True)
                    ins.then_inc(S["scores"], 1)


def experts(env, x1, xn2, table, gate):
    nc, I, O, A, T, bank, sem = (env[k] for k in ("nc", "I", "O", "A", "T", "bank", "sem"))
    R = 8
    NDIAG = 4
    u_ring, v_ring = A.take(R, D), A.take(R, D)
    junk = A.take(D)
    stage = A.take(TOPK)
    dots, act_, wts = A.take(TOPK), A.take(TOPK), A.take(TOPK)
    diag = A.take(NDIAG, P)
    g_row = A.take(D)
    ms = A.take(NT, 1)
    u_in, v_in = [sem(f"p7_u_in{i}") for i in range(R)], [sem(f"p7_v_in{i}") for i in range(R)]
    ready, staged = sem("p7_ready"), sem("p7_staged")
    u_used, v_used = sem("p7_u_used"), sem("p7_v_used")
    gelu, weighed, diags, added = sem("p7_gelu"), sem("p7_weighed"), sem("p7_diags"), sem("p7_added")
    own, squares, roots, y_done, stored = (sem("p7_" + n) for n in ("own", "squares", "roots", "y", "stored"))
    gathers = sem("p7_gathers")
    NPG = NCH * G_TILE

    with nc.Block() as block:
        @block.sync
        def _(sp):
            sp.dma_start(g_row, I["normf_row"].broadcast_to([P, D])).then_inc(ready, 16)
            for c in range(NT):
                sp.wait_ge(y_done, c + 1)
                dst = O["y_prompt"][c * P:(c + 1) * P, :] if c < NCH else O["y_sample"]
                sp.dma_start(dst, x1[0:rows(c), c, :]).then_inc(stored, 16)
            sp.wait_ge(stored, 16 * NT)

        @block.gpsimd
        def _(pool):
            idx = stage.bitcast(U32)
            pool.wait_ge(ready, 16)
            with pool.Fori(0, NGRP) as g:
                pool.wait_ge(ready, 16)
                pool.wait_ge(v_used, TOPK * g + R)
                pool.tensor_copy(idx, table.bitcast(U32)[:, bass.ds(g, 1), :].rearrange("p a k -> p (a k)")).then_inc(staged, 1)
                pool.wait_ge(staged, g + 1)
                pool.sem_inc(gathers, 1)
                for ring, arrived, used, rows_of in ((u_ring, u_in, u_used, I["expert_u"]), (v_ring, v_in, v_used, I["expert_v"])):
                    for k in range(TOPK):
                        pool.wait_ge(used, TOPK * g + (k + 1))
                        pool.sem_inc(gathers, 1)
                        pool.indirect_dma_start(ring[:, k % R, :], None, rows_of,
                                                bass.IndirectOffsetOnAxis(idx[:, k:k + 1], 0)).then_inc(arrived[k % R], 16)

        @block.vector
        def _(dve):
            chain = Chain(dve, own)
            dve.memset(ms.rearrange("p a b -> p (a b)"), 0.0).then_inc(u_used, R)

            def group(g, tile):
                for k in range(TOPK):
                    dve.wait_ge(u_in[k % R], 32 * g + (16 * (k // R) + 16))
                    dve.scalar_tensor_tensor(out=junk, in0=u_ring[:, k % R, :], scalar=1.0,
                                             in1=xn2[:, bass.ds(tile, 1), :].rearrange("p a d -> p (a d)"), op0=ALU.mult,
                                             op1=ALU.mult, accum_out=dots[:, k:k + 1]).then_inc(u_used, 1)
                    dve.wait_ge(u_used, TOPK * g + (k + R + 1))
                dve.wait_ge(gelu, g + 1)
                dve.tensor_tensor(wts, act_, gate[:, bass.ds(g, 1), :].rearrange("p a k -> p (a k)"), ALU.mult).then_inc(weighed, 1)
                dve.wait_ge(v_used, TOPK * g + (TOPK + R))
                for j in range(2):
                    x = x1[:, bass.ds(tile, 1), j * GRP:(j + 1) * GRP].rearrange("p a d -> p (a d)")
                    dve.tensor_tensor(x, x, bank[j][:, :], ALU.add).then_inc(added, 1)

            for c in range(NT):
                g0 = c * G_TILE
                with dve.Fori(g0, g0 + (G_TILE if c < NCH else G_SAMPLE)) as g:
                    group(g, c)
            for c in range(NT):
                n = rows(c)
                dve.wait_ge(roots, c + 1)
                chain.then(dve.reciprocal(ms[0:n, c, :], ms[0:n, c, :]))
                dve.scalar_tensor_tensor(out=x1[0:n, c, :], in0=x1[0:n, c, :], scalar=ms[0:n, c, :], in1=g_row[0:n, :],
                                         op0=ALU.mult, op1=ALU.mult).then_inc(y_done, 1)

        @block.scalar
        def _(act):
            act.wait_ge(ready, 16)

            def group(g, spread):
                act.wait_ge(u_used, TOPK * g + (TOPK + R))
                act.activation(act_, dots, ACT.Gelu).then_inc(gelu, 1)
                act.wait_ge(weighed, g + 1)
                for k in range(TOPK):
                    act.wait_ge(v_used, TOPK * g + (k + R - NDIAG + 1))
                    act.activation(diag[:, k % NDIAG, :], spread, ACT.Copy, scale=wts[:, k:k + 1]).then_inc(diags, 1)

            with act.Fori(0, NPG) as g:
                group(g, T["ident"])
            with act.Fori(NPG, NGRP) as g:
                group(g, T["fold2"])
            act.wait_ge(added, 2 * NGRP + 1)
            for c in range(NT):
                n = rows(c)
                if c:
                    act.wait_ge(squares, c)
                act.activation(junk[0:n, :], x1[0:n, c, :], ACT.Square, accum_out=ms[0:n, c, :]).then_inc(squares, 1)
            act.wait_ge(squares, NT)
            for c in range(NT):
                n = rows(c)
                act.activation(ms[0:n, c, :], ms[0:n, c, :], ACT.Sqrt, bias=EPS, scale=1.0 / D).then_inc(roots, 1)

        @block.tensor
        def _(pe):
            pe.sem_inc(v_used, R)
            pe.sem_inc(added, 1)
            with pe.Fori(0, NGRP) as g:
                for k in range(TOPK):
                    if k == 0:
                        pe.wait_ge(added, 2 * g + 1)
                    pe.wait_ge(diags, TOPK * g + (k + 1))
                    pe.wait_ge(v_in[k % R], 32 * g + (16 * (k // R) + 16))
                    for j in range(2):
                        ins = pe.matmul(bank[j][:, :], diag[:, k % NDIAG, :], v_ring[:, k % R, j * GRP:(j + 1) * GRP],
                                        start=k == 0, stop=k == TOPK - 1)
                    ins.then_inc(v_used, 1)


OUTS = {
    "y_prompt": (SEQ, D), "y_sample": (NS, D),
    "ret_p": (H, DK, DV), "C_p": (H, DH, DH), "n_p": (H, DH), "m_p": (1, H), "conv_p": (CW - 1, D),
    "ret_s": (NB, H, DK, DV), "C_s": (NB, H, DH, DH), "n_s": (NB * H, DH), "m_s": (NB, H), "conv_s": (NB * (CW - 1), D),
}
SHAPES = [(1, SEQ, D), (NB, TS, D), (1, 1, H, DK, DV), (1, 1, H, DH, DH), (1, 1, H, DH), (1, 1, H), (1, 1, CW - 1, D),
          (1, NB, H, DK, DV), (1, NB, H, DH, DH), (1, NB, H, DH), (1, NB, H), (1, NB, CW - 1, D)]


def layout(inputs):
    a = {k: np.asarray(v) for k, v in inputs.items()}
    per_channel = [a["norm1_g"][0], a["norm2_g"][0], a["ret_norm_g"][0].reshape(-1), a["mlstm_norm_g"][0].reshape(-1),
                   a["conv_b"][0]] + [a["conv_w"][0, j] for j in range(CW)]
    return {
        "x_prompt": a["x_prompt"][0], "x_sample": a["x_sample"].reshape(NS, D),
        "state_ret": a["state_ret"][0], "state_C": a["state_mlstm_C"][0], "state_n": a["state_mlstm_n"][0].reshape(NB * H, DH),
        "state_m": a["state_mlstm_m"][0], "state_conv": a["state_conv"][0].reshape(NB * (CW - 1), D),
        "w_in": a["w_in"][0], "w_mq": a["w_mq"][0], "w_mk": a["w_mk"][0], "w_br": a["w_br"][0], "w_bm": a["w_bm"][0],
        "w_out": a["w_out"][0], "w_pq": a["w_pq"][0],
        "keys1": np.ascontiguousarray(a["sub_keys1"][0].T), "keys2": np.ascontiguousarray(a["sub_keys2"][0].T),
        "expert_u": a["expert_u"][0], "expert_v": a["expert_v"][0],
        "bias": np.concatenate([a["b_i"], a["b_f"]], 1), "norm2_row": a["norm2_g"], "normf_row": a["norm_f_g"].reshape(1, D),
        "cols": np.ascontiguousarray(np.stack(per_channel).reshape(len(COLS), KD, P).transpose(2, 0, 1)).reshape(P, -1),
        "tables": _TABLES,
    }


def kernel(**inputs):
    import concourse.bacc as _bacc
    from concourse.bass_utils import run_bass_kernel_spmd as _run

    nc = _bacc.Bacc("TRN2", target_bir_lowering=False, num_devices=1)
    arrays = {f"in_{k}": np.ascontiguousarray(v) for k, v in layout(inputs).items()}
    I = {k[3:]: nc.dram_tensor(k, v.shape, mybir.dt.from_np(v.dtype), kind="ExternalInput").ap() for k, v in arrays.items()}
    O = {k: nc.dram_tensor(f"out_{k}", s, F32, kind="ExternalOutput").ap() for k, s in OUTS.items()}
    program(nc, I, O)
    r = _run(nc, [arrays], core_ids=[0])
    return tuple(r.results[0][f"out_{k}"].reshape(s) for k, s in zip(OUTS, SHAPES))
```

```python
import math

import numpy as np

import concourse.bass as bass
from concourse import mybir
from contextlib import ExitStack

F32 = mybir.dt.float32
U32 = mybir.dt.uint32
ACT = mybir.ActivationFunctionType
ALU = mybir.AluOpType
AX = mybir.AxisListType.X

P = 128
D = 1024
KD = D // P
SEQ = 512
NB = 8
TS = 8
NS = NB * TS
NCH = SEQ // P
NT = NCH + 1
TOK = SEQ + NS
HALF_TOK = TOK // 2
PAST = 4096
H = 4
DK = 128
DV = 256
DH = 256
CW = 4
QK_R = H * DK
V_R = H * DV
PH = 8
NKEY = 128
TOPK = 16
NCAND = TOPK * TOPK
NSLOT = PH * TOPK
EPS = 1e-6
NEG = -1.0e30
LOWEST = -3.0e38
GRP = 512
C_QKVG = 0
C_XM = 2 * QK_R + 2 * V_R
C_VM = C_XM + D
C_IF = C_XM + 3 * D
C_GR = C_IF + 2 * H
C_GM = C_GR + D
G_TILE = PH
G_SAMPLE = PH // 2
NGRP = NCH * G_TILE + G_SAMPLE


def _log_gamma():
    return np.log1p(-np.exp2(-5.0 - np.arange(H, dtype=np.float32))).astype(np.float32)


def _tables():
    t = {}
    lg = _log_gamma()
    half = DK // 2
    freqs = np.exp(np.float32(-math.log(10000.0)) * np.arange(half, dtype=np.float32) / np.float32(half)).astype(np.float32)
    pos = np.concatenate([np.arange(SEQ), np.tile(PAST + np.arange(TS), NB)]).astype(np.float32)
    ang = (pos[:, None] * freqs[None, :]).astype(np.float32)
    cs = np.zeros((NT * P, 2, half), np.float32)
    cs[:TOK, 0], cs[:TOK, 1] = np.cos(ang), np.sin(ang)
    t["rope"] = cs.reshape(NT, P, 2 * half).transpose(1, 0, 2).reshape(P, -1)
    i = np.arange(P, dtype=np.float32)
    r = np.arange(NS)
    same = (r[:, None] // TS) == (r[None, :] // TS)
    scale = np.float32(DK ** -0.5)

    def pad(a):
        out = np.zeros((P,) + a.shape[1:], np.float32)
        out[:a.shape[0]] = a
        return out.reshape(P, -1)

    diff = i[None, :] - i[:, None]
    dm = np.where(diff >= 0, np.exp(lg[:, None, None] * np.maximum(diff, 0)), 0) * scale
    t["ret_mask_p"] = dm.transpose(1, 0, 2).reshape(P, -1)
    sdiff = (r[None, :] - r[:, None]).astype(np.float32)
    sok = same & (sdiff >= 0)
    sm = np.where(sok, np.exp(lg[:, None, None] * np.maximum(sdiff, 0)), 0) * scale
    t["ret_mask_s"] = pad(sm.transpose(1, 0, 2))
    t["ret_qdec_p"] = np.broadcast_to((np.exp(lg[:, None] * (i + 1)) * scale).reshape(1, -1), (P, H * P))
    t["ret_qdec_s"] = np.broadcast_to((np.exp(lg[:, None] * (r % TS + 1)) * scale).reshape(1, -1), (P, H * NS))
    t["ret_kdec_p"] = np.exp(lg[None, :] * (P - 1 - i)[:, None])
    t["ret_kdec_s"] = pad(np.exp(lg[None, :] * (TS - 1 - r % TS)[:, None]))
    t["batch_cols"] = np.broadcast_to((r[None, :] // TS == np.arange(NB)[:, None]).astype(np.float32).reshape(1, -1), (P, NB * NS))
    t["batch_rows"] = pad((r[:, None] // TS == np.arange(NB)[None, :]).astype(np.float32))
    t["last_rows"] = pad((r[:, None] == np.arange(NB)[None, :] * TS + TS - 1).astype(np.float32))
    t["tri_p"] = (diff >= 0).astype(np.float32)
    t["tri_s"] = pad(sok.astype(np.float32))
    t["mask_ts_p"] = np.where(diff.T >= 0, 0, NEG)
    t["mask_ts_s"] = pad(np.where(sok.T, 0, NEG))
    t["mask_st_p"] = np.where(diff >= 0, 0, NEG)
    t["mask_st_s"] = pad(np.where(sok, 0, NEG))
    t["pick_p"] = (np.arange(P)[:, None] == P - 1).astype(np.float32) * np.ones((1, P), np.float32)
    t["pick_s"] = pad((r[:, None] == (r[None, :] // TS) * TS + TS - 1).astype(np.float32))
    t["ones"] = np.ones((P, P))
    t["ident"] = np.eye(P)
    t["fold2"] = np.concatenate([np.concatenate([np.eye(NS), np.eye(NS)], 0), np.zeros((P, P - NS))], 1)
    t["iota16"] = np.broadcast_to(np.arange(TOPK, dtype=np.float32)[None, :], (P, TOPK))
    where, at, parts = {}, 0, []
    for k, v in t.items():
        v = np.ascontiguousarray(v, dtype=np.float32)
        where[k] = (at, v.shape[1])
        at += v.shape[1]
        parts.append(v)
    return where, np.concatenate(parts, 1)


_WHERE, _TABLES = _tables()
NTAB = _TABLES.shape[1]

COLS = ["norm1_g", "norm2_g", "ret_norm_g", "mlstm_norm_g", "conv_b", "conv_w0", "conv_w1", "conv_w2", "conv_w3"]


class Arena:

    def __init__(self, tensor, words):
        self.tensor, self.words, self.top = tensor, words, 0

    def take(self, *shape, at=None):
        n = int(np.prod(shape))
        a = self.top if at is None else at
        if at is None:
            self.top += n
        assert a + n <= self.words, (a, n, self.words)
        v = self.tensor[:, a:a + n]
        if len(shape) == 1:
            return v
        names = "abcd"[:len(shape)]
        return v.rearrange("p (" + " ".join(names) + ") -> p " + " ".join(names),
                           **{k: s for k, s in zip(names[1:], shape[1:])})


class Chain:

    def __init__(self, eng, sem):
        self.eng, self.sem, self.n = eng, sem, 0

    def then(self, ins):
        self.n += 1
        ins.then_inc(self.sem, 1)
        self.eng.wait_ge(self.sem, self.n)


def rows(c):
    return P if c < NCH else NS


def bc(ap, *shape):
    return ap.unsqueeze(len(shape) - 1).to_broadcast(list(shape))


def mid(ap, n, *shape):
    return ap.unsqueeze(1).to_broadcast(list(shape))


def program(nc, I, O):
    with ExitStack() as ctx:
        WORDS = 52480
        sbuf = ctx.enter_context(nc.sbuf_tensor("arena", [P, WORDS], F32))
        A = Arena(sbuf, WORDS)
        bank = [ctx.enter_context(nc.psum_tensor(f"bank{i}", [P, GRP], F32)) for i in range(8)]

        tab = A.take(NTAB)
        T = {k: tab[:, a:a + n] for k, (a, n) in _WHERE.items()}
        cols = A.take(len(COLS), KD)
        col = {k: cols[:, i, :] for i, k in enumerate(COLS)}
        xnT = A.take(KD, TOK)
        yrT = A.take(KD, TOK)
        BASE = A.top
        held = []

        def sem(name):
            held.append(nc.alloc_semaphore(name=name))
            return held[-1]

        def give_back():
            with nc.Block() as block:
                @block.gpsimd
                def _(pool):
                    for s in held:
                        pool.sem_clear(s)
            for s in held:
                nc.release_semaphore(s)
            held.clear()

        env = dict(nc=nc, I=I, O=O, A=A, bank=bank, T=T, tab=tab, cols=cols, col=col, xnT=xnT, yrT=yrT, sem=sem)
        proj = A.take(NT, 2 * QK_R + 2 * V_R)
        norm_and_retention_projection(env, proj)
        retention(env, proj)
        A.top = BASE
        v = A.take(NT, H, DH + 1)
        o = A.take(NT, D)
        kT = A.take(KD, TOK)
        qT = A.take(KD, TOK)
        gates = A.take(NT, 2 * H)
        MID = A.top
        mlstm_projection(env, v, o, kT, qT, gates)
        A.top = MID
        mlstm(env, v, o, kT, qT, gates)
        hmT = qT
        give_back()
        A.top = BASE
        x1 = A.take(NT, D)
        xn2 = A.take(NT, D)
        assert A.top <= BASE + NT * H * (DH + 1) + NT * D
        A.top = MID
        env["kT_place"] = kT.rearrange("p k t -> p (k t)")
        xn2T = merge_and_norm(env, hmT, x1, xn2)
        A.top = BASE + 2 * NT * D
        table = A.take(NGRP, TOPK)
        gate = A.take(NGRP, TOPK)
        scores = A.take(NGRP, 2 * NKEY, at=BASE - 2 * KD * TOK)
        query_scores(env, xn2, xn2T, scores)
        A.top = BASE + 2 * NT * D + 2 * NGRP * TOPK
        experts(env, x1, xn2, scores, table, gate)


def transpose_tile(pe, src, ident, banks, n, last_sem, before=None):
    for half in range(2):
        if before:
            before(half)
        for j in range(4):
            k = half * 4 + j
            ins = pe.transpose(banks[half][:, j * P:j * P + n], src[0:n, k * P:(k + 1) * P], ident[0:n, 0:n])
        ins.then_inc(last_sem, 1)


def quarter(b, n):
    return b[:, :].rearrange("p (k t) -> p k t", k=4)[:, :, 0:n]


def norm_and_retention_projection(env, proj):
    nc, I, A, T, bank, sem = (env[k] for k in ("nc", "I", "A", "T", "bank", "sem"))
    xnT, col = env["xnT"], env["col"]
    x = A.take(NT, D)
    junk = A.take(D)
    ms = A.take(NT, 1)
    NW = 2
    ring = A.take(NW, KD, GRP)
    NG = proj.shape[2] // GRP
    tables, loaded = sem("p1_tables"), sem("p1_x_loaded")
    weights = [sem(f"p1_weights{i}") for i in range(NW)]
    squares, roots, normed = sem("p1_squares"), sem("p1_roots"), sem("p1_normed")
    turned, kept = sem("p1_turned"), sem("p1_kept")
    product, copied, own = sem("p1_product"), sem("p1_copied"), sem("p1_own")
    w_in = I["w_in"].rearrange("(k p) c -> p k c", p=P)

    with nc.Block() as block:
        @block.sync
        def _(sp):
            sp.dma_start(x[:, 0:NCH, :], I["x_prompt"].rearrange("(t p) d -> p t d", p=P)).then_inc(loaded, 16)
            sp.dma_start(x[0:NS, NCH, :], I["x_sample"]).then_inc(loaded, 16)
            sp.dma_start(env["tab"], I["tables"]).then_inc(tables, 16)
            sp.dma_start(env["cols"].rearrange("p a b -> p (a b)"), I["cols"]).then_inc(tables, 16)
            for g in range(NW):
                sp.dma_start(ring[:, g], w_in[:, :, g * GRP:(g + 1) * GRP]).then_inc(weights[g], 16)
            with sp.Fori(1, NG // NW) as r:
                for g in range(NW):
                    sp.wait_ge(product, NT * (NW * (r - 1) + g + 1))
                    sp.dma_start(ring[:, g], w_in[:, :, bass.ds((NW * r + g) * GRP, GRP)]).then_inc(weights[g], 16)

        @block.scalar
        def _(act):
            act.wait_ge(loaded, 32)
            for c in range(NT):
                n = rows(c)
                if c:
                    act.wait_ge(squares, c)
                act.activation(junk[0:n, :], x[0:n, c, :], ACT.Square, accum_out=ms[0:n, c, :]).then_inc(squares, 1)
            act.wait_ge(squares, NT)
            for c in range(NT):
                n = rows(c)
                act.activation(ms[0:n, c, :], ms[0:n, c, :], ACT.Sqrt, bias=EPS, scale=1.0 / D).then_inc(roots, 1)
            with act.Fori(0, NG) as g:
                for c in range(NT):
                    n = rows(c)
                    act.wait_ge(product, NT * g + (c + 1))
                    act.activation(proj[0:n, c, bass.ds(g * GRP, GRP)], bank[c][0:n, :], ACT.Copy).then_inc(copied, 1)

        @block.vector
        def _(dve):
            chain = Chain(dve, own)
            for c in range(NT):
                n = rows(c)
                dve.wait_ge(roots, c + 1)
                chain.then(dve.reciprocal(ms[0:n, c, :], ms[0:n, c, :]))
                dve.tensor_scalar(x[0:n, c, :], x[0:n, c, :], ms[0:n, c, :], None, ALU.mult).then_inc(normed, 1)
            dve.wait_ge(tables, 32)
            for c in range(NT):
                n = rows(c)
                for half in range(2):
                    dve.wait_ge(turned, 2 * c + half + 1)
                    k = 4 * half
                    dve.tensor_tensor(xnT[:, k:k + 4, c * P:c * P + n], quarter(bank[6 + half], n),
                                      bc(col["norm1_g"][:, k:k + 4], P, 4, n), ALU.mult).then_inc(kept, 1)

        @block.tensor
        def _(pe):
            pe.wait_ge(tables, 32)
            for c in range(NT):
                pe.wait_ge(normed, c + 1)

                def free(half, c=c):
                    if c:
                        pe.wait_ge(kept, 2 * (c - 1) + half + 1)
                transpose_tile(pe, x[:, c, :], T["ident"], bank[6:8], rows(c), turned, free)
            pe.wait_ge(kept, 2 * NT)
            project_groups(pe, xnT, ring, weights, bank, product, copied, NG, NW)


def project_groups(pe, xT, ring, weights, bank, product, copied, NG, NW):
    def body(r, first):
        for s in range(NW):
            pe.wait_ge(weights[s], 16 * (r + 1))
            for c in range(NT):
                n = rows(c)
                if not (first and s == 0):
                    pe.wait_ge(copied, NT * (NW * r + s - 1) + c + 1)
                for k in range(KD):
                    ins = pe.matmul(bank[c][0:n, :], xT[:, k, c * P:c * P + n], ring[:, s, k, :], start=k == 0, stop=k == KD - 1)
                ins.then_inc(product, 1)
    body(0, True)
    if NG > NW:
        with pe.Fori(1, NG // NW) as r:
            body(r, False)


def retention(env, proj):
    nc, I, O, A, T, bank, sem = (env[k] for k in ("nc", "I", "O", "A", "T", "bank", "sem"))
    yrT, col = env["yrT"], env["col"]
    top = A.top
    A.top = top - (NT * D + D + NT + 2 * KD * GRP)
    rr = A.take(2 * H, DK)
    part = A.take(4, 2 * H, DK // 2)
    qT, kT, qdT = A.take(H, P), A.take(H, P), A.take(H, P)
    kd = A.take(H, DK)
    prob = A.take(H, P)
    S = A.take(H, DV)
    y = A.take(H, DV)
    stats, mv, rstd = A.take(H, 6), A.take(H, 2), A.take(H)
    SS = A.take(H, NB, DV)
    qz = A.take(H, NB, NS)
    kz = A.take(H, NB, DK)
    gamma = np.exp(_log_gamma())
    cdec = [float(np.exp(_log_gamma()[h] * L)) for L in (P, TS) for h in range(H)]

    states, silu = sem("p2_states"), sem("p2_silu")
    own, rotated = sem("p2_own"), sem("p2_rotated")
    turned, q_out, k_out, qd_out = sem("p2_turned"), sem("p2_q_out"), sem("p2_k_out"), sem("p2_qd_out")
    scores, probs, ydone, kv, kd_out = sem("p2_scores"), sem("p2_probs"), sem("p2_y"), sem("p2_kv"), sem("p2_kd")
    new_state, var, root, yn, yturned, ykept = (sem("p2_" + n) for n in ("new_state", "var", "root", "ynormed", "yturned", "ykept"))
    masked, stored = sem("p2_masked"), sem("p2_stored")
    UNITS = 2 * H

    with nc.Block() as block:
        @block.sync
        def _(sp):
            for h in range(H):
                sp.dma_start(SS[:, h], I["state_ret"].rearrange("b h k v -> h k b v")[h]).then_inc(states, 16)
            sp.wait_ge(new_state, NCH * H)
            sp.dma_start(O["ret_p"].rearrange("h k v -> k h v"), S).then_inc(stored, 16)
            for h in range(H):
                sp.wait_ge(new_state, NCH * H + NB * (h + 1))
                sp.dma_start(O["ret_s"].rearrange("b h k v -> h k b v")[h], SS[:, h]).then_inc(stored, 16)
            sp.wait_ge(stored, 16 * (H + 1))

        @block.scalar
        def _(act):
            for c in range(NT):
                n = rows(c)
                g = proj[0:n, c, 2 * QK_R + V_R:]
                act.activation(g, g, ACT.Silu).then_inc(silu, 1)
            for c in range(NT):
                n = rows(c)
                act.wait_ge(turned, 2 * c + 1)
                if c:
                    act.wait_ge(scores, c)
                    act.wait_ge(qd_out, c)
                act.activation(qT[:, :, 0:n], quarter(bank[0], n), ACT.Copy).then_inc(q_out, 1)
                act.wait_ge(turned, 2 * c + 2)
                act.activation(kT[:, :, 0:n], quarter(bank[1], n), ACT.Copy).then_inc(k_out, 1)
                act.wait_ge(var, c + 1)
                act.activation(rstd[0:n, :], mv[0:n, :, 1], ACT.Sqrt, bias=EPS).then_inc(root, 1)

        @block.vector
        def _(dve):
            chain = Chain(dve, own)
            for c in range(NT):
                n = rows(c)
                sample = c == NCH
                k_ = "s" if sample else "p"
                qk = proj[0:n, c, 0:2 * QK_R].rearrange("p (h two d) -> p h two d", two=2, d=DK // 2)
                cs = T["rope"].rearrange("p (t two d) -> p t two d", t=NT, two=2)[0:n, c]
                for i, (x, f) in enumerate(((0, 0), (1, 1), (0, 1), (1, 0))):
                    ins = dve.tensor_tensor(part[0:n, i], qk[:, :, x, :],
                                            mid(cs[:, f, :], 2 * H, n, 2 * H, DK // 2), ALU.mult)
                chain.then(ins)
                if c:
                    dve.wait_ge(turned, 2 * c)
                dve.tensor_tensor(rr[0:n, :, 0:DK // 2], part[0:n, 0], part[0:n, 1], ALU.subtract)
                dve.tensor_tensor(rr[0:n, :, DK // 2:], part[0:n, 2], part[0:n, 3], ALU.add).then_inc(rotated, 1)
                dve.wait_ge(rotated, c + 1)
                if c:
                    dve.wait_ge(kv, c)
                dve.tensor_tensor(kd[0:n], rr[0:n, H:2 * H], bc(T["ret_kdec_" + k_][0:n], n, H, DK), ALU.mult).then_inc(kd_out, 1)
                dve.wait_ge(q_out, c + 1)
                dve.tensor_tensor(qdT[:, :, 0:n], qT[:, :, 0:n],
                                  T["ret_qdec_" + k_].rearrange("p (h t) -> p h t", h=H), ALU.mult).then_inc(qd_out, 1)
                if sample:
                    dve.wait_ge(qd_out, c + 1)
                    dve.wait_ge(kd_out, c + 1)
                    for h in range(H):
                        dve.tensor_tensor(qz[:, h], mid(qdT[:, h, 0:n], NB, P, NB, n),
                                          T["batch_cols"].rearrange("p (b t) -> p b t", b=NB), ALU.mult).then_inc(masked, 1)
                    for h in range(H):
                        dve.tensor_tensor(kz[0:n, h], mid(kd[0:n, h, :], NB, n, NB, DK),
                                          bc(T["batch_rows"][0:n], n, NB, DK), ALU.mult).then_inc(masked, 1)
                dve.wait_ge(scores, c + 1)
                if c:
                    dve.wait_ge(ydone, c)
                dve.tensor_tensor(prob[0:n, :, 0:n], quarter(bank[2], n)[0:n],
                                  T["ret_mask_" + k_].rearrange("p (h t) -> p h t", h=H)[0:n], ALU.mult).then_inc(probs, 1)
                if not sample:
                    dve.wait_ge(kv, c + 1)
                    dve.wait_ge(ydone, c + 1)
                    for h in range(H):
                        src = bank[5 + h // 2][:, (h % 2) * DV:(h % 2 + 1) * DV]
                        if c == 0:
                            dve.tensor_copy(S[:, h], src).then_inc(new_state, 1)
                        else:
                            dve.scalar_tensor_tensor(out=S[:, h], in0=S[:, h], scalar=cdec[h], in1=src,
                                                     op0=ALU.mult, op1=ALU.add).then_inc(new_state, 1)
                else:
                    dve.wait_ge(ydone, c + 1)
                    for u in range(UNITS):
                        dve.wait_ge(kv, NCH + u + 1)
                        for j in range(4):
                            h, b = u // 2, (u % 2) * 4 + j
                            src = bank[5 + j // 2][:, (j % 2) * DV:(j % 2 + 1) * DV]
                            dve.scalar_tensor_tensor(out=SS[:, h, b], in0=SS[:, h, b], scalar=cdec[H + h], in1=src,
                                                     op0=ALU.mult, op1=ALU.add).then_inc(new_state, 1)
                for h in range(H):
                    ins = dve.bn_stats(stats[0:n, h], bank[3 + h // 2][0:n, (h % 2) * DV:(h % 2 + 1) * DV])
                chain.then(ins)
                for h in range(H):
                    ins = dve.bn_aggr(mv[0:n, h], stats[0:n, h])
                ins.then_inc(var, 1)
                dve.wait_ge(root, c + 1)
                chain.then(dve.reciprocal(rstd[0:n, :], rstd[0:n, :]))
                if c:
                    dve.wait_ge(yturned, 2 * c)
                for h in range(H):
                    ins = dve.tensor_scalar(y[0:n, h], bank[3 + h // 2][0:n, (h % 2) * DV:(h % 2 + 1) * DV],
                                            mv[0:n, h, 0:1], rstd[0:n, h:h + 1], ALU.subtract, ALU.mult)
                chain.then(ins)
                dve.wait_ge(silu, NT)
                dve.tensor_tensor(y[0:n].rearrange("p h v -> p (h v)"), y[0:n].rearrange("p h v -> p (h v)"),
                                  proj[0:n, c, 2 * QK_R + V_R:], ALU.mult).then_inc(yn, 1)
                for half in range(2):
                    dve.wait_ge(yturned, 2 * c + half + 1)
                    k = 4 * half
                    dve.tensor_tensor(yrT[:, k:k + 4, c * P:c * P + n], quarter(bank[7], n),
                                      bc(col["ret_norm_g"][:, k:k + 4], P, 4, n), ALU.mult).then_inc(ykept, 1)

        @block.tensor
        def _(pe):
            for c in range(NT):
                n = rows(c)
                sample = c == NCH
                pe.wait_ge(rotated, c + 1)
                for side in range(2):
                    if c:
                        pe.wait_ge(qd_out, c)
                        pe.wait_ge(k_out, c)
                    for h in range(H):
                        ins = pe.transpose(bank[side][:, h * P:h * P + n], rr[0:n, side * H + h, :], T["ident"][0:n, 0:n])
                    ins.then_inc(turned, 1)
                pe.wait_ge(q_out, c + 1)
                pe.wait_ge(k_out, c + 1)
                if c:
                    pe.wait_ge(probs, c)
                for h in range(H):
                    ins = pe.matmul(bank[2][0:n, h * P:h * P + n], kT[:, h, 0:n], qT[:, h, 0:n], start=True, stop=True)
                ins.then_inc(scores, 1)
                pe.wait_ge(probs, c + 1)
                pe.wait_ge(qd_out, c + 1)
                if c:
                    pe.wait_ge(yn, c)
                    pe.wait_ge(new_state, c * H)
                if sample:
                    pe.wait_ge(masked, 2 * H)
                    pe.wait_ge(states, 16 * H)
                for h in range(H):
                    out = bank[3 + h // 2][0:n, (h % 2) * DV:(h % 2 + 1) * DV]
                    vh = proj[0:n, c, 2 * QK_R + h * DV:2 * QK_R + (h + 1) * DV]
                    ins = pe.matmul(out, prob[0:n, h, 0:n], vh, start=True, stop=c == 0)
                    if sample:
                        for b in range(NB):
                            ins = pe.matmul(out, qz[:, h, b], SS[:, h, b], start=False, stop=b == NB - 1)
                    elif c:
                        ins = pe.matmul(out, qdT[:, h, 0:n], S[:, h], start=False, stop=True)
                ins.then_inc(ydone, 1)
                pe.wait_ge(kd_out, c + 1)
                if not sample:
                    for h in range(H):
                        ins = pe.matmul(bank[5 + h // 2][:, (h % 2) * DV:(h % 2 + 1) * DV], kd[0:n, h],
                                        proj[0:n, c, 2 * QK_R + h * DV:2 * QK_R + (h + 1) * DV], start=True, stop=True)
                    ins.then_inc(kv, 1)
                else:
                    for u in range(UNITS):
                        pe.wait_ge(new_state, NCH * H + 4 * u)
                        for j in range(4):
                            h, b = u // 2, (u % 2) * 4 + j
                            ins = pe.matmul(bank[5 + j // 2][:, (j % 2) * DV:(j % 2 + 1) * DV], kz[0:n, h, b],
                                            proj[0:n, c, 2 * QK_R + h * DV:2 * QK_R + (h + 1) * DV], start=True, stop=True)
                        ins.then_inc(kv, 1)
                pe.wait_ge(yn, c + 1)
                for half in range(2):
                    if c or half:
                        pe.wait_ge(ykept, 2 * c + half)
                    for j in range(4):
                        k = half * 4 + j
                        ins = pe.transpose(bank[7][:, j * P:j * P + n], y[0:n].rearrange("p h v -> p (h v)")[:, k * P:(k + 1) * P],
                                           T["ident"][0:n, 0:n])
                    ins.then_inc(yturned, 1)


def token_tiles_of(half):
    if half == 0:
        return [(0, HALF_TOK, False)]
    return [(HALF_TOK, SEQ - HALF_TOK, False), (SEQ, NS, True)]


def mlstm_projection(env, v, o, kT, qT, gates):
    nc, I, O, A, T, bank, sem = (env[k] for k in ("nc", "I", "O", "A", "T", "bank", "sem"))
    xnT, col = env["xnT"], env["col"]
    PAD = CW - 1
    xm = A.take(KD, PAD + SEQ)
    xs = A.take(KD, NB * (PAD + TS)).rearrange("p k (b t) -> p k b t", b=NB)
    xcT = A.take(KD, TOK)
    NW = 2
    ring = A.take(NW, KD, GRP)
    wif = A.take(KD, 2 * H)
    bias = A.take(2 * H)
    past = A.take(D)
    tails = A.take(KD, (NB + 1) * PAD)
    tail_rows = past
    NTAIL = (NB + 1) * PAD
    small, weights = sem("p3_small"), [sem(f"p3_weights{i}") for i in range(NW)]
    past_turned, past_in, cleared = sem("p3_past_turned"), sem("p3_past_in"), sem("p3_cleared")
    xm_done, xm_copied = sem("p3_xm_done"), sem("p3_xm_copied")
    product, copied = sem("p3_product"), sem("p3_copied")
    if_done, if_kept = sem("p3_if_done"), sem("p3_if_kept")
    own, conv, act_out = sem("p3_own"), sem("p3_conv"), sem("p3_silu")
    tail_in, tail_turned, tail_out = sem("p3_tail_in"), sem("p3_tail_turned"), sem("p3_tail_out")
    q_done, k_done, q_kept, k_kept, stored = (sem("p3_" + n) for n in ("q_done", "k_done", "q_kept", "k_kept", "stored"))
    w_in = I["w_in"].rearrange("(k p) c -> p k c", p=P)
    NG = 3 * D // GRP
    XG = D // GRP
    wq = ring[:, 0].rearrange("p k c -> p (k c)")[:, 0:KD * DH].rearrange("p (k e) -> p k e", k=KD)
    wk = ring[:, 1].rearrange("p k c -> p (k c)")[:, 0:KD * DH].rearrange("p (k e) -> p k e", k=KD)

    with nc.Block() as block:
        @block.sync
        def _(sp):
            for g in range(NW):
                sp.dma_start(ring[:, g], w_in[:, :, C_XM + g * GRP:C_XM + (g + 1) * GRP]).then_inc(weights[g], 16)
            sp.dma_start(past[0:NB * PAD, :], I["state_conv"]).then_inc(small, 16)
            sp.dma_start(wif, w_in[:, :, C_IF:C_IF + 2 * H]).then_inc(small, 16)
            sp.dma_start(bias, I["bias"].broadcast_to([P, 2 * H])).then_inc(small, 16)
            for g in range(NW):
                sp.wait_ge(xm_done, 8 * (g + 1))
                sp.dma_start(ring[:, g], w_in[:, :, C_VM + g * GRP:C_VM + (g + 1) * GRP]).then_inc(weights[g], 16)
            for g in range(NW):
                sp.wait_ge(product, NT * (g + 1))
                sp.dma_start(ring[:, g], w_in[:, :, C_VM + (NW + g) * GRP:C_VM + (NW + g + 1) * GRP]).then_inc(weights[g], 16)
            sp.wait_ge(product, NT * 3)
            sp.dma_start(wq, I["w_mq"].rearrange("h (k p) e -> p (h k) e", p=P)).then_inc(weights[0], 16)
            sp.wait_ge(product, NT * 4)
            sp.dma_start(wk, I["w_mk"].rearrange("h (k p) e -> p (h k) e", p=P)).then_inc(weights[1], 16)
            sp.wait_ge(tail_out, 2)
            sp.dma_start(O["conv_p"], tail_rows[0:PAD, :]).then_inc(stored, 16)
            sp.dma_start(O["conv_s"], tail_rows[PAD:NTAIL, :]).then_inc(stored, 16)
            sp.wait_ge(stored, 32)

        @block.scalar
        def _(act):
            act.wait_ge(cleared, 1)
            for j in range(KD):
                for half in range(2):
                    act.wait_ge(xm_done, 2 * j + half + 1)
                    for t0, m, sample in token_tiles_of(half):
                        src = bank[2 * (j % 2) + half][:, t0 - half * HALF_TOK:t0 - half * HALF_TOK + m]
                        if sample:
                            act.activation(xs[:, j, :, PAD:], src.rearrange("p (b t) -> p b t", b=NB), ACT.Copy).then_inc(xm_copied, 1)
                        else:
                            act.activation(xm[:, j, PAD + t0:PAD + t0 + m], src, ACT.Copy).then_inc(xm_copied, 1)
            for g in range(NG - XG):
                for c in range(NT):
                    n = rows(c)
                    act.wait_ge(product, NT * g + c + 1)
                    if g < XG:
                        act.activation(v[0:n, c, 2 * g:2 * g + 2, 0:DH], bank[c][0:n, :].rearrange("p (h e) -> p h e", h=2),
                                       ACT.Copy).then_inc(copied, 1)
                    else:
                        act.activation(o[0:n, c, (g - XG) * GRP:(g - XG + 1) * GRP], bank[c][0:n, :], ACT.Sigmoid).then_inc(copied, 1)
            act.wait_ge(conv, 1)
            act.activation(xcT.rearrange("p k t -> p (k t)"), xcT.rearrange("p k t -> p (k t)"), ACT.Silu).then_inc(act_out, 1)
            for u in range(2 * KD):
                k, half = u // 2, u % 2
                act.wait_ge(q_done, u + 1)
                act.activation(qT[:, k, half * HALF_TOK:(half + 1) * HALF_TOK], bank[half][:, 0:HALF_TOK], ACT.Copy,
                               scale=DH ** -0.5).then_inc(q_kept, 1)

        @block.vector
        def _(dve):
            chain = Chain(dve, own)
            dve.memset(gates.rearrange("p c g -> p (c g)"), 0.0)
            dve.memset(v[:, :, :, DH], 1.0)
            dve.memset(xm[:, :, 0:PAD], 0.0).then_inc(cleared, 1)
            dve.wait_ge(past_turned, 1)
            dve.tensor_copy(xs[:, :, :, 0:PAD],
                            bank[5][:, 0:KD * NB * PAD].rearrange("p (k b t) -> p k b t", k=KD, b=NB)).then_inc(past_in, 1)
            dve.wait_ge(past_in, 1)
            dve.wait_ge(cleared, 1)
            for j in range(KD):
                dve.wait_ge(xm_copied, 3 * (j + 1))
                out_p = xcT[:, j, 0:SEQ]
                out_s = xcT[:, j, SEQ:].rearrange("p (b t) -> p b t", b=NB)
                for i in range(CW):
                    w = col[f"conv_w{i}"][:, j:j + 1]
                    for out, src in ((out_p, xm[:, j, i:i + SEQ]), (out_s, xs[:, j, :, i:i + TS])):
                        if i == 0:
                            ins = dve.tensor_scalar(out, src, w, col["conv_b"][:, j:j + 1], ALU.mult, ALU.add)
                        else:
                            ins = dve.scalar_tensor_tensor(out=out, in0=src, scalar=w, in1=out, op0=ALU.mult, op1=ALU.add)
                    if j == KD - 1 and i == CW - 1:
                        ins.then_inc(conv, 1)
                    else:
                        chain.then(ins)
            tv = tails.rearrange("p k (b t) -> p k b t", t=PAD)
            dve.tensor_copy(tv[:, :, 0, :], xm[:, :, SEQ:SEQ + PAD])
            dve.tensor_copy(tv[:, :, 1:, :], xs[:, :, :, TS:TS + PAD]).then_inc(tail_in, 1)
            dve.wait_ge(if_done, 1)
            dve.tensor_tensor(gates[:, 0:NCH, :], bank[7][:, 0:NCH * 2 * H].rearrange("p (c g) -> p c g", c=NCH),
                              mid(bias, NCH, P, NCH, 2 * H), ALU.add)
            dve.tensor_tensor(gates[0:NS, NCH, :], bank[7][0:NS, NCH * 2 * H:NT * 2 * H], bias[0:NS], ALU.add).then_inc(if_kept, 1)
            for half in range(2):
                dve.wait_ge(tail_turned, half + 1)
                dve.tensor_copy(tail_rows[0:NTAIL, half * GRP:(half + 1) * GRP], bank[5 + half][0:NTAIL, :]).then_inc(tail_out, 1)
            for u in range(2 * KD):
                k, half = u // 2, u % 2
                dve.wait_ge(k_done, u + 1)
                dve.tensor_copy(kT[:, k, half * HALF_TOK:(half + 1) * HALF_TOK], bank[2 + half][:, 0:HALF_TOK]).then_inc(k_kept, 1)

        @block.tensor
        def _(pe):
            pe.wait_ge(small, 48)
            n = NB * PAD
            for k in range(KD):
                ins = pe.transpose(bank[5][:, k * n:(k + 1) * n], past[0:n, k * P:(k + 1) * P], T["ident"][0:n, 0:n])
            ins.then_inc(past_turned, 1)
            for j in range(KD):
                if j % 4 == 0:
                    pe.wait_ge(weights[j // 4], 16)
                for half in range(2):
                    if j >= 2:
                        pe.wait_ge(xm_copied, 3 * (j - 2) + (1, 3)[half])
                    for k in range(KD):
                        ins = pe.matmul(bank[2 * (j % 2) + half][:, 0:HALF_TOK], ring[:, j // 4, k, (j % 4) * P:(j % 4 + 1) * P],
                                        xnT[:, k, half * HALF_TOK:(half + 1) * HALF_TOK], start=k == 0, stop=k == KD - 1)
                    ins.then_inc(xm_done, 1)
            pe.wait_ge(xm_copied, 3 * KD)
            for c in range(NT):
                m = rows(c)
                for k in range(KD):
                    ins = pe.matmul(bank[7][0:m, c * 2 * H:(c + 1) * 2 * H], xnT[:, k, c * P:c * P + m], wif[:, k, :],
                                    start=k == 0, stop=k == KD - 1)
            ins.then_inc(if_done, 1)
            for g in range(NG - XG):
                pe.wait_ge(weights[g % NW], 16 * (g // NW + 2))
                for c in range(NT):
                    m = rows(c)
                    if g:
                        pe.wait_ge(copied, NT * (g - 1) + c + 1)
                    for k in range(KD):
                        ins = pe.matmul(bank[c][0:m, :], xnT[:, k, c * P:c * P + m], ring[:, g % NW, k, :], start=k == 0, stop=k == KD - 1)
                    ins.then_inc(product, 1)
            pe.wait_ge(past_in, 1)
            pe.wait_ge(tail_in, 1)
            for half in range(2):
                for j in range(4):
                    ins = pe.transpose(bank[5 + half][0:NTAIL, j * P:(j + 1) * P], tails[:, half * 4 + j, :], T["ident"])
                ins.then_inc(tail_turned, 1)
            pe.wait_ge(act_out, 1)
            pe.wait_ge(copied, NT * (NG - XG))
            for g in range(2):
                pe.wait_ge(weights[g], 16 * 4)
            for u in range(2 * KD):
                k, half = u // 2, u % 2
                h, e = k // 2, k % 2
                for w, b0, done, kept in ((wq, 0, q_done, q_kept), (wk, 2, k_done, k_kept)):
                    if u >= 2:
                        pe.wait_ge(kept, u - 1)
                    for d in range(2):
                        ins = pe.matmul(bank[b0 + half][:, 0:HALF_TOK], w[:, 2 * h + d, e * P:(e + 1) * P],
                                        xcT[:, 2 * h + d, half * HALF_TOK:(half + 1) * HALF_TOK], start=d == 0, stop=d == 1)
                    ins.then_inc(done, 1)


def mlstm(env, v, o, kT, qT, gates):
    nc, I, O, A, T, bank, sem = (env[k] for k in ("nc", "I", "O", "A", "T", "bank", "sem"))
    col = env["col"]
    NE = DH + 1
    lf, a, b = A.take(NT, H), A.take(NT, H), A.take(NT, H)
    sp_ = A.take(NT, H)
    m_prev = A.take(2, H)
    m_last = A.take(2, H)
    top_, mb, u, w_prev, floor_ = A.take(H), A.take(2 * H), A.take(H), A.take(H), A.take(H)
    expo, wkd = A.take(2 * H), A.take(2 * H)
    den = A.take(H)
    stats, mv, rstd = A.take(H, 6), A.take(H, 2), A.take(H)
    dA, dM, dW = A.take(H, P), A.take(H, P), A.take(H, P)
    tmp, prob = A.take(H, P), A.take(H, P)
    qh, kw, yb = A.take(H, 2, P), A.take(H, DH), A.take(H, NE)
    Cp = A.take(H, 2, NE)
    Cs = A.take(2, NB, 2 * NE).rearrange("p s b (e n) -> p s b e n", e=2)
    qz = A.take(2, NB, NS)
    n_rows = A.take(DH)
    nT_in, nT_out = A.take(2, NB * H), A.take(2, H + NB * H)
    decm, decB = A.take(NB, H), A.take(NB, H)
    kz = A.take(NB, DH, at=0)
    names = ("small loads0 loads1 stored stored_h0 stored_h1 absolute lf_in lf_done b_done a_done own act_own diagA bcA mx diagM "
             "w_en diagW picked bcM bcW scores kturned expo wkd masked dwT probs qh kw y ycopied kv C_new var root ydone "
             "yturned hm qz kz decm dec_done dec_in n_turned n_in n_out n_out_turned n_out_rows n_col ml").split()
    S = {x: sem("p4_" + x) for x in names}
    C_dram = I["state_C"].rearrange("b h (e p) v -> h p b e v", p=P)
    C_out = O["C_s"].rearrange("b h (e p) v -> h p b e v", p=P)
    qTv = qT.rearrange("p (h e) t -> p h e t", h=H)

    with nc.Block() as block:
        @block.sync
        def _(sp):
            def load(h):
                for e in range(2):
                    sp.dma_start(Cs[:, h % 2, :, e, 0:DH], C_dram[h][:, :, e, :]).then_inc(S[f"loads{h % 2}"], 16)
            sp.dma_start(n_rows[0:NB * H, :], I["state_n"]).then_inc(S["small"], 16)
            for s in range(NB):
                sp.dma_start(m_prev[s * TS:(s + 1) * TS, 1, :], I["state_m"][s:s + 1, :].broadcast_to([TS, H])).then_inc(S["small"], 16)
            load(0)
            load(1)
            sp.wait_ge(S["C_new"], NCH * 2 * H)
            for e in range(2):
                sp.dma_start(O["C_p"].rearrange("h (e p) v -> e p h v", p=P)[e], Cp[:, :, e, 0:DH]).then_inc(S["stored"], 16)
            for h in range(H):
                sp.wait_ge(S["n_col"], h + 1)
                for e in range(2):
                    sp.dma_start(C_out[h][:, :, e, :], Cs[:, h % 2, :, e, 0:DH]).then_inc(S[f"stored_h{h % 2}"], 16)
                if h + 2 < H:
                    sp.wait_ge(S[f"stored_h{h % 2}"], 32 * (h // 2 + 1))
                    load(h + 2)
            sp.wait_ge(S["n_out_rows"], 1)
            sp.dma_start(O["n_p"], n_rows[0:H, :]).then_inc(S["stored"], 16)
            sp.dma_start(O["n_s"], n_rows[H:H + NB * H, :]).then_inc(S["stored"], 16)
            sp.dma_start(O["m_p"], m_last[0:1, 0, :]).then_inc(S["stored"], 16)
            sp.dma_start(O["m_s"], m_last[0:NS:TS, 1, :]).then_inc(S["stored"], 16)
            sp.wait_ge(S["stored"], 16 * 6)
            for i in range(2):
                sp.wait_ge(S[f"stored_h{i}"], 64)

        @block.scalar
        def _(act):
            z = gates[:, :, H:2 * H]
            chain = Chain(act, S["act_own"])
            chain.then(act.activation(sp_, z, ACT.Abs))
            chain.then(act.activation(sp_, sp_, ACT.Exp, scale=-1.0))
            act.activation(sp_, sp_, ACT.Ln, bias=1.0).then_inc(S["absolute"], 1)
            for c in range(NT):
                n = rows(c)
                act.wait_ge(S["mx"], c + 1)
                act.activation(w_prev[0:n], u[0:n], ACT.Exp)
                act.activation(floor_[0:n], mb[0:n, H:2 * H], ACT.Exp, scale=-1.0).then_inc(S["w_en"], 1)
                act.wait_ge(S["expo"], c + 1)
                act.activation(wkd[0:n], expo[0:n], ACT.Exp).then_inc(S["wkd"], 1)
                act.wait_ge(S["masked"], c + 1)
                for h in range(H):
                    act.activation(tmp[0:n, h, 0:n], tmp[0:n, h, 0:n], ACT.Exp, bias=a[0:n, c, h:h + 1]).then_inc(S["dwT"], 1)
                if c:
                    act.wait_ge(S["ydone"], c)
                for h in range(H):
                    act.wait_ge(S["y"], H * c + h + 1)
                    act.activation(yb[0:n, h], bank[6 + h % 2][0:n, 0:NE], ACT.Copy).then_inc(S["ycopied"], 1)
                act.wait_ge(S["var"], c + 1)
                act.activation(rstd[0:n, :], mv[0:n, :, 1], ACT.Sqrt, bias=EPS).then_inc(S["root"], 1)

        @block.vector
        def _(dve):
            chain = Chain(dve, S["own"])
            dve.memset(m_prev[:, 0, :], 0.0)
            dve.wait_ge(S["absolute"], 1)
            dve.scalar_tensor_tensor(out=lf, in0=gates[:, :, H:2 * H], scalar=0.0, in1=sp_, op0=ALU.min,
                                     op1=ALU.subtract).then_inc(S["lf_done"], 1)
            dve.wait_ge(S["small"], 16 * (NB + 1))
            dve.wait_ge(S["n_turned"], 1)
            dve.tensor_copy(nT_in, bank[3][:, 0:2 * NB * H].rearrange("p (e n) -> p e n", e=2)).then_inc(S["n_in"], 1)
            dve.wait_ge(S["b_done"], 1)
            dve.tensor_copy(b[:, 0:NCH, :], bank[0][:, 0:NCH * H].rearrange("p (c h) -> p c h", c=NCH))
            dve.tensor_copy(b[0:NS, NCH, :], bank[0][0:NS, NCH * H:NT * H]).then_inc(S["own"], 1)
            chain.n += 1
            dve.wait_ge(S["own"], chain.n)
            dve.tensor_tensor(a[:, 0:NCH, :], gates[:, 0:NCH, 0:H], b[:, 0:NCH, :], ALU.subtract)
            chain.then(dve.tensor_tensor(a[0:NS, NCH, :], gates[0:NS, NCH, 0:H], b[0:NS, NCH, :], ALU.subtract))
            for c in range(NT):
                n = rows(c)
                sample = c == NCH
                k_ = "s" if sample else "p"
                mp = m_prev[0:n, 1 if sample else 0, :]
                ident = mid(T["ident"][0:n, 0:n], H, n, H, n)
                if c:
                    dve.wait_ge(S["bcA"], c)
                dve.tensor_tensor(dA[0:n, :, 0:n], ident, bc(a[0:n, c, :], n, H, n), ALU.mult).then_inc(S["diagA"], 1)
                dve.wait_ge(S["bcA"], c + 1)
                if c:
                    dve.wait_ge(S["probs"], c)
                chain.then(dve.tensor_tensor(tmp[0:n, :, 0:n], quarter(bank[1], n)[0:n],
                                             mid(T["mask_ts_" + k_][0:n, 0:n], H, n, H, n), ALU.add))
                chain.then(dve.tensor_reduce(top_[0:n], tmp[0:n, :, 0:n], AX, ALU.max))
                if c:
                    dve.wait_ge(S["picked"], c)
                chain.then(dve.tensor_tensor(mb[0:n, 0:H], top_[0:n], mp, ALU.max))
                dve.tensor_tensor(mb[0:n, H:2 * H], mb[0:n, 0:H], b[0:n, c, :], ALU.add)
                dve.tensor_tensor(u[0:n], mp, mb[0:n, 0:H], ALU.subtract).then_inc(S["mx"], 1)
                if c:
                    dve.wait_ge(S["bcM"], c)
                    dve.wait_ge(S["bcW"], c)
                dve.tensor_tensor(dM[0:n, :, 0:n], ident, bc(mb[0:n, 0:H], n, H, n), ALU.mult).then_inc(S["diagM"], 1)
                dve.wait_ge(S["w_en"], c + 1)
                dve.tensor_tensor(dW[0:n, :, 0:n], ident, bc(w_prev[0:n], n, H, n), ALU.mult).then_inc(S["diagW"], 1)
                dve.wait_ge(S["picked"], c + 1)
                dve.tensor_tensor(expo[0:n, 0:H], a[0:n, c, :], bank[0][0:n, 32:32 + H], ALU.subtract)
                dve.tensor_tensor(expo[0:n, H:2 * H], mp, bank[0][0:n, 32:32 + H], ALU.subtract).then_inc(S["expo"], 1)
                dve.tensor_copy(m_last[0:n, 1 if sample else 0, :], bank[0][0:n, 32 + H:32 + 2 * H])
                if not sample:
                    dve.wait_ge(S["expo"], c + 1)
                    dve.tensor_copy(mp, bank[0][0:n, 32 + H:32 + 2 * H]).then_inc(S["ml"], 1)
                dve.wait_ge(S["bcM"], c + 1)
                dve.tensor_tensor(tmp[0:n, :, 0:n], mid(T["mask_st_" + k_][0:n, 0:n], H, n, H, n), quarter(bank[1], n)[0:n],
                                  ALU.subtract).then_inc(S["masked"], 1)
                dve.wait_ge(S["bcW"], c + 1)
                if c:
                    dve.wait_ge(S["y"], H * c)
                for e in range(2):
                    ins = dve.tensor_tensor(qh[:, :, e, 0:n], qTv[:, :, e, c * P:c * P + n], quarter(bank[2], n), ALU.mult)
                ins.then_inc(S["qh"], 1)
                dve.wait_ge(S["wkd"], c + 1)
                if c:
                    dve.wait_ge(S["kv"], 2 * H * c)
                for half in range(2):
                    dve.wait_ge(S["kturned"], 2 * c + half + 1)
                    dve.tensor_tensor(kw[0:n, 2 * half:2 * half + 2], bank[4 + half][0:n, :].rearrange("p (h e) -> p h e", h=2),
                                      bc(wkd[0:n, 2 * half:2 * half + 2], n, 2, DH), ALU.mult).then_inc(S["kw"], 1)
                dve.wait_ge(S["scores"], c + 1)
                dve.wait_ge(S["dwT"], H * (c + 1))
                dve.tensor_tensor(prob[0:n, :, 0:n], quarter(bank[3], n)[0:n], tmp[0:n, :, 0:n], ALU.mult).then_inc(S["probs"], 1)
                if not sample:
                    dve.wait_ge(S["y"], H * (c + 1))
                    for h in range(H):
                        for e in range(2):
                            dve.wait_ge(S["kv"], 2 * H * c + 2 * h + e + 1)
                            if c == 0:
                                dve.tensor_copy(Cp[:, h, e], bank[4 + e][:, 0:NE]).then_inc(S["C_new"], 1)
                            else:
                                dve.scalar_tensor_tensor(out=Cp[:, h, e], in0=Cp[:, h, e], scalar=wkd[:, H + h:H + h + 1],
                                                         in1=bank[4 + e][:, 0:NE], op0=ALU.mult, op1=ALU.add).then_inc(S["C_new"], 1)
                else:
                    dve.tensor_tensor(decm[0:n], bc(T["last_rows"][0:n], n, NB, H), mid(wkd[0:n, H:2 * H], NB, n, NB, H),
                                      ALU.mult).then_inc(S["decm"], 1)
                    dve.wait_ge(S["dec_done"], 1)
                    chain.then(dve.tensor_copy(decB.rearrange("p b h -> p (b h)"), bank[0][:, 64:64 + NB * H]))
                    dve.wait_ge(S["C_new"], NCH * 2 * H)
                    dve.wait_ge(S["n_in"], 1)
                    dve.tensor_copy(nT_out[:, :, 0:H], Cp[:, :, :, DH].rearrange("p h e -> p e h"))
                    n_in_v = nT_in.rearrange("p e (b h) -> p e b h", b=NB)
                    n_out_v = nT_out[:, :, H:].rearrange("p e (b h) -> p e b h", b=NB)
                    for h in range(H):
                        dve.wait_ge(S[f"loads{h % 2}"], 32 * (h // 2 + 1))
                        dve.tensor_copy(Cs[:, h % 2, :, :, DH].rearrange("p b e -> p e b"), n_in_v[:, :, :, h])
                        if h:
                            dve.wait_ge(S["y"], H * NCH + h)
                        dve.tensor_tensor(qz, qh[:, h, :, 0:n].unsqueeze(2).to_broadcast([P, 2, NB, n]),
                                          T["batch_cols"].rearrange("p (b t) -> p b t", b=NB).unsqueeze(1).to_broadcast([P, 2, NB, n]),
                                          ALU.mult).then_inc(S["qz"], 1)
                        dve.tensor_tensor(kz[0:n], mid(kw[0:n, h, :], NB, n, NB, DH), bc(T["batch_rows"][0:n], n, NB, DH),
                                          ALU.mult).then_inc(S["kz"], 1)
                        dve.wait_ge(S["y"], H * NCH + h + 1)
                        for s in range(NB):
                            for e in range(2):
                                dve.wait_ge(S["kv"], 2 * H * NCH + 2 * NB * h + 2 * s + e + 1)
                                dve.scalar_tensor_tensor(out=Cs[:, h % 2, s, e], in0=Cs[:, h % 2, s, e],
                                                         scalar=decB[:, s, h:h + 1], in1=bank[4 + e][:, 0:NE],
                                                         op0=ALU.mult, op1=ALU.add).then_inc(S["C_new"], 1)
                        dve.wait_ge(S["C_new"], 2 * H * NCH + 2 * NB * (h + 1))
                        dve.tensor_copy(n_out_v[:, :, :, h], Cs[:, h % 2, :, :, DH].rearrange("p b e -> p e b")).then_inc(S["n_col"], 1)
                    dve.wait_ge(S["n_out_turned"], 1)
                    dve.tensor_copy(n_rows[0:H + NB * H, :], bank[3][0:H + NB * H, 0:DH]).then_inc(S["n_out_rows"], 1)
                dve.wait_ge(S["ycopied"], H * (c + 1))
                chain.then(dve.scalar_tensor_tensor(out=den[0:n], in0=yb[0:n, :, DH], scalar=-1.0, in1=yb[0:n, :, DH],
                                                    op0=ALU.mult, op1=ALU.max))
                chain.then(dve.tensor_tensor(den[0:n], den[0:n], floor_[0:n], ALU.max))
                chain.then(dve.reciprocal(den[0:n], den[0:n]))
                chain.then(dve.tensor_tensor(yb[0:n, :, 0:DH], yb[0:n, :, 0:DH], bc(den[0:n], n, H, DH), ALU.mult))
                for h in range(H):
                    ins = dve.bn_stats(stats[0:n, h], yb[0:n, h, 0:DH])
                chain.then(ins)
                for h in range(H):
                    ins = dve.bn_aggr(mv[0:n, h], stats[0:n, h])
                ins.then_inc(S["var"], 1)
                dve.wait_ge(S["root"], c + 1)
                chain.then(dve.reciprocal(rstd[0:n, :], rstd[0:n, :]))
                for h in range(H):
                    ins = dve.tensor_scalar(yb[0:n, h, 0:DH], yb[0:n, h, 0:DH], mv[0:n, h, 0:1], rstd[0:n, h:h + 1],
                                            ALU.subtract, ALU.mult)
                chain.then(ins)
                oc = o[0:n, c, :].rearrange("p (h e) -> p h e", h=H)
                dve.tensor_tensor(oc, yb[0:n, :, 0:DH], oc, ALU.mult).then_inc(S["ydone"], 1)
                for half in range(2):
                    dve.wait_ge(S["yturned"], 2 * c + half + 1)
                    k = 4 * half
                    dve.tensor_tensor(qT[:, k:k + 4, c * P:c * P + n], quarter(bank[1 + half], n),
                                      bc(col["mlstm_norm_g"][:, k:k + 4], P, 4, n), ALU.mult).then_inc(S["hm"], 1)

        @block.tensor
        def _(pe):
            pe.wait_ge(S["small"], 16 * (NB + 1))
            for e in range(2):
                ins = pe.transpose(bank[3][:, e * NB * H:(e + 1) * NB * H], n_rows[0:NB * H, e * P:(e + 1) * P],
                                   T["ident"][0:NB * H, 0:NB * H])
            ins.then_inc(S["n_turned"], 1)
            pe.wait_ge(S["lf_done"], 1)
            for c in range(NT):
                n = rows(c)
                ins = pe.matmul(bank[0][0:n, c * H:(c + 1) * H], T["tri_s" if c == NCH else "tri_p"][0:n, 0:n], lf[0:n, c, :],
                                start=True, stop=True)
            ins.then_inc(S["b_done"], 1)
            pe.wait_ge(S["n_in"], 1)
            for c in range(NT):
                n = rows(c)
                sample = c == NCH
                tok = slice(c * P, c * P + n)
                pe.wait_ge(S["diagA"], c + 1)
                if c:
                    pe.wait_ge(S["hm"], 2 * c)
                pe.matmul(quarter(bank[1], n)[0:n], T["ones"][0:n, 0:n], dA[0:n, :, 0:n], start=True, stop=True).then_inc(S["bcA"], 1)
                if c:
                    pe.wait_ge(S["probs"], c)
                for h in range(H):
                    for e in range(2):
                        ins = pe.matmul(bank[3][0:n, h * P:h * P + n], kT[:, 2 * h + e, tok], qT[:, 2 * h + e, tok],
                                        start=e == 0, stop=e == 1)
                ins.then_inc(S["scores"], 1)
                if c:
                    pe.wait_ge(S["C_new"], 2 * H * c)
                for half in range(2):
                    for j in range(4):
                        ins = pe.transpose(bank[4 + half][0:n, j * P:(j + 1) * P], kT[:, 4 * half + j, tok], T["ident"])
                    ins.then_inc(S["kturned"], 1)
                pe.wait_ge(S["mx"], c + 1)
                if c:
                    pe.wait_ge(S["ml"], c)
                pe.matmul(bank[0][0:n, 32:32 + 2 * H], T["pick_s" if sample else "pick_p"][0:n, 0:n], mb[0:n, :],
                          start=True, stop=True).then_inc(S["picked"], 1)
                pe.wait_ge(S["diagM"], c + 1)
                pe.matmul(quarter(bank[1], n)[0:n], T["ones"][0:n, 0:n], dM[0:n, :, 0:n], start=True, stop=True).then_inc(S["bcM"], 1)
                pe.wait_ge(S["diagW"], c + 1)
                pe.matmul(quarter(bank[2], n), T["ones"][0:n, :], dW[0:n, :, 0:n], start=True, stop=True).then_inc(S["bcW"], 1)
                pe.wait_ge(S["probs"], c + 1)
                pe.wait_ge(S["qh"], c + 1)
                if sample:
                    pe.wait_ge(S["decm"], 1)
                    pe.matmul(bank[0][:, 64:64 + NB * H], T["ones"][0:n, :], decm[0:n].rearrange("p b h -> p (b h)"),
                              start=True, stop=True).then_inc(S["dec_done"], 1)
                for h in range(H):
                    out = bank[6 + h % 2][0:n, 0:NE]
                    if c or h >= 2:
                        pe.wait_ge(S["ycopied"], H * c + h - 1)
                    if sample:
                        pe.wait_ge(S["qz"], h + 1)
                    ins = pe.matmul(out, prob[0:n, h, 0:n], v[0:n, c, h, :], start=True, stop=c == 0)
                    if sample:
                        for s in range(NB):
                            for e in range(2):
                                ins = pe.matmul(out, qz[:, e, s], Cs[:, h % 2, s, e], start=False, stop=s == NB - 1 and e == 1)
                    elif c:
                        for e in range(2):
                            ins = pe.matmul(out, qh[:, h, e, 0:n], Cp[:, h, e], start=False, stop=e == 1)
                    ins.then_inc(S["y"], 1)
                    if sample:
                        pe.wait_ge(S["kz"], h + 1)
                        for s in range(NB):
                            for e in range(2):
                                i = 2 * NB * h + 2 * s + e
                                pe.wait_ge(S["kw"], 2 * NT)
                                if i >= 2:
                                    pe.wait_ge(S["C_new"], 2 * H * NCH + i - 1)
                                pe.matmul(bank[4 + e][:, 0:NE], kz[0:n, s, e * P:(e + 1) * P], v[0:n, c, h, :],
                                          start=True, stop=True).then_inc(S["kv"], 1)
                if not sample:
                    pe.wait_ge(S["kw"], 2 * (c + 1))
                    for h in range(H):
                        for e in range(2):
                            if h:
                                pe.wait_ge(S["C_new"], 2 * H * c + 2 * h + e - 1)
                            pe.matmul(bank[4 + e][:, 0:NE], kw[0:n, h, e * P:(e + 1) * P], v[0:n, c, h, :],
                                      start=True, stop=True).then_inc(S["kv"], 1)
                else:
                    pe.wait_ge(S["n_col"], H)
                    for e in range(2):
                        ins = pe.transpose(bank[3][0:H + NB * H, e * P:(e + 1) * P], nT_out[:, e, :], T["ident"])
                    ins.then_inc(S["n_out_turned"], 1)
                pe.wait_ge(S["ydone"], c + 1)
                for half in range(2):
                    for j in range(4):
                        k = 4 * half + j
                        ins = pe.transpose(bank[1 + half][:, j * P:j * P + n], o[0:n, c, k * P:(k + 1) * P], T["ident"][0:n, 0:n])
                    ins.then_inc(S["yturned"], 1)


def merge_and_norm(env, hmT, x1, xn2):
    nc, I, A, T, bank, sem = (env[k] for k in ("nc", "I", "A", "T", "bank", "sem"))
    xnT, yrT = env["xnT"], env["yrT"]
    NG = D // GRP
    KINDS = 4
    ring = A.take(KINDS - 1, KD, GRP)
    slots = [ring[:, i] for i in range(KINDS - 1)] + [env["kT_place"][:, 0:KD * GRP].rearrange("p (k c) -> p k c", k=KD)]
    merged = A.take(NT, D)
    other = A.take(2, GRP)
    junk = other.rearrange("p a b -> p (a b)")
    ms = A.take(NT, 1)
    g_row = slots[2].rearrange("p k c -> p (k c)")[:, 0:D]
    mT = xnT
    xn2T = yrT
    w_in = I["w_in"].rearrange("(k p) c -> p k c", p=P)
    w_of = [w_in[:, :, C_GR:C_GR + D], I["w_br"].rearrange("(k p) c -> p k c", p=P),
            w_in[:, :, C_GM:C_GM + D], I["w_bm"].rearrange("(k p) c -> p k c", p=P)]
    xin, row = sem("p5_x"), sem("p5_row")
    weights = [sem(f"p5_weights{i}") for i in range(KINDS)]
    product = sem("p5_product")
    sig, merge, own = sem("p5_sigmoids"), sem("p5_merged"), sem("p5_own")
    turned, mT_in, out_done, x1_in = sem("p5_turned"), sem("p5_mT"), sem("p5_out"), sem("p5_x1")
    squares, roots, normed, turned2, xn2T_in = (sem("p5_" + n) for n in ("squares", "roots", "normed", "turned2", "xn2T"))

    with nc.Block() as block:
        @block.sync
        def _(sp):
            for k in range(KINDS):
                sp.dma_start(slots[k], w_of[k][:, :, 0:GRP]).then_inc(weights[k], 16)
            sp.dma_start(x1[:, 0:NCH, :], I["x_prompt"].rearrange("(t p) d -> p t d", p=P)).then_inc(xin, 16)
            sp.dma_start(x1[0:NS, NCH, :], I["x_sample"]).then_inc(xin, 16)
            for k in range(KINDS):
                sp.wait_ge(product, KINDS * (NT - 1) + k + 1)
                sp.dma_start(slots[k], w_of[k][:, :, GRP:2 * GRP]).then_inc(weights[k], 16)
            w_out = I["w_out"].rearrange("(k p) c -> p k c", p=P)
            for g in range(NG):
                sp.wait_ge(product, KINDS * (2 * NT - 1) + g + 1)
                sp.dma_start(slots[g], w_out[:, :, g * GRP:(g + 1) * GRP]).then_inc(weights[g], 16)
            sp.wait_ge(product, KINDS * 2 * NT)
            sp.dma_start(g_row, I["norm2_row"].broadcast_to([P, D])).then_inc(row, 16)

        @block.scalar
        def _(act):
            for i in range(NG * NT):
                g, c = i // NT, i % NT
                n = rows(c)
                act.wait_ge(product, KINDS * i + 1)
                act.activation(merged[0:n, c, g * GRP:(g + 1) * GRP], bank[4 * (i % 2)][0:n, :], ACT.Sigmoid).then_inc(sig, 1)
                act.wait_ge(product, KINDS * i + 3)
                if i >= 2:
                    act.wait_ge(merge, i - 1)
                act.activation(other[0:n, i % 2], bank[4 * (i % 2) + 2][0:n, :], ACT.Sigmoid).then_inc(sig, 1)
            for c in range(NT):
                n = rows(c)
                for half in range(2):
                    act.wait_ge(turned, 2 * c + half + 1)
                    act.activation(mT[:, 4 * half:4 * half + 4, c * P:c * P + n], quarter(bank[half], n), ACT.Copy).then_inc(mT_in, 1)
            for c in range(NT):
                n = rows(c)
                act.wait_ge(x1_in, NG * (c + 1))
                if c:
                    act.wait_ge(squares, c)
                act.activation(junk[0:n, :], x1[0:n, c, :], ACT.Square, accum_out=ms[0:n, c, :]).then_inc(squares, 1)
            act.wait_ge(squares, NT)
            for c in range(NT):
                n = rows(c)
                act.activation(ms[0:n, c, :], ms[0:n, c, :], ACT.Sqrt, bias=EPS, scale=1.0 / D).then_inc(roots, 1)
            for c in range(NT):
                n = rows(c)
                for half in range(2):
                    act.wait_ge(turned2, 2 * c + half + 1)
                    act.activation(xn2T[:, 4 * half:4 * half + 4, c * P:c * P + n], quarter(bank[6 + half], n), ACT.Copy).then_inc(xn2T_in, 1)

        @block.vector
        def _(dve):
            chain = Chain(dve, own)
            dve.memset(x1[NS:P, NCH, :], 0.0)
            for i in range(NG * NT):
                g, c = i // NT, i % NT
                n = rows(c)
                m, b0 = merged[0:n, c, g * GRP:(g + 1) * GRP], 4 * (i % 2)
                dve.wait_ge(product, KINDS * i + 4)
                dve.wait_ge(sig, 2 * i + 2)
                dve.tensor_tensor(m, m, bank[b0 + 1][0:n, :], ALU.mult)
                chain.then(dve.tensor_tensor(other[0:n, i % 2], other[0:n, i % 2], bank[b0 + 3][0:n, :], ALU.mult))
                dve.tensor_tensor(m, m, other[0:n, i % 2], ALU.add).then_inc(merge, 1)
            dve.wait_ge(xin, 32)
            for c in range(NT):
                n = rows(c)
                for g in range(NG):
                    dve.wait_ge(out_done, NG * c + g + 1)
                    x = x1[0:n, c, g * GRP:(g + 1) * GRP]
                    dve.tensor_tensor(x, x, bank[2 + (NG * c + g) % 4][0:n, :], ALU.add).then_inc(x1_in, 1)
            dve.wait_ge(row, 16)
            for c in range(NT):
                n = rows(c)
                dve.wait_ge(roots, c + 1)
                chain.then(dve.reciprocal(ms[0:n, c, :], ms[0:n, c, :]))
                dve.scalar_tensor_tensor(out=xn2[0:n, c, :], in0=x1[0:n, c, :], scalar=ms[0:n, c, :], in1=g_row[0:n, :],
                                         op0=ALU.mult, op1=ALU.mult).then_inc(normed, 1)

        @block.tensor
        def _(pe):
            lhs = [xnT, yrT, xnT, hmT]
            for i in range(NG * NT):
                g, c = i // NT, i % NT
                n = rows(c)
                if i >= 2:
                    pe.wait_ge(merge, i - 1)
                for k in range(KINDS):
                    pe.wait_ge(weights[k], 16 * (g + 1))
                    for d in range(KD):
                        ins = pe.matmul(bank[4 * (i % 2) + k][0:n, :], lhs[k][:, d, c * P:c * P + n], slots[k][:, d, :],
                                        start=d == 0, stop=d == KD - 1)
                    ins.then_inc(product, 1)
            pe.wait_ge(merge, NG * NT)
            for c in range(NT):
                def free(half, c=c):
                    if c:
                        pe.wait_ge(mT_in, 2 * (c - 1) + half + 1)
                transpose_tile(pe, merged[:, c, :], T["ident"], bank[0:2], rows(c), turned, free)
            for g in range(NG):
                pe.wait_ge(weights[g], 16 * 3)
            for c in range(NT):
                n = rows(c)
                pe.wait_ge(mT_in, 2 * (c + 1))
                for g in range(NG):
                    i = NG * c + g
                    if i >= 4:
                        pe.wait_ge(x1_in, i - 3)
                    for d in range(KD):
                        ins = pe.matmul(bank[2 + i % 4][0:n, :], mT[:, d, c * P:c * P + n], slots[g][:, d, :],
                                        start=d == 0, stop=d == KD - 1)
                    ins.then_inc(out_done, 1)
            for c in range(NT):
                pe.wait_ge(normed, c + 1)

                def free2(half, c=c):
                    if c:
                        pe.wait_ge(xn2T_in, 2 * (c - 1) + half + 1)
                transpose_tile(pe, xn2[:, c, :], T["ident"], bank[6:8], rows(c), turned2, free2)
    return xn2T


def query_scores(env, xn2, xn2T, scores):
    nc, I, A, bank, sem = (env[k] for k in ("nc", "I", "A", "bank", "sem"))
    NQ = 2 * PH
    NW = 2
    GQ = GRP // P
    keys = A.take(2, NKEY)
    qpT = A.take(NQ, TOK)
    ring = A.take(NW, KD, GRP)
    loaded, product, kept, scored, stored, moved = (sem("p6_" + n) for n in ("keys", "product", "kept", "scored", "stored", "moved"))
    weights = [sem(f"p6_weights{i}") for i in range(NW)]
    w_pq = I["w_pq"].rearrange("(k p) c -> p k c", p=P)

    with nc.Block() as block:
        @block.sync
        def _(sp):
            for g in range(NW):
                sp.dma_start(ring[:, g], w_pq[:, :, g * GRP:(g + 1) * GRP]).then_inc(weights[g], 16)
            sp.dma_start(keys[:, 0], I["keys1"]).then_inc(loaded, 16)
            sp.dma_start(keys[:, 1], I["keys2"]).then_inc(loaded, 16)
            sp.dma_start(xn2[NS:P, NCH, :], xn2[0:NS, NCH, :]).then_inc(moved, 16)
            for g in range(NW):
                sp.wait_ge(product, 2 * GQ * (g + 1))
                sp.dma_start(ring[:, g], w_pq[:, :, (NW + g) * GRP:(NW + g + 1) * GRP]).then_inc(weights[g], 16)
            sp.wait_ge(moved, 16)

        @block.scalar
        def _(act):
            for q in range(NQ):
                for half in range(2):
                    act.wait_ge(product, 2 * q + half + 1)
                    act.activation(qpT[:, q, half * HALF_TOK:(half + 1) * HALF_TOK], bank[4 + 2 * (q % 2) + half][:, 0:HALF_TOK],
                                   ACT.Copy).then_inc(kept, 1)
            for i in range(NGRP // 2):
                act.wait_ge(scored, i + 1)
                act.activation(scores[:, 2 * i:2 * i + 2, :], bank[i % 4][:, :].rearrange("p (g k) -> p g k", g=2),
                               ACT.Copy).then_inc(stored, 1)

        @block.tensor
        def _(pe):
            for q in range(NQ):
                g = q // GQ
                pe.wait_ge(weights[g % NW], 16 * (g // NW + 1))
                for half in range(2):
                    if q >= 2:
                        pe.wait_ge(kept, 2 * (q - 2) + half + 1)
                    for d in range(KD):
                        ins = pe.matmul(bank[4 + 2 * (q % 2) + half][:, 0:HALF_TOK], ring[:, g % NW, d, (q % GQ) * P:(q % GQ + 1) * P],
                                        xn2T[:, d, half * HALF_TOK:(half + 1) * HALF_TOK], start=d == 0, stop=d == KD - 1)
                    ins.then_inc(product, 1)
            pe.wait_ge(kept, 2 * NQ)
            pe.wait_ge(loaded, 32)
            for i in range(NGRP // 2):
                if i >= 4:
                    pe.wait_ge(stored, i - 3)
                for r in (2 * i, 2 * i + 1):
                    c, h = r // G_TILE, r % G_TILE
                    parts = [(slice(0, P), h)] if c < NCH else [(slice(0, NS), h), (slice(NS, P), h + G_SAMPLE)]
                    for where, head in parts:
                        for t in range(2):
                            ins = pe.matmul(bank[i % 4][where, (r % 2) * 2 * NKEY + t * NKEY:(r % 2) * 2 * NKEY + (t + 1) * NKEY],
                                            qpT[:, 2 * head + t, c * P:c * P + rows(c)], keys[:, t], start=True, stop=True)
                ins.then_inc(scored, 1)


def experts(env, x1, xn2, scores, table, gate):
    nc, I, O, A, T, bank, sem = (env[k] for k in ("nc", "I", "O", "A", "T", "bank", "sem"))
    R = 8
    NDIAG = 4
    AHEAD = 3
    LINKS = 13
    u_ring, v_ring = A.take(R, D), A.take(R, D)
    junk = A.take(D)
    stage = A.take(4, TOPK)
    dots, act_, wts = A.take(TOPK), A.take(TOPK), A.take(TOPK)
    diag = A.take(NDIAG, P)
    g_row = A.take(D)
    ms = A.take(NT, 1)
    s, s_left = A.take(2, NKEY), A.take(2, NKEY)
    vals, picks, picks_f = A.take(2, TOPK), A.take(2, TOPK), A.take(2, TOPK)
    cand, cand_left = A.take(NCAND), A.take(NCAND)
    top_s, top_p = A.take(TOPK), A.take(TOPK)
    at, at_f, found = A.take(2, TOPK), A.take(2, TOPK), A.take(2, TOPK)
    onehot = A.take(2, TOPK, TOPK)
    w, total = A.take(TOPK), A.take(1)
    u_in, v_in = [sem(f"p7_u_in{i}") for i in range(R)], [sem(f"p7_v_in{i}") for i in range(R)]
    ready, staged = sem("p7_ready"), sem("p7_staged")
    u_used, v_used = sem("p7_u_used"), sem("p7_v_used")
    gelu, weighed, diags, added = sem("p7_gelu"), sem("p7_weighed"), sem("p7_diags"), sem("p7_added")
    own, squares, roots, y_done, stored = (sem("p7_" + n) for n in ("own", "squares", "roots", "y", "stored"))
    s_in, s_read, link, expos, exped, routed, summed, gated = (
        sem("p7_" + n) for n in ("s_in", "s_read", "link", "expos", "exped", "routed", "summed", "gated"))
    posts = sem("p7_posts")
    NPG = NCH * G_TILE

    with nc.Block() as block:
        @block.sync
        def _(sp):
            sp.dma_start(g_row, I["normf_row"].broadcast_to([P, D])).then_inc(ready, 16)
            for c in range(NT):
                sp.wait_ge(y_done, c + 1)
                dst = O["y_prompt"][c * P:(c + 1) * P, :] if c < NCH else O["y_sample"]
                sp.dma_start(dst, x1[0:rows(c), c, :]).then_inc(stored, 16)
            sp.wait_ge(stored, 16 * NT)

        @block.gpsimd
        def _(pool):
            u_idx, v_idx = stage[:, 0:2, :].bitcast(U32), stage[:, 2:4, :].bitcast(U32)

            def stage_numbers(which, place, r, count):
                pool.tensor_copy(which[:, place, :], table.bitcast(U32)[:, bass.ds(r, 1), :].rearrange("p a k -> p (a k)")).then_inc(staged, 1)
                pool.wait_ge(staged, count)
                pool.sem_inc(posts, 1)

            def gather(ring, which, place, k, rows_of, arrived, used, count):
                pool.wait_ge(used, count)
                pool.sem_inc(posts, 1)
                pool.indirect_dma_start(ring[:, k % R, :], None, rows_of,
                                        bass.IndirectOffsetOnAxis(which[:, place, k:k + 1], 0)).then_inc(arrived[k % R], 16)

            def turn(g, parity, last_u=False):
                for k in range(TOPK):
                    gather(v_ring, v_idx, parity, k, I["expert_v"], v_in, v_used, TOPK * g + (k + 1))
                    gather(u_ring, u_idx, 1 - parity, k, I["expert_u"], u_in, u_used, TOPK * g + (TOPK + k + 1))
                    if k == R:
                        stage_numbers(v_idx, 1 - parity, g + 1, 2 * g + 4)
                        if not last_u:
                            pool.wait_ge(routed, g + 3)
                            pool.sem_inc(posts, 1)
                            stage_numbers(u_idx, parity, g + 2, 2 * g + 5)

            pool.wait_ge(routed, 1)
            stage_numbers(u_idx, 0, 0, 1)
            stage_numbers(v_idx, 0, 0, 2)
            for k in range(TOPK):
                gather(u_ring, u_idx, 0, k, I["expert_u"], u_in, u_used, k + 1)
            pool.wait_ge(routed, 2)
            stage_numbers(u_idx, 1, 1, 3)
            with pool.Fori(0, NGRP // 2 - 1) as pair:
                for parity in range(2):
                    turn(2 * pair + parity, parity)
            turn(NGRP - 2, 0, last_u=True)
            for k in range(TOPK):
                gather(v_ring, v_idx, 1, k, I["expert_v"], v_in, v_used, TOPK * (NGRP - 1) + k + 1)

        @block.vector
        def _(dve):
            chain = Chain(dve, own)
            pk, tp, atu = picks.bitcast(U32), top_p.bitcast(U32), at.bitcast(U32)
            dve.memset(ms.rearrange("p a b -> p (a b)"), 0.0).then_inc(u_used, R)

            def top16_of(r):
                n = [0]

                def then(ins):
                    n[0] += 1
                    ins.then_inc(link, 1)
                    dve.wait_ge(link, LINKS * r + n[0])

                def post():
                    dve.sem_inc(posts, 1)

                dve.wait_ge(s_in, r + 1)
                post()
                for t in range(2):
                    ins = dve.max(vals[:, t, 0:8], s[:, t, :])
                then(ins)
                post()
                for t in range(2):
                    dve.max_index(pk[:, t, 0:8], vals[:, t, 0:8], s[:, t, :])
                    ins = dve.match_replace(s_left[:, t, :], vals[:, t, 0:8], s[:, t, :], LOWEST)
                ins.then_inc(s_read, 1)
                dve.wait_ge(s_read, r + 1)
                post()
                for t in range(2):
                    ins = dve.max(vals[:, t, 8:16], s_left[:, t, :])
                then(ins)
                post()
                for t in range(2):
                    ins = dve.max_index(pk[:, t, 8:16], vals[:, t, 8:16], s_left[:, t, :])
                then(ins)
                dve.tensor_copy(picks_f, pk)
                then(dve.tensor_tensor(cand.rearrange("p (i j) -> p i j", i=TOPK), bc(vals[:, 0, :], P, TOPK, TOPK),
                                       mid(vals[:, 1, :], TOPK, P, TOPK, TOPK), ALU.add))
                post()
                then(dve.max(top_s[:, 0:8], cand))
                post()
                dve.max_index(tp[:, 0:8], top_s[:, 0:8], cand)
                then(dve.match_replace(cand_left, top_s[:, 0:8], cand, LOWEST))
                post()
                then(dve.max(top_s[:, 8:16], cand_left))
                post()
                then(dve.max_index(tp[:, 8:16], top_s[:, 8:16], cand_left))
                dve.tensor_tensor(w, top_s, top_s[:, 0:1].to_broadcast([P, TOPK]), ALU.subtract).then_inc(expos, 1)
                dve.tensor_single_scalar(atu[:, 0], tp, 4, ALU.logical_shift_right)
                then(dve.tensor_single_scalar(atu[:, 1], tp, 15, ALU.bitwise_and))
                then(dve.tensor_copy(at_f, atu))
                then(dve.tensor_tensor(onehot, at_f.unsqueeze(3).to_broadcast([P, 2, TOPK, TOPK]),
                                       T["iota16"].unsqueeze(1).unsqueeze(1).to_broadcast([P, 2, TOPK, TOPK]), ALU.is_equal))
                then(dve.tensor_tensor(onehot, onehot, picks_f.unsqueeze(2).to_broadcast([P, 2, TOPK, TOPK]), ALU.mult))
                then(dve.tensor_reduce(found, onehot, AX, ALU.add))
                e_out = table.bitcast(U32)[:, bass.ds(r, 1), :].rearrange("p a k -> p (a k)")
                dve.scalar_tensor_tensor(out=e_out, in0=found[:, 0], scalar=float(NKEY), in1=found[:, 1], op0=ALU.mult,
                                         op1=ALU.add).then_inc(routed, 1)
                assert n[0] == LINKS, n

            def weights_of(r):
                dve.wait_ge(exped, r + 1)
                dve.tensor_reduce(total, w, AX, ALU.add).then_inc(summed, 1)
                dve.wait_ge(summed, 2 * r + 1)
                dve.reciprocal(total, total).then_inc(summed, 1)
                dve.wait_ge(summed, 2 * r + 2)
                dve.tensor_scalar(gate[:, bass.ds(r, 1), :].rearrange("p a k -> p (a k)"), w, total, None, ALU.mult).then_inc(gated, 1)

            def tile_of(ap, g):
                return ap[:, bass.ds(g // G_TILE, 1), :].rearrange("p a d -> p (a d)")

            def dots_of(g, weights_at=None):
                for k in range(TOPK):
                    dve.wait_ge(u_in[k % R], 32 * g + (16 * (k // R) + 16))
                    dve.scalar_tensor_tensor(out=junk, in0=u_ring[:, k % R, :], scalar=1.0, in1=tile_of(xn2, g), op0=ALU.mult,
                                             op1=ALU.mult, accum_out=dots[:, k:k + 1]).then_inc(u_used, 1)
                    dve.wait_ge(u_used, TOPK * g + (k + R + 1))
                    if weights_at is not None and k == R:
                        weights_of(weights_at)

            def weigh(g):
                dve.wait_ge(gelu, g + 1)
                dve.wait_ge(gated, g + 1)
                dve.tensor_tensor(wts, act_, gate[:, bass.ds(g, 1), :].rearrange("p a k -> p (a k)"), ALU.mult).then_inc(weighed, 1)

            def add(g):
                dve.wait_ge(v_used, TOPK * g + (TOPK + R))
                for j in range(2):
                    x = x1[:, bass.ds(g // G_TILE, 1), j * GRP:(j + 1) * GRP].rearrange("p a d -> p (a d)")
                    dve.tensor_tensor(x, x, bank[j][:, :], ALU.add).then_inc(added, 1)

            def turn(g, ahead):
                dots_of(g + 1, g + AHEAD - 1 if ahead else None)
                dve.wait_ge(diags, TOPK * g + TOPK)
                weigh(g + 1)
                add(g)
                if ahead:
                    top16_of(g + AHEAD)

            for r in range(AHEAD):
                top16_of(r)
                if r < AHEAD - 1:
                    weights_of(r)
            dots_of(0)
            weigh(0)
            with dve.Fori(0, NGRP - AHEAD) as g:
                turn(g, True)
            weights_of(NGRP - 1)
            with dve.Fori(NGRP - AHEAD, NGRP - 1) as g:
                turn(g, False)
            add(NGRP - 1)
            dve.wait_ge(ready, 16)
            for c in range(NT):
                n = rows(c)
                dve.wait_ge(roots, c + 1)
                chain.then(dve.reciprocal(ms[0:n, c, :], ms[0:n, c, :]))
                dve.scalar_tensor_tensor(out=x1[0:n, c, :], in0=x1[0:n, c, :], scalar=ms[0:n, c, :], in1=g_row[0:n, :],
                                         op0=ALU.mult, op1=ALU.mult).then_inc(y_done, 1)

        @block.scalar
        def _(act):
            def stage_scores(r):
                if not isinstance(r, int) or r:
                    act.wait_ge(s_read, r)
                act.activation(s, scores[:, bass.ds(r, 1), :].rearrange("p a (t k) -> p (a t) k", t=2), ACT.Copy).then_inc(s_in, 1)

            def exps(r):
                act.wait_ge(expos, r + 1)
                act.activation(w, w, ACT.Exp).then_inc(exped, 1)

            def gelu_of(g):
                act.wait_ge(u_used, TOPK * g + (TOPK + R))
                act.activation(act_, dots, ACT.Gelu).then_inc(gelu, 1)

            def turn(g, spread, ahead=True, last=False):
                if ahead:
                    stage_scores(g + AHEAD)
                act.wait_ge(weighed, g + 1)
                for k in range(TOPK):
                    act.wait_ge(v_used, TOPK * g + (k + R - NDIAG + 1))
                    act.activation(diag[:, k % NDIAG, :], spread, ACT.Copy, scale=wts[:, k:k + 1]).then_inc(diags, 1)
                    if ahead and k == NDIAG:
                        exps(g + AHEAD - 1)
                if not last:
                    gelu_of(g + 1)

            for r in range(AHEAD):
                stage_scores(r)
                if r < AHEAD - 1:
                    exps(r)
            gelu_of(0)
            with act.Fori(0, NPG) as g:
                turn(g, T["ident"])
            turn(NPG, T["fold2"])
            exps(NGRP - 1)
            with act.Fori(NPG + 1, NGRP - 1) as g:
                turn(g, T["fold2"], ahead=False)
            turn(NGRP - 1, T["fold2"], ahead=False, last=True)
            act.wait_ge(added, 2 * NGRP + 1)
            for c in range(NT):
                n = rows(c)
                if c:
                    act.wait_ge(squares, c)
                act.activation(junk[0:n, :], x1[0:n, c, :], ACT.Square, accum_out=ms[0:n, c, :]).then_inc(squares, 1)
            act.wait_ge(squares, NT)
            for c in range(NT):
                n = rows(c)
                act.activation(ms[0:n, c, :], ms[0:n, c, :], ACT.Sqrt, bias=EPS, scale=1.0 / D).then_inc(roots, 1)

        @block.tensor
        def _(pe):
            pe.sem_inc(v_used, R)
            pe.sem_inc(added, 1)
            with pe.Fori(0, NGRP) as g:
                for k in range(TOPK):
                    if k == 0:
                        pe.wait_ge(added, 2 * g + 1)
                    pe.wait_ge(diags, TOPK * g + (k + 1))
                    pe.wait_ge(v_in[k % R], 32 * g + (16 * (k // R) + 16))
                    for j in range(2):
                        ins = pe.matmul(bank[j][:, :], diag[:, k % NDIAG, :], v_ring[:, k % R, j * GRP:(j + 1) * GRP],
                                        start=k == 0, stop=k == TOPK - 1)
                    ins.then_inc(v_used, 1)


OUTS = {
    "y_prompt": (SEQ, D), "y_sample": (NS, D),
    "ret_p": (H, DK, DV), "C_p": (H, DH, DH), "n_p": (H, DH), "m_p": (1, H), "conv_p": (CW - 1, D),
    "ret_s": (NB, H, DK, DV), "C_s": (NB, H, DH, DH), "n_s": (NB * H, DH), "m_s": (NB, H), "conv_s": (NB * (CW - 1), D),
}
SHAPES = [(1, SEQ, D), (NB, TS, D), (1, 1, H, DK, DV), (1, 1, H, DH, DH), (1, 1, H, DH), (1, 1, H), (1, 1, CW - 1, D),
          (1, NB, H, DK, DV), (1, NB, H, DH, DH), (1, NB, H, DH), (1, NB, H), (1, NB, CW - 1, D)]


def layout(inputs):
    a = {k: np.asarray(v) for k, v in inputs.items()}
    per_channel = [a["norm1_g"][0], a["norm2_g"][0], a["ret_norm_g"][0].reshape(-1), a["mlstm_norm_g"][0].reshape(-1),
                   a["conv_b"][0]] + [a["conv_w"][0, j] for j in range(CW)]
    return {
        "x_prompt": a["x_prompt"][0], "x_sample": a["x_sample"].reshape(NS, D),
        "state_ret": a["state_ret"][0], "state_C": a["state_mlstm_C"][0], "state_n": a["state_mlstm_n"][0].reshape(NB * H, DH),
        "state_m": a["state_mlstm_m"][0], "state_conv": a["state_conv"][0].reshape(NB * (CW - 1), D),
        "w_in": a["w_in"][0], "w_mq": a["w_mq"][0], "w_mk": a["w_mk"][0], "w_br": a["w_br"][0], "w_bm": a["w_bm"][0],
        "w_out": a["w_out"][0], "w_pq": a["w_pq"][0],
        "keys1": np.ascontiguousarray(a["sub_keys1"][0].T), "keys2": np.ascontiguousarray(a["sub_keys2"][0].T),
        "expert_u": a["expert_u"][0], "expert_v": a["expert_v"][0],
        "bias": np.concatenate([a["b_i"], a["b_f"]], 1), "norm2_row": a["norm2_g"], "normf_row": a["norm_f_g"].reshape(1, D),
        "cols": np.ascontiguousarray(np.stack(per_channel).reshape(len(COLS), KD, P).transpose(2, 0, 1)).reshape(P, -1),
        "tables": _TABLES,
    }


def kernel(**inputs):
    import concourse.bacc as _bacc
    from concourse.bass_utils import run_bass_kernel_spmd as _run

    nc = _bacc.Bacc("TRN2", target_bir_lowering=False, num_devices=1)
    arrays = {f"in_{k}": np.ascontiguousarray(v) for k, v in layout(inputs).items()}
    I = {k[3:]: nc.dram_tensor(k, v.shape, mybir.dt.from_np(v.dtype), kind="ExternalInput").ap() for k, v in arrays.items()}
    O = {k: nc.dram_tensor(f"out_{k}", s, F32, kind="ExternalOutput").ap() for k, s in OUTS.items()}
    program(nc, I, O)
    r = _run(nc, [arrays], core_ids=[0])
    return tuple(r.results[0][f"out_{k}"].reshape(s) for k, s in zip(OUTS, SHAPES))
```

```python
import math

import numpy as np

import concourse.bass as bass
from concourse import mybir
from contextlib import ExitStack

F32 = mybir.dt.float32
F32R = mybir.dt.float32r
U32 = mybir.dt.uint32
ACT = mybir.ActivationFunctionType
ALU = mybir.AluOpType
AX = mybir.AxisListType.X

P = 128
D = 1024
KD = D // P
SEQ = 512
NB = 8
TS = 8
NS = NB * TS
NCH = SEQ // P
NT = NCH + 1
TOK = SEQ + NS
HALF_TOK = TOK // 2
PAST = 4096
H = 4
DK = 128
DV = 256
DH = 256
CW = 4
QK_R = H * DK
V_R = H * DV
PH = 8
NKEY = 128
TOPK = 16
NCAND = TOPK * TOPK
NSLOT = PH * TOPK
EPS = 1e-6
NEG = -1.0e30
LOWEST = -3.0e38
GRP = 512
C_QKVG = 0
C_XM = 2 * QK_R + 2 * V_R
C_VM = C_XM + D
C_IF = C_XM + 3 * D
C_GR = C_IF + 2 * H
C_GM = C_GR + D
G_TILE = PH
G_SAMPLE = PH // 2
NGRP = NCH * G_TILE + G_SAMPLE


def _log_gamma():
    return np.log1p(-np.exp2(-5.0 - np.arange(H, dtype=np.float32))).astype(np.float32)


def _tables():
    t = {}
    lg = _log_gamma()
    half = DK // 2
    freqs = np.exp(np.float32(-math.log(10000.0)) * np.arange(half, dtype=np.float32) / np.float32(half)).astype(np.float32)
    pos = np.concatenate([np.arange(SEQ), np.tile(PAST + np.arange(TS), NB)]).astype(np.float32)
    ang = (pos[:, None] * freqs[None, :]).astype(np.float32)
    cs = np.zeros((NT * P, 2, half), np.float32)
    cs[:TOK, 0], cs[:TOK, 1] = np.cos(ang), np.sin(ang)
    t["rope"] = cs.reshape(NT, P, 2 * half).transpose(1, 0, 2).reshape(P, -1)
    i = np.arange(P, dtype=np.float32)
    r = np.arange(NS)
    same = (r[:, None] // TS) == (r[None, :] // TS)
    scale = np.float32(DK ** -0.5)

    def pad(a):
        out = np.zeros((P,) + a.shape[1:], np.float32)
        out[:a.shape[0]] = a
        return out.reshape(P, -1)

    diff = i[None, :] - i[:, None]
    dm = np.where(diff >= 0, np.exp(lg[:, None, None] * np.maximum(diff, 0)), 0) * scale
    t["ret_mask_p"] = dm.transpose(1, 0, 2).reshape(P, -1)
    sdiff = (r[None, :] - r[:, None]).astype(np.float32)
    sok = same & (sdiff >= 0)
    sm = np.where(sok, np.exp(lg[:, None, None] * np.maximum(sdiff, 0)), 0) * scale
    t["ret_mask_s"] = pad(sm.transpose(1, 0, 2))
    t["ret_qdec_p"] = np.broadcast_to((np.exp(lg[:, None] * (i + 1)) * scale).reshape(1, -1), (P, H * P))
    t["ret_qdec_s"] = np.broadcast_to((np.exp(lg[:, None] * (r % TS + 1)) * scale).reshape(1, -1), (P, H * NS))
    t["ret_kdec_p"] = np.exp(lg[None, :] * (P - 1 - i)[:, None])
    t["ret_kdec_s"] = pad(np.exp(lg[None, :] * (TS - 1 - r % TS)[:, None]))
    t["batch_cols"] = np.broadcast_to((r[None, :] // TS == np.arange(NB)[:, None]).astype(np.float32).reshape(1, -1), (P, NB * NS))
    t["batch_rows"] = pad((r[:, None] // TS == np.arange(NB)[None, :]).astype(np.float32))
    t["last_rows"] = pad((r[:, None] == np.arange(NB)[None, :] * TS + TS - 1).astype(np.float32))
    t["tri_p"] = (diff >= 0).astype(np.float32)
    t["tri_s"] = pad(sok.astype(np.float32))
    t["mask_ts_p"] = np.where(diff.T >= 0, 0, NEG)
    t["mask_ts_s"] = pad(np.where(sok.T, 0, NEG))
    t["mask_st_p"] = np.where(diff >= 0, 0, NEG)
    t["mask_st_s"] = pad(np.where(sok, 0, NEG))
    t["pick_p"] = (np.arange(P)[:, None] == P - 1).astype(np.float32) * np.ones((1, P), np.float32)
    t["pick_s"] = pad((r[:, None] == (r[None, :] // TS) * TS + TS - 1).astype(np.float32))
    t["ones"] = np.ones((P, P))
    t["ident"] = np.eye(P)
    t["fold2"] = np.concatenate([np.concatenate([np.eye(NS), np.eye(NS)], 0), np.zeros((P, P - NS))], 1)
    t["iota16"] = np.broadcast_to(np.arange(TOPK, dtype=np.float32)[None, :], (P, TOPK))
    where, at, parts = {}, 0, []
    for k, v in t.items():
        v = np.ascontiguousarray(v, dtype=np.float32)
        where[k] = (at, v.shape[1])
        at += v.shape[1]
        parts.append(v)
    return where, np.concatenate(parts, 1)


_WHERE, _TABLES = _tables()
NTAB = _TABLES.shape[1]

COLS = ["norm1_g", "norm2_g", "ret_norm_g", "mlstm_norm_g", "conv_b", "conv_w0", "conv_w1", "conv_w2", "conv_w3"]


class Arena:

    def __init__(self, tensor, words):
        self.tensor, self.words, self.top = tensor, words, 0
        self.upper, self.upper_words = None, 0

    def set_upper(self, tensor, words):
        self.upper, self.upper_words = tensor, words

    def take(self, *shape, at=None):
        n = int(np.prod(shape))
        if at is None and self.top < self.words < self.top + n:
            self.top = self.words
        a = self.top if at is None else at
        if at is None:
            self.top += n
        if a < self.words:
            assert a + n <= self.words, (a, n, self.words)
            v = self.tensor[:, a:a + n]
        else:
            a -= self.words
            assert a + n <= self.upper_words, (a, n, self.upper_words)
            v = self.upper[:, a:a + n]
        if len(shape) == 1:
            return v
        names = "abcd"[:len(shape)]
        return v.rearrange("p (" + " ".join(names) + ") -> p " + " ".join(names),
                           **{k: s for k, s in zip(names[1:], shape[1:])})


class Chain:

    def __init__(self, eng, sem):
        self.eng, self.sem, self.n = eng, sem, 0

    def then(self, ins):
        self.n += 1
        ins.then_inc(self.sem, 1)
        self.eng.wait_ge(self.sem, self.n)


def rows(c):
    return P if c < NCH else NS


def bc(ap, *shape):
    return ap.unsqueeze(len(shape) - 1).to_broadcast(list(shape))


def mid(ap, n, *shape):
    return ap.unsqueeze(1).to_broadcast(list(shape))


class SplitProducts:

    UK = 2
    U = KD // UK

    def __init__(self, sem, prefix, xs, ws, wf, nf, products):
        self.xs, self.ws, self.wf, self.nf, self.products = xs, ws, wf, nf, products
        self.arrived = [sem(f"{prefix}_w_arrived{i}") for i in range(nf)]
        self.hi, self.lo, self.steps = sem(prefix + "_split_hi"), sem(prefix + "_split_lo"), sem(prefix + "_steps")

    def start(self, g):
        if isinstance(self.products, int):
            return g * (self.U - 1 + self.products)
        return g * (self.U - 1) + sum(self.products[0:g])

    def unit_done(self, g, u):
        return self.start(g) + u + 1 if u < self.U - 1 else self.start(g + 1)

    def product_done(self, g, j):
        return self.start(g) + self.U - 1 + j + 1

    def load(self, sp, g, u, first, weight):
        if not first or u >= self.nf:
            sp.wait_ge(self.lo, self.U * g + (u + 1 - self.nf))
        sp.dma_start(self.wf[:, u % self.nf], weight[:, u * self.UK:(u + 1) * self.UK, :]).then_inc(self.arrived[u % self.nf], 16)

    def split_hi(self, act, g, u, first, x=None):
        act.wait_ge(self.arrived[u % self.nf], 16 * ((self.U // self.nf) * g + (u // self.nf + 1)))
        if u >= 2:
            act.wait_ge(self.steps, self.unit_done(g, u - 2))
        elif not first:
            act.wait_ge(self.steps, self.unit_done(g - 1, self.U - 2 + u))
        k = slice(u * self.UK, (u + 1) * self.UK)
        if x is not None:
            act.activation(self.xs[:, 0, k, :], x[:, k, :], ACT.Copy)
        act.activation(self.ws[:, u % 2, 0], self.wf[:, u % self.nf], ACT.Copy).then_inc(self.hi, 1)

    def split_lo(self, dve, g, u, x=None):
        dve.wait_ge(self.hi, self.U * g + (u + 1))
        k = slice(u * self.UK, (u + 1) * self.UK)
        if x is not None:
            dve.tensor_tensor(self.xs[:, 1, k, :], x[:, k, :], self.xs[:, 0, k, :].bitcast(F32), ALU.subtract)
        dve.tensor_tensor(self.ws[:, u % 2, 1], self.wf[:, u % self.nf], self.ws[:, u % 2, 0].bitcast(F32),
                          ALU.subtract).then_inc(self.lo, 1)

    def multiply(self, pe, g, bank, token_major, free):
        passes = ((0, 0), (0, 1), (1, 0))
        for u in range(self.U):
            pe.wait_ge(self.lo, self.U * g + (u + 1))
            for j in range(NT if token_major else GRP // P):
                if u == 0:
                    free(j)
                for kk in range(self.UK):
                    k = u * self.UK + kk
                    for xp, wp in passes:
                        flags = dict(start=k == 0 and xp + wp == 0, stop=k == KD - 1 and xp == 1)
                        w = self.ws[:, u % 2, wp, kk]
                        if token_major:
                            ins = pe.matmul(bank[j][0:rows(j), :], self.xs[:, xp, k, j * P:j * P + rows(j)], w, **flags)
                        else:
                            for half in range(2):
                                ins = pe.matmul(bank[2 * j + half][:, 0:HALF_TOK], w[:, j * P:(j + 1) * P],
                                                self.xs[:, xp, k, half * HALF_TOK:(half + 1) * HALF_TOK], **flags)
                if u == self.U - 1:
                    ins.then_inc(self.steps, 1)
            if u < self.U - 1:
                ins.then_inc(self.steps, 1)


def program(nc, I, O):
    with ExitStack() as ctx:
        LOWER = NTAB + len(COLS) * KD + 4 * KD * TOK + NT * H * (DH + 1) + NT * D + NT * 2 * H
        UPPER = 53200 - LOWER
        SPLIT = 2 * KD * TOK + 2 * 2 * SplitProducts.UK * GRP
        A = Arena(ctx.enter_context(nc.sbuf_tensor("lower", [P, LOWER], F32)), LOWER)
        bank = [ctx.enter_context(nc.psum_tensor(f"bank{i}", [P, GRP], F32)) for i in range(8)]

        tab = A.take(NTAB)
        T = {k: tab[:, a:a + n] for k, (a, n) in _WHERE.items()}
        cols = A.take(len(COLS), KD)
        col = {k: cols[:, i, :] for i, k in enumerate(COLS)}
        xnT = A.take(KD, TOK)
        yrT = A.take(KD, TOK)
        BASE = A.top
        held = []

        def sem(name):
            held.append(nc.alloc_semaphore(name=name))
            return held[-1]

        def retire():
            env["finished"] = held[:]
            held.clear()

        def release():
            for s in env["finished"]:
                nc.release_semaphore(s)

        env = dict(nc=nc, I=I, O=O, A=A, bank=bank, T=T, tab=tab, cols=cols, col=col, xnT=xnT, yrT=yrT, sem=sem)

        def plain_upper(stack, name):
            A.set_upper(stack.enter_context(nc.sbuf_tensor(name, [P, UPPER], F32)), UPPER)

        def split_upper(stack, name):
            A.set_upper(stack.enter_context(nc.sbuf_tensor(name, [P, UPPER - SPLIT], F32)), UPPER - SPLIT)
            xs = stack.enter_context(nc.sbuf_tensor(name + "_x_split", [P, 2 * KD * TOK], F32R))
            ws = stack.enter_context(nc.sbuf_tensor(name + "_w_split", [P, 2 * 2 * SplitProducts.UK * GRP], F32R))
            env["xs"] = xs[:, :].rearrange("p (s k t) -> p s k t", s=2, k=KD)
            env["ws"] = ws[:, :].rearrange("p (r s k c) -> p r s k c", r=2, s=2, k=SplitProducts.UK)

        proj = A.take(NT, 2 * QK_R + 2 * V_R)
        PROJ_END = A.top
        with ExitStack() as upper:
            split_upper(upper, "upper1")
            norm_and_retention_projection(env, proj)
        A.top = PROJ_END
        with ExitStack() as upper:
            plain_upper(upper, "upper2")
            retention(env, proj)
        A.top = BASE
        v = A.take(NT, H, DH + 1)
        o = A.take(NT, D)
        kT = A.take(KD, TOK)
        qT = A.take(KD, TOK)
        gates = A.take(NT, 2 * H)
        assert A.top == LOWER
        with ExitStack() as upper:
            split_upper(upper, "upper3")
            mlstm_projection(env, v, o, kT, qT, gates)
        A.top = LOWER
        with ExitStack() as upper:
            plain_upper(upper, "upper4")
            retire()
            mlstm(env, v, o, kT, qT, gates)
            release()
        hmT = qT
        A.top = BASE
        x1 = A.take(NT, D)
        xn2 = A.take(NT, D)
        with ExitStack() as upper:
            split_upper(upper, "upper5")
            keys = A.take(2, NKEY, at=3 * D)
            qpT = A.take(2 * PH, TOK)
            A.top = LOWER
            retire()
            merge_norm_and_queries(env, hmT, kT, x1, xn2, qpT, keys)
            release()
        A.top = LOWER
        scores = A.take(NGRP, 2 * NKEY, at=BASE - 2 * KD * TOK)
        with ExitStack() as upper:
            plain_upper(upper, "upper6")
            experts(env, x1, xn2, qpT, keys, scores)


def transpose_tile(pe, src, ident, banks, n, last_sem, before=None):
    for half in range(2):
        if before:
            before(half)
        for j in range(4):
            k = half * 4 + j
            ins = pe.transpose(banks[half][:, j * P:j * P + n], src[0:n, k * P:(k + 1) * P], ident[0:n, 0:n])
        ins.then_inc(last_sem, 1)


def quarter(b, n):
    return b[:, :].rearrange("p (k t) -> p k t", k=4)[:, :, 0:n]


def norm_and_retention_projection(env, proj):
    nc, I, A, T, bank, sem = (env[k] for k in ("nc", "I", "A", "T", "bank", "sem"))
    xnT, col = env["xnT"], env["col"]
    NF = 4
    wf = A.take(NF, SplitProducts.UK, GRP)
    ms = A.take(NT, 1)
    x, junk = proj[:, :, 0:D], proj[:, 0, D:2 * D]
    NG = proj.shape[2] // GRP
    i0 = _WHERE["ident"][0]
    split = SplitProducts(sem, "p1", env["xs"], env["ws"], wf, NF, NT)
    U = split.U
    tables, ident, loaded = sem("p1_tables"), sem("p1_ident"), [sem(f"p1_x_loaded{c}") for c in range(NT)]
    squares, roots, normed = sem("p1_squares"), sem("p1_roots"), sem("p1_normed")
    turned, kept = sem("p1_turned"), sem("p1_kept")
    copied, own = sem("p1_copied"), sem("p1_own")
    w_in = I["w_in"].rearrange("(k p) c -> p k c", p=P)

    with nc.Block() as block:
        @block.sync
        def _(sp):
            for c in range(NCH):
                sp.dma_start(x[:, c, :], I["x_prompt"][c * P:(c + 1) * P, :]).then_inc(loaded[c], 16)
                if c == 0:
                    sp.dma_start(T["ident"], I["tables"][:, i0:i0 + P]).then_inc(ident, 16)
                    sp.dma_start(env["cols"].rearrange("p a b -> p (a b)"), I["cols"]).then_inc(ident, 16)
            sp.dma_start(x[0:NS, NCH, :], I["x_sample"]).then_inc(loaded[NCH], 16)
            for u in range(U):
                split.load(sp, 0, u, True, w_in[:, :, 0:GRP])
            sp.dma_start(env["tab"][:, 0:i0], I["tables"][:, 0:i0]).then_inc(tables, 16)
            sp.dma_start(env["tab"][:, i0 + P:], I["tables"][:, i0 + P:]).then_inc(tables, 16)
            with sp.Fori(1, NG) as g:
                for u in range(U):
                    split.load(sp, g, u, False, w_in[:, :, bass.ds(g * GRP, GRP)])
            sp.wait_ge(tables, 32)

        @block.scalar
        def _(act):
            for c in range(NT):
                n = rows(c)
                act.wait_ge(loaded[c], 16)
                if c:
                    act.wait_ge(squares, c)
                act.activation(junk[0:n, :], x[0:n, c, :], ACT.Square, accum_out=ms[0:n, c, :]).then_inc(squares, 1)
                act.wait_ge(squares, c + 1)
                act.activation(ms[0:n, c, :], ms[0:n, c, :], ACT.Sqrt, bias=EPS, scale=1.0 / D).then_inc(roots, 1)

            def copy_out(g):
                for c in range(NT):
                    n = rows(c)
                    act.wait_ge(split.steps, split.product_done(g, c))
                    act.activation(proj[0:n, c, bass.ds(g * GRP, GRP)], bank[c][0:n, :], ACT.Copy).then_inc(copied, 1)
            act.wait_ge(kept, 2 * NT)
            for u in range(U):
                split.split_hi(act, 0, u, True, xnT)
            with act.Fori(1, NG) as g:
                split.split_hi(act, g, 0, False)
                copy_out(g - 1)
                for u in range(1, U):
                    split.split_hi(act, g, u, False)
            copy_out(NG - 1)

        @block.vector
        def _(dve):
            chain = Chain(dve, own)

            def scale(c):
                n = rows(c)
                dve.wait_ge(roots, c + 1)
                chain.then(dve.reciprocal(ms[0:n, c, :], ms[0:n, c, :]))
                dve.tensor_scalar(x[0:n, c, :], x[0:n, c, :], ms[0:n, c, :], None, ALU.mult).then_inc(normed, 1)
            scale(0)
            dve.wait_ge(ident, 32)
            for c in range(NT):
                n = rows(c)
                if c < NCH:
                    scale(c + 1)
                for half in range(2):
                    dve.wait_ge(turned, 2 * c + half + 1)
                    k = 4 * half
                    dve.tensor_tensor(xnT[:, k:k + 4, c * P:c * P + n], quarter(bank[6 + half], n),
                                      bc(col["norm1_g"][:, k:k + 4], P, 4, n), ALU.mult).then_inc(kept, 1)
            dve.wait_ge(kept, 2 * NT)
            for u in range(U):
                split.split_lo(dve, 0, u, xnT)
            with dve.Fori(1, NG) as g:
                for u in range(U):
                    split.split_lo(dve, g, u)

        @block.tensor
        def _(pe):
            pe.wait_ge(ident, 32)
            for c in range(NT):
                pe.wait_ge(normed, c + 1)

                def free(half, c=c):
                    if c:
                        pe.wait_ge(kept, 2 * (c - 1) + half + 1)
                transpose_tile(pe, x[:, c, :], T["ident"], bank[6:8], rows(c), turned, free)
            split.multiply(pe, 0, bank, True, lambda c: None)
            with pe.Fori(1, NG) as g:
                split.multiply(pe, g, bank, True, lambda c: pe.wait_ge(copied, NT * (g - 1) + (c + 1)))


def retention(env, proj):
    nc, I, O, A, T, bank, sem = (env[k] for k in ("nc", "I", "O", "A", "T", "bank", "sem"))
    yrT, col = env["yrT"], env["col"]
    rr = A.take(2, 2 * H, DK)
    part = A.take(4, 2 * H, DK // 2)
    qT, kT, qdT = A.take(H, P), A.take(H, P), A.take(H, P)
    kd = A.take(H, DK)
    prob = A.take(H, P)
    S = A.take(H, DV)
    y = A.take(2, H, DV)
    stats, mv, rstd = A.take(H, 6), A.take(H, 2), A.take(H)
    SS = A.take(H, NB, DV)
    qz = A.take(H, NB, NS)
    kz = A.take(H, NB, DK)
    gamma = np.exp(_log_gamma())
    cdec = [float(np.exp(_log_gamma()[h] * L)) for L in (P, TS) for h in range(H)]

    states, silu = sem("p2_states"), sem("p2_silu")
    own, pool_own, rotated = sem("p2_own"), sem("p2_pool_own"), sem("p2_rotated")
    turned, q_out, k_out, qd_out = sem("p2_turned"), sem("p2_q_out"), sem("p2_k_out"), sem("p2_qd_out")
    scores, probs, ydone, y_out, kv, kd_out = (sem("p2_" + n) for n in ("scores", "probs", "y", "y_out", "kv", "kd"))
    new_state, var, root, yn, yturned, ykept = (sem("p2_" + n) for n in ("new_state", "var", "root", "ynormed", "yturned", "ykept"))
    masked, stored = sem("p2_masked"), sem("p2_stored")
    UNITS = 2 * H

    def kv_banks(u):
        return bank[5:7] if u % 2 == 0 else bank[0:2]

    def rotate(eng, chain, c):
        n = rows(c)
        k_ = "s" if c == NCH else "p"
        qk = proj[0:n, c, 0:2 * QK_R].rearrange("p (h two d) -> p h two d", two=2, d=DK // 2)
        cs = T["rope"].rearrange("p (t two d) -> p t two d", t=NT, two=2)[0:n, c]
        for i, (x, f) in enumerate(((0, 0), (1, 1), (0, 1), (1, 0))):
            ins = eng.tensor_tensor(part[0:n, i], qk[:, :, x, :],
                                    mid(cs[:, f, :], 2 * H, n, 2 * H, DK // 2), ALU.mult)
        chain.then(ins)
        if c >= 2:
            eng.wait_ge(turned, 2 * (c - 1))
        eng.tensor_tensor(rr[0:n, c % 2, :, 0:DK // 2], part[0:n, 0], part[0:n, 1], ALU.subtract)
        eng.tensor_tensor(rr[0:n, c % 2, :, DK // 2:], part[0:n, 2], part[0:n, 3], ALU.add).then_inc(rotated, 1)
        eng.wait_ge(rotated, c + 1)
        if c:
            eng.wait_ge(kv, c)
        eng.tensor_tensor(kd[0:n], rr[0:n, c % 2, H:2 * H], bc(T["ret_kdec_" + k_][0:n], n, H, DK), ALU.mult).then_inc(kd_out, 1)

    with nc.Block() as block:
        @block.sync
        def _(sp):
            for h in range(H):
                sp.dma_start(SS[:, h], I["state_ret"].rearrange("b h k v -> h k b v")[h]).then_inc(states, 16)
            sp.wait_ge(new_state, NCH * H)
            sp.dma_start(O["ret_p"].rearrange("h k v -> k h v"), S).then_inc(stored, 16)
            for h in range(H):
                sp.wait_ge(new_state, NCH * H + NB * (h + 1))
                sp.dma_start(O["ret_s"].rearrange("b h k v -> h k b v")[h], SS[:, h]).then_inc(stored, 16)
            sp.wait_ge(stored, 16 * (H + 1))

        @block.scalar
        def _(act):
            for c in range(NT):
                n = rows(c)
                g = proj[0:n, c, 2 * QK_R + V_R:]
                act.activation(g, g, ACT.Silu).then_inc(silu, 1)

            def turned_out(c):
                n = rows(c)
                act.wait_ge(turned, 2 * c + 1)
                if c:
                    act.wait_ge(scores, c)
                    act.wait_ge(qd_out, c)
                act.activation(qT[:, :, 0:n], quarter(bank[0], n), ACT.Copy).then_inc(q_out, 1)
                act.wait_ge(turned, 2 * c + 2)
                act.activation(kT[:, :, 0:n], quarter(bank[1], n), ACT.Copy).then_inc(k_out, 1)
            turned_out(0)
            for c in range(NT):
                n = rows(c)
                act.wait_ge(ydone, c + 1)
                if c >= 2:
                    act.wait_ge(yturned, 2 * (c - 1))
                for j in range(2):
                    act.activation(y[0:n, c % 2, 2 * j:2 * j + 2], bank[3 + j][0:n, :].rearrange("p (h v) -> p h v", h=2),
                                   ACT.Copy).then_inc(y_out, 1)
                if c < NCH:
                    turned_out(c + 1)
                act.wait_ge(var, c + 1)
                act.activation(rstd[0:n, :], mv[0:n, :, 1], ACT.Sqrt, bias=EPS).then_inc(root, 1)

        @block.gpsimd
        def _(pool):
            chain = Chain(pool, pool_own)
            pool.wait_ge(rotated, 1)
            pool.wait_ge(kd_out, 1)
            for c in range(1, NT):
                rotate(pool, chain, c)

        @block.vector
        def _(dve):
            chain = Chain(dve, own)

            def mask_k(c):
                n = rows(c)
                if c == NCH:
                    dve.wait_ge(kd_out, c + 1)
                    for h in range(H):
                        dve.tensor_tensor(kz[0:n, h], mid(kd[0:n, h, :], NB, n, NB, DK),
                                          bc(T["batch_rows"][0:n], n, NB, DK), ALU.mult).then_inc(masked, 1)

            def weigh(c):
                n = rows(c)
                k_ = "s" if c == NCH else "p"
                dve.wait_ge(q_out, c + 1)
                if c:
                    dve.wait_ge(ydone, c)
                dve.tensor_tensor(qdT[:, :, 0:n], qT[:, :, 0:n],
                                  T["ret_qdec_" + k_].rearrange("p (h t) -> p h t", h=H), ALU.mult).then_inc(qd_out, 1)
                if c == NCH:
                    dve.wait_ge(qd_out, c + 1)
                    for h in range(H):
                        dve.tensor_tensor(qz[:, h], mid(qdT[:, h, 0:n], NB, P, NB, n),
                                          T["batch_cols"].rearrange("p (b t) -> p b t", b=NB), ALU.mult).then_inc(masked, 1)
                dve.wait_ge(scores, c + 1)
                dve.tensor_tensor(prob[0:n, :, 0:n], quarter(bank[2], n)[0:n],
                                  T["ret_mask_" + k_].rearrange("p (h t) -> p h t", h=H)[0:n], ALU.mult).then_inc(probs, 1)

            def new_states(c):
                dve.wait_ge(ydone, c + 1)
                if c < NCH:
                    dve.wait_ge(kv, c + 1)
                    for h in range(H):
                        src = bank[5 + h // 2][:, (h % 2) * DV:(h % 2 + 1) * DV]
                        if c == 0:
                            dve.tensor_copy(S[:, h], src).then_inc(new_state, 1)
                        else:
                            dve.scalar_tensor_tensor(out=S[:, h], in0=S[:, h], scalar=cdec[h], in1=src,
                                                     op0=ALU.mult, op1=ALU.add).then_inc(new_state, 1)
                else:
                    for u in range(UNITS):
                        dve.wait_ge(kv, NCH + u + 1)
                        for j in range(4):
                            h, b = u // 2, (u % 2) * 4 + j
                            src = kv_banks(u)[j // 2][:, (j % 2) * DV:(j % 2 + 1) * DV]
                            dve.scalar_tensor_tensor(out=SS[:, h, b], in0=SS[:, h, b], scalar=cdec[H + h], in1=src,
                                                     op0=ALU.mult, op1=ALU.add).then_inc(new_state, 1)

            def head_norm(c):
                n = rows(c)
                yc = y[0:n, c % 2]
                dve.wait_ge(y_out, 2 * (c + 1))
                for h in range(H):
                    ins = dve.bn_stats(stats[0:n, h], yc[:, h])
                chain.then(ins)
                for h in range(H):
                    ins = dve.bn_aggr(mv[0:n, h], stats[0:n, h])
                ins.then_inc(var, 1)
                dve.wait_ge(root, c + 1)
                chain.then(dve.reciprocal(rstd[0:n, :], rstd[0:n, :]))
                for h in range(H):
                    ins = dve.tensor_scalar(yc[:, h], yc[:, h], mv[0:n, h, 0:1], rstd[0:n, h:h + 1], ALU.subtract, ALU.mult)
                chain.then(ins)
                dve.wait_ge(silu, NT)
                yr = yc.rearrange("p h v -> p (h v)")
                dve.tensor_tensor(yr, yr, proj[0:n, c, 2 * QK_R + V_R:], ALU.mult).then_inc(yn, 1)

            def keep_y(c):
                n = rows(c)
                for half in range(2):
                    dve.wait_ge(yturned, 2 * c + half + 1)
                    k = 4 * half
                    dve.tensor_tensor(yrT[:, k:k + 4, c * P:c * P + n], quarter(bank[7], n),
                                      bc(col["ret_norm_g"][:, k:k + 4], P, 4, n), ALU.mult).then_inc(ykept, 1)
            rotate(dve, chain, 0)
            weigh(0)
            for c in range(NCH):
                new_states(c)
                weigh(c + 1)
                if c:
                    keep_y(c - 1)
                head_norm(c)
            mask_k(NCH)
            keep_y(NCH - 1)
            new_states(NCH)
            head_norm(NCH)
            keep_y(NCH)

        @block.tensor
        def _(pe):
            def scores_of(c):
                n = rows(c)
                pe.wait_ge(rotated, c + 1)
                for side in range(2):
                    if c:
                        pe.wait_ge((q_out, k_out)[side], c)
                    for h in range(H):
                        ins = pe.transpose(bank[side][:, h * P:h * P + n], rr[0:n, c % 2, side * H + h, :], T["ident"][0:n, 0:n])
                    ins.then_inc(turned, 1)
                pe.wait_ge(q_out, c + 1)
                pe.wait_ge(k_out, c + 1)
                if c:
                    pe.wait_ge(probs, c)
                for h in range(H):
                    ins = pe.matmul(bank[2][0:n, h * P:h * P + n], kT[:, h, 0:n], qT[:, h, 0:n], start=True, stop=True)
                ins.then_inc(scores, 1)

            def outputs_of(c):
                n = rows(c)
                sample = c == NCH
                pe.wait_ge(probs, c + 1)
                pe.wait_ge(qd_out, c + 1)
                if c:
                    pe.wait_ge(y_out, 2 * c)
                    pe.wait_ge(new_state, c * H)
                if sample:
                    pe.wait_ge(masked, H)
                    pe.wait_ge(states, 16 * H)
                for h in range(H):
                    out = bank[3 + h // 2][0:n, (h % 2) * DV:(h % 2 + 1) * DV]
                    vh = proj[0:n, c, 2 * QK_R + h * DV:2 * QK_R + (h + 1) * DV]
                    ins = pe.matmul(out, prob[0:n, h, 0:n], vh, start=True, stop=c == 0)
                    if sample:
                        for b in range(NB):
                            ins = pe.matmul(out, qz[:, h, b], SS[:, h, b], start=False, stop=b == NB - 1)
                    elif c:
                        ins = pe.matmul(out, qdT[:, h, 0:n], S[:, h], start=False, stop=True)
                ins.then_inc(ydone, 1)

            def state_products(c):
                n = rows(c)
                pe.wait_ge(kd_out, c + 1)
                if c == NCH:
                    pe.wait_ge(masked, 2 * H)
                if c < NCH:
                    for h in range(H):
                        ins = pe.matmul(bank[5 + h // 2][:, (h % 2) * DV:(h % 2 + 1) * DV], kd[0:n, h],
                                        proj[0:n, c, 2 * QK_R + h * DV:2 * QK_R + (h + 1) * DV], start=True, stop=True)
                    ins.then_inc(kv, 1)
                else:
                    for u in range(UNITS):
                        pe.wait_ge(new_state, NCH * H + 4 * max(u - 1, 0))
                        for j in range(4):
                            h, b = u // 2, (u % 2) * 4 + j
                            ins = pe.matmul(kv_banks(u)[j // 2][:, (j % 2) * DV:(j % 2 + 1) * DV], kz[0:n, h, b],
                                            proj[0:n, c, 2 * QK_R + h * DV:2 * QK_R + (h + 1) * DV], start=True, stop=True)
                        ins.then_inc(kv, 1)

            def turn_y(c):
                n = rows(c)
                pe.wait_ge(yn, c + 1)
                for half in range(2):
                    if c or half:
                        pe.wait_ge(ykept, 2 * c + half)
                    for j in range(4):
                        k = half * 4 + j
                        ins = pe.transpose(bank[7][:, j * P:j * P + n], y[0:n, c % 2].rearrange("p h v -> p (h v)")[:, k * P:(k + 1) * P],
                                           T["ident"][0:n, 0:n])
                    ins.then_inc(yturned, 1)
            scores_of(0)
            for c in range(NT):
                outputs_of(c)
                if c < NCH:
                    state_products(c)
                    scores_of(c + 1)
                    if c:
                        turn_y(c - 1)
            turn_y(NCH - 1)
            state_products(NCH)
            turn_y(NCH)


def token_tiles_of(half):
    if half == 0:
        return [(0, HALF_TOK, False)]
    return [(HALF_TOK, SEQ - HALF_TOK, False), (SEQ, NS, True)]


def mlstm_projection(env, v, o, kT, qT, gates):
    nc, I, O, A, T, bank, sem = (env[k] for k in ("nc", "I", "O", "A", "T", "bank", "sem"))
    xnT, col = env["xnT"], env["col"]
    PAD = CW - 1
    xm = kT.rearrange("p k t -> p (k t)")[:, 0:KD * (PAD + SEQ)].rearrange("p (k t) -> p k t", k=KD)
    xs = A.take(KD, NB * (PAD + TS)).rearrange("p k (b t) -> p k b t", b=NB)
    xcT = qT
    NF = 2
    wf = A.take(NF, SplitProducts.UK, GRP)
    wqk = A.take(2, KD, DH)
    wif = A.take(KD, 2 * H)
    bias = A.take(2 * H)
    past = A.take(D, at=0)
    tails = A.take(KD, (NB + 1) * PAD)
    tail_rows = past
    NTAIL = (NB + 1) * PAD
    past_read, small, wqk_in = sem("p3_past_read"), sem("p3_small"), sem("p3_wqk")
    past_turned, past_in, cleared = sem("p3_past_turned"), sem("p3_past_in"), sem("p3_cleared")
    xm_copied, copied = sem("p3_xm_copied"), sem("p3_copied")
    if_done, if_kept = sem("p3_if_done"), sem("p3_if_kept")
    own, conv, act_out = sem("p3_own"), sem("p3_conv"), sem("p3_silu")
    tail_in, tail_turned, tail_out = sem("p3_tail_in"), sem("p3_tail_turned"), sem("p3_tail_out")
    products_qk, q_kept, k_kept, stored = (sem("p3_" + n) for n in ("products_qk", "q_kept", "k_kept", "stored"))
    w_in = I["w_in"].rearrange("(k p) c -> p k c", p=P)
    NG = 3 * D // GRP
    XG = D // GRP
    NB4 = GRP // P
    split = SplitProducts(sem, "p3", env["xs"], env["ws"], wf, NF, [NB4] * XG + [NT] * (NG - XG))
    U = split.U
    EH = DH // P

    def weight(g):
        return w_in[:, :, C_XM + g * GRP:C_XM + (g + 1) * GRP]

    with nc.Block() as block:
        @block.sync
        def _(sp):
            sp.dma_start(past[0:NB * PAD, :], I["state_conv"]).then_inc(past_read, 16)
            for g in range(NG):
                for u in range(U):
                    split.load(sp, g, u, g == 0, weight(g))
                if g == 0:
                    sp.dma_start(wif, w_in[:, :, C_IF:C_IF + 2 * H]).then_inc(small, 16)
                    sp.dma_start(bias, I["bias"].broadcast_to([P, 2 * H])).then_inc(small, 16)
                    sp.dma_start(wqk[:, 0], I["w_mq"].rearrange("h (k p) e -> p (h k) e", p=P)).then_inc(wqk_in, 16)
                    sp.dma_start(wqk[:, 1], I["w_mk"].rearrange("h (k p) e -> p (h k) e", p=P)).then_inc(wqk_in, 16)
            sp.wait_ge(tail_out, 2)
            sp.dma_start(O["conv_p"], tail_rows[0:PAD, :]).then_inc(stored, 16)
            sp.dma_start(O["conv_s"], tail_rows[PAD:NTAIL, :]).then_inc(stored, 16)
            sp.wait_ge(stored, 32)

        @block.scalar
        def _(act):
            act.wait_ge(cleared, 1)

            def copy_xm(g):
                for b in range(NB4):
                    j = g * NB4 + b
                    act.wait_ge(split.steps, split.product_done(g, b))
                    for half in range(2):
                        for t0, m, sample in token_tiles_of(half):
                            src = bank[2 * b + half][:, t0 - half * HALF_TOK:t0 - half * HALF_TOK + m]
                            if sample:
                                act.activation(xs[:, j, :, PAD:], src.rearrange("p (b t) -> p b t", b=NB), ACT.Copy).then_inc(xm_copied, 1)
                            else:
                                act.activation(xm[:, j, PAD + t0:PAD + t0 + m], src, ACT.Copy)

            def copy_out(g):
                for c in range(NT):
                    n = rows(c)
                    act.wait_ge(split.steps, split.product_done(g, c))
                    if g < 2 * XG:
                        h = 2 * (g - XG)
                        act.activation(v[0:n, c, h:h + 2, 0:DH], bank[c][0:n, :].rearrange("p (h e) -> p h e", h=2),
                                       ACT.Copy).then_inc(copied, 1)
                    else:
                        act.activation(o[0:n, c, (g - 2 * XG) * GRP:(g - 2 * XG + 1) * GRP], bank[c][0:n, :], ACT.Sigmoid).then_inc(copied, 1)
            for g in range(NG):
                for u in range(U):
                    split.split_hi(act, g, u, g == 0, xnT if g == 0 else None)
                    if u == 0 and g:
                        (copy_xm if g <= XG else copy_out)(g - 1)
                    if u == 0 and g == NG - 1:
                        act.wait_ge(conv, 1)
                        act.activation(xcT.rearrange("p k t -> p (k t)"), xcT.rearrange("p k t -> p (k t)"), ACT.Silu).then_inc(act_out, 1)
            copy_out(NG - 1)
            for h in range(H):
                act.wait_ge(products_qk, h + 1)
                for i in range(2 * EH):
                    e, half = i // 2, i % 2
                    act.activation(qT[:, EH * h + e, half * HALF_TOK:(half + 1) * HALF_TOK], bank[i][:, 0:HALF_TOK], ACT.Copy,
                                   scale=DH ** -0.5).then_inc(q_kept, 1)

        @block.vector
        def _(dve):
            chain = Chain(dve, own)
            dve.memset(gates.rearrange("p c g -> p (c g)"), 0.0)
            dve.memset(v[:, :, :, DH], 1.0)
            dve.memset(xm[:, :, 0:PAD], 0.0).then_inc(cleared, 1)
            dve.wait_ge(past_turned, 1)
            dve.tensor_copy(xs[:, :, :, 0:PAD],
                            bank[5][:, 0:KD * NB * PAD].rearrange("p (k b t) -> p k b t", k=KD, b=NB)).then_inc(past_in, 1)
            dve.wait_ge(past_in, 1)
            dve.wait_ge(cleared, 1)

            def convolve(j):
                dve.wait_ge(xm_copied, j + 1)
                out_p = xcT[:, j, 0:SEQ]
                out_s = xcT[:, j, SEQ:].rearrange("p (b t) -> p b t", b=NB)
                for i in range(CW):
                    w = col[f"conv_w{i}"][:, j:j + 1]
                    for out, src in ((out_p, xm[:, j, i:i + SEQ]), (out_s, xs[:, j, :, i:i + TS])):
                        if i == 0:
                            ins = dve.tensor_scalar(out, src, w, col["conv_b"][:, j:j + 1], ALU.mult, ALU.add)
                        else:
                            ins = dve.scalar_tensor_tensor(out=out, in0=src, scalar=w, in1=out, op0=ALU.mult, op1=ALU.add)
                    if j == KD - 1 and i == CW - 1:
                        ins.then_inc(conv, 1)
                    else:
                        chain.then(ins)
            for g in range(NG):
                for u in range(U):
                    split.split_lo(dve, g, u, xnT if g == 0 else None)
                    if XG <= g < 2 * XG and u % 2:
                        for b in range(2):
                            convolve((g - XG) * NB4 + 2 * (u // 2) + b)
                if g == 2 * XG - 1:
                    tv = tails.rearrange("p k (b t) -> p k b t", t=PAD)
                    dve.tensor_copy(tv[:, :, 0, :], xm[:, :, SEQ:SEQ + PAD])
                    dve.tensor_copy(tv[:, :, 1:, :], xs[:, :, :, TS:TS + PAD]).then_inc(tail_in, 1)
            dve.wait_ge(if_done, 1)
            dve.tensor_tensor(gates[:, 0:NCH, :], bank[7][:, 0:NCH * 2 * H].rearrange("p (c g) -> p c g", c=NCH),
                              mid(bias, NCH, P, NCH, 2 * H), ALU.add)
            dve.tensor_tensor(gates[0:NS, NCH, :], bank[7][0:NS, NCH * 2 * H:NT * 2 * H], bias[0:NS], ALU.add).then_inc(if_kept, 1)
            for half in range(2):
                dve.wait_ge(tail_turned, half + 1)
                dve.tensor_copy(tail_rows[0:NTAIL, half * GRP:(half + 1) * GRP], bank[5 + half][0:NTAIL, :]).then_inc(tail_out, 1)
            for h in range(H):
                dve.wait_ge(products_qk, h + 1)
                for i in range(2 * EH):
                    e, half = i // 2, i % 2
                    dve.tensor_copy(kT[:, EH * h + e, half * HALF_TOK:(half + 1) * HALF_TOK], bank[4 + i][:, 0:HALF_TOK]).then_inc(k_kept, 1)

        @block.tensor
        def _(pe):
            pe.wait_ge(past_read, 16)
            n = NB * PAD
            for k in range(KD):
                ins = pe.transpose(bank[5][:, k * n:(k + 1) * n], past[0:n, k * P:(k + 1) * P], T["ident"][0:n, 0:n])
            ins.then_inc(past_turned, 1)
            pe.wait_ge(past_in, 1)
            for g in range(NG):
                def free(j, g=g):
                    if 1 <= g < XG:
                        pe.wait_ge(xm_copied, NB4 * (g - 1) + j + 1)
                    elif g == XG:
                        pe.wait_ge(xm_copied, NB4 * (g - 1) + j // 2 + 1)
                    elif g > XG:
                        pe.wait_ge(copied, NT * (g - 1 - XG) + j + 1)
                split.multiply(pe, g, bank, g >= XG, free)
                if g == XG:
                    pe.wait_ge(xm_copied, KD)
                    pe.wait_ge(small, 32)
                    for c in range(NT):
                        m = rows(c)
                        for k in range(KD):
                            ins = pe.matmul(bank[7][0:m, c * 2 * H:(c + 1) * 2 * H], xnT[:, k, c * P:c * P + m], wif[:, k, :],
                                            start=k == 0, stop=k == KD - 1)
                    ins.then_inc(if_done, 1)
            pe.wait_ge(tail_in, 1)
            for half in range(2):
                for j in range(4):
                    ins = pe.transpose(bank[5 + half][0:NTAIL, j * P:(j + 1) * P], tails[:, half * 4 + j, :], T["ident"])
                ins.then_inc(tail_turned, 1)
            pe.wait_ge(act_out, 1)
            pe.wait_ge(wqk_in, 32)
            pe.wait_ge(if_kept, 1)
            for h in range(H):
                for s, kept in ((0, q_kept), (1, k_kept)):
                    for i in range(2 * EH):
                        e, half = i // 2, i % 2
                        if h:
                            pe.wait_ge(kept, 2 * EH * (h - 1) + i + 1)
                        else:
                            if 4 * s + i < NT:
                                pe.wait_ge(copied, NT * (NG - 1 - XG) + 4 * s + i + 1)
                            elif 4 * s + i < 7:
                                pe.wait_ge(tail_out, 4 * s + i - 4)
                        for d in range(EH):
                            ins = pe.matmul(bank[4 * s + i][:, 0:HALF_TOK], wqk[:, s, EH * h + d, e * P:(e + 1) * P],
                                            xcT[:, EH * h + d, half * HALF_TOK:(half + 1) * HALF_TOK], start=d == 0, stop=d == EH - 1)
                ins.then_inc(products_qk, 1)


def mlstm(env, v, o, kT, qT, gates):
    nc, I, O, A, T, bank, sem = (env[k] for k in ("nc", "I", "O", "A", "T", "bank", "sem"))
    col = env["col"]
    NE = DH + 1
    lf, a, b = A.take(NT, H), A.take(NT, H), A.take(NT, H)
    sp_ = A.take(NT, H)
    m_prev = A.take(2, H)
    m_last = A.take(2, H)
    top_, mb, u, w_prev, floor_ = A.take(H), A.take(2 * H), A.take(H), A.take(H), A.take(3, H)
    expo, wkd = A.take(2 * H), A.take(2 * H)
    den = A.take(H)
    stats, mv, rstd = A.take(H, 6), A.take(H, 2), A.take(H)
    dA, dM, dW = A.take(H, P), A.take(H, P), A.take(H, P)
    tmp, prob = A.take(H, P), A.take(H, P)
    qh, kw, yb = A.take(H, 2, P), A.take(H, DH), A.take(H, NE)
    Cp = A.take(H, 2, NE)
    Cs = A.take(2, NB, 2 * NE).rearrange("p s b (e n) -> p s b e n", e=2)
    qz = A.take(2, NB, NS)
    prob_s, qh_s, kw_s, yb_s, wkd_s = A.take(H, NS), A.take(H, 2, NS), A.take(H, DH), A.take(H, NE), A.take(2 * H)
    n_rows = A.take(DH)
    nT_in, nT_out = A.take(2, NB * H), A.take(2, H + NB * H)
    decm, decB = A.take(NB, H), A.take(NB, H)
    kz = A.take(NB, DH, at=0)
    names = ("small loads0 loads1 stored stored_h0 stored_h1 absolute lf_done b_done own act_own diagA bcA mx diagM "
             "w_en diagW picked bcM bcW scores kturned expo wkd masked dwT probs qh kw y ycopied kv C_new var root ydone "
             "yturned hm qz kz decm dec_done dec_in n_turned n_in n_out n_out_turned n_out_rows n_col ml "
             "y_s ys_copied kv_s Cs_new").split()
    S = {x: sem("p4_" + x) for x in names}
    C_dram = I["state_C"].rearrange("b h (e p) v -> h p b e v", p=P)
    C_out = O["C_s"].rearrange("b h (e p) v -> h p b e v", p=P)

    FRONT = [NCH] + list(range(NCH))
    BACK = list(range(NCH - 1)) + [NCH, NCH - 1]
    assert H == NCH

    sample_y = bank[0][0:NS, P:P + NE]

    def kv_bank(i):
        return bank[4 + i % 4][:, 0:NE]

    def of(c, prompt, sample):
        return sample if c == NCH else prompt
    qTv = qT.rearrange("p (h e) t -> p h e t", h=H)

    with nc.Block() as block:
        @block.gpsimd
        def _(pool):
            for s in env["finished"]:
                pool.sem_clear(s)

        @block.sync
        def _(sp):
            def load(h):
                for e in range(2):
                    sp.dma_start(Cs[:, h % 2, :, e, 0:DH], C_dram[h][:, :, e, :]).then_inc(S[f"loads{h % 2}"], 16)
            sp.dma_start(n_rows[0:NB * H, :], I["state_n"]).then_inc(S["small"], 16)
            for s in range(NB):
                sp.dma_start(m_prev[s * TS:(s + 1) * TS, 1, :], I["state_m"][s:s + 1, :].broadcast_to([TS, H])).then_inc(S["small"], 16)
            load(0)
            load(1)
            for h in range(H):
                for part in range(2):
                    sp.wait_ge(S["Cs_new"], 2 * NB * h + NB * (part + 1))
                    some = slice(part * NB // 2, (part + 1) * NB // 2)
                    for e in range(2):
                        sp.dma_start(C_out[h][:, some, e, :], Cs[:, h % 2, some, e, 0:DH]).then_inc(S[f"stored_h{h % 2}"], 16)
                sp.wait_ge(S["n_col"], h + 1)
                if h + 2 < H:
                    sp.wait_ge(S[f"stored_h{h % 2}"], 64 * (h // 2 + 1))
                    load(h + 2)
            sp.wait_ge(S["C_new"], NCH * 2 * H)
            for e in range(2):
                sp.dma_start(O["C_p"].rearrange("h (e p) v -> e p h v", p=P)[e], Cp[:, :, e, 0:DH]).then_inc(S["stored"], 16)
            sp.wait_ge(S["n_out_rows"], 1)
            sp.dma_start(O["n_p"], n_rows[0:H, :]).then_inc(S["stored"], 16)
            sp.dma_start(O["n_s"], n_rows[H:H + NB * H, :]).then_inc(S["stored"], 16)
            sp.dma_start(O["m_p"], m_last[0:1, 0, :]).then_inc(S["stored"], 16)
            sp.dma_start(O["m_s"], m_last[0:NS:TS, 1, :]).then_inc(S["stored"], 16)
            sp.wait_ge(S["stored"], 16 * 6)
            for i in range(2):
                sp.wait_ge(S[f"stored_h{i}"], 64 * H // 2)

        @block.scalar
        def _(act):
            z = gates[:, :, H:2 * H]
            chain = Chain(act, S["act_own"])
            chain.then(act.activation(sp_, z, ACT.Abs))
            chain.then(act.activation(sp_, sp_, ACT.Exp, scale=-1.0))
            act.activation(sp_, sp_, ACT.Ln, bias=1.0).then_inc(S["absolute"], 1)

            def stabiliser_exps(c):
                n = rows(c)
                act.wait_ge(S["mx"], FRONT.index(c) + 1)
                act.activation(w_prev[0:n], u[0:n], ACT.Exp)
                act.activation(floor_[0:n, of(c, c % 2, 2)], mb[0:n, H:2 * H], ACT.Exp, scale=-1.0).then_inc(S["w_en"], 1)

            def weight_exps(c):
                n = rows(c)
                act.wait_ge(S["expo"], FRONT.index(c) + 1)
                act.activation(of(c, wkd, wkd_s)[0:n], expo[0:n], ACT.Exp).then_inc(S["wkd"], 1)
                act.wait_ge(S["masked"], FRONT.index(c) + 1)
                for h in range(H):
                    act.activation(tmp[0:n, h, 0:n], tmp[0:n, h, 0:n], ACT.Exp, bias=a[0:n, c, h:h + 1]).then_inc(S["dwT"], 1)

            def copy_sample_output(h):
                act.wait_ge(S["y_s"], h + 1)
                act.activation(yb_s[0:NS, h], sample_y, ACT.Copy).then_inc(S["ys_copied"], 1)

            def root(c):
                n = rows(c)
                act.wait_ge(S["var"], BACK.index(c) + 1)
                act.activation(rstd[0:n, :], mv[0:n, :, 1], ACT.Sqrt, bias=EPS).then_inc(S["root"], 1)
            for c in (NCH, 0):
                stabiliser_exps(c)
                weight_exps(c)
            copy_sample_output(0)
            for c in range(NCH):
                if c == NCH - 1:
                    root(NCH)
                if c:
                    act.wait_ge(S["ydone"], BACK.index(c - 1) + 1)
                for h in range(H):
                    act.wait_ge(S["y"], H * c + h + 1)
                    act.activation(yb[:, h], bank[6 + h % 2][:, 0:NE], ACT.Copy).then_inc(S["ycopied"], 1)
                if c < NCH - 1:
                    stabiliser_exps(c + 1)
                root(c)
                if c < NCH - 1:
                    weight_exps(c + 1)
                    copy_sample_output(c + 1)

        @block.vector
        def _(dve):
            chain = Chain(dve, S["own"])
            dve.memset(m_prev[:, 0, :], 0.0)
            dve.wait_ge(S["absolute"], 1)
            dve.scalar_tensor_tensor(out=lf, in0=gates[:, :, H:2 * H], scalar=0.0, in1=sp_, op0=ALU.min,
                                     op1=ALU.subtract).then_inc(S["lf_done"], 1)
            dve.wait_ge(S["b_done"], 1)
            dve.tensor_copy(b[:, 0:NCH, :], bank[0][:, 0:NCH * H].rearrange("p (c h) -> p c h", c=NCH))
            dve.tensor_copy(b[0:NS, NCH, :], bank[0][0:NS, NCH * H:NT * H]).then_inc(S["own"], 1)
            chain.n += 1
            dve.wait_ge(S["own"], chain.n)
            dve.tensor_tensor(a[:, 0:NCH, :], gates[:, 0:NCH, 0:H], b[:, 0:NCH, :], ALU.subtract)
            chain.then(dve.tensor_tensor(a[0:NS, NCH, :], gates[0:NS, NCH, 0:H], b[0:NS, NCH, :], ALU.subtract))

            dve.wait_ge(S["small"], 16 * (NB + 1))
            dve.wait_ge(S["n_turned"], 1)
            dve.tensor_copy(nT_in, bank[3][:, 0:2 * NB * H].rearrange("p (e n) -> p e n", e=2)).then_inc(S["n_in"], 1)
            n_in_v = nT_in.rearrange("p e (b h) -> p e b h", b=NB)
            n_out_v = nT_out[:, :, H:].rearrange("p e (b h) -> p e b h", b=NB)

            def diag_a(c):
                n = rows(c)
                ident = mid(T["ident"][0:n, 0:n], H, n, H, n)
                f = FRONT.index(c)
                if f:
                    dve.wait_ge(S["bcA"], f)
                dve.tensor_tensor(dA[0:n, :, 0:n], ident, bc(a[0:n, c, :], n, H, n), ALU.mult).then_inc(S["diagA"], 1)

            def running_max(c):
                n = rows(c)
                sample = c == NCH
                k_ = "s" if sample else "p"
                mp = m_prev[0:n, 1 if sample else 0, :]
                ident = mid(T["ident"][0:n, 0:n], H, n, H, n)
                f = FRONT.index(c)
                dve.wait_ge(S["bcA"], f + 1)
                if f:
                    dve.wait_ge(S["probs"], f)
                chain.then(dve.tensor_tensor(tmp[0:n, :, 0:n], quarter(bank[1], n)[0:n],
                                             mid(T["mask_ts_" + k_][0:n, 0:n], H, n, H, n), ALU.add))
                chain.then(dve.tensor_reduce(top_[0:n], tmp[0:n, :, 0:n], AX, ALU.max))
                if f:
                    dve.wait_ge(S["picked"], f)
                chain.then(dve.tensor_tensor(mb[0:n, 0:H], top_[0:n], mp, ALU.max))
                dve.tensor_tensor(mb[0:n, H:2 * H], mb[0:n, 0:H], b[0:n, c, :], ALU.add)
                dve.tensor_tensor(u[0:n], mp, mb[0:n, 0:H], ALU.subtract).then_inc(S["mx"], 1)
                if f:
                    dve.wait_ge(S["bcM"], f)
                    dve.wait_ge(S["bcW"], f)
                dve.tensor_tensor(dM[0:n, :, 0:n], ident, bc(mb[0:n, 0:H], n, H, n), ALU.mult).then_inc(S["diagM"], 1)

            def state_weights(c):
                n = rows(c)
                sample = c == NCH
                k_ = "s" if sample else "p"
                mp = m_prev[0:n, 1 if sample else 0, :]
                ident = mid(T["ident"][0:n, 0:n], H, n, H, n)
                f = FRONT.index(c)
                dve.wait_ge(S["w_en"], f + 1)
                dve.tensor_tensor(dW[0:n, :, 0:n], ident, bc(w_prev[0:n], n, H, n), ALU.mult).then_inc(S["diagW"], 1)
                dve.wait_ge(S["picked"], f + 1)
                dve.tensor_tensor(expo[0:n, 0:H], a[0:n, c, :], bank[0][0:n, 32:32 + H], ALU.subtract)
                dve.tensor_tensor(expo[0:n, H:2 * H], mp, bank[0][0:n, 32:32 + H], ALU.subtract).then_inc(S["expo"], 1)
                ins = dve.tensor_copy(m_last[0:n, 1 if sample else 0, :], bank[0][0:n, 32 + H:32 + 2 * H])
                if not sample:
                    dve.wait_ge(S["expo"], f + 1)
                    ins = dve.tensor_copy(mp, bank[0][0:n, 32 + H:32 + 2 * H])
                ins.then_inc(S["ml"], 1)

            def mask_and_weigh(c):
                n = rows(c)
                sample = c == NCH
                k_ = "s" if sample else "p"
                f = FRONT.index(c)
                dve.wait_ge(S["bcM"], f + 1)
                dve.tensor_tensor(tmp[0:n, :, 0:n], mid(T["mask_st_" + k_][0:n, 0:n], H, n, H, n), quarter(bank[1], n)[0:n],
                                  ALU.subtract).then_inc(S["masked"], 1)
                dve.wait_ge(S["bcW"], f + 1)
                if 0 < c < NCH:
                    dve.wait_ge(S["y"], H * c)
                for e in range(2):
                    ins = dve.tensor_tensor(of(c, qh, qh_s)[:, :, e, 0:n], qTv[:, :, e, c * P:c * P + n], quarter(bank[2], n), ALU.mult)
                ins.then_inc(S["qh"], 1)
                dve.wait_ge(S["wkd"], f + 1)
                if 0 < c < NCH:
                    dve.wait_ge(S["kv"], 2 * H * c)
                for half in range(2):
                    dve.wait_ge(S["kturned"], 2 * f + half + 1)
                    dve.tensor_tensor(of(c, kw, kw_s)[0:n, 2 * half:2 * half + 2], bank[4 + half][0:n, :].rearrange("p (h e) -> p h e", h=2),
                                      bc(of(c, wkd, wkd_s)[0:n, 2 * half:2 * half + 2], n, 2, DH), ALU.mult).then_inc(S["kw"], 1)

            def weighed_scores(c):
                n = rows(c)
                f = FRONT.index(c)
                dve.wait_ge(S["scores"], f + 1)
                dve.wait_ge(S["dwT"], H * (f + 1))
                dve.tensor_tensor(of(c, prob, prob_s)[0:n, :, 0:n], quarter(bank[3], n)[0:n], tmp[0:n, :, 0:n], ALU.mult).then_inc(S["probs"], 1)

            def prompt_state(c):
                dve.wait_ge(S["y"], H * (c + 1))
                for h in range(H):
                    for e in range(2):
                        dve.wait_ge(S["kv"], 2 * H * c + 2 * h + e + 1)
                        if c == 0:
                            dve.tensor_copy(Cp[:, h, e], kv_bank(2 * h + e)).then_inc(S["C_new"], 1)
                        else:
                            dve.scalar_tensor_tensor(out=Cp[:, h, e], in0=Cp[:, h, e], scalar=wkd[:, H + h:H + h + 1],
                                                     in1=kv_bank(2 * h + e), op0=ALU.mult, op1=ALU.add).then_inc(S["C_new"], 1)

            def sample_decays():
                dve.tensor_tensor(decm[0:NS], bc(T["last_rows"][0:NS], NS, NB, H), mid(wkd_s[0:NS, H:2 * H], NB, NS, NB, H),
                                  ALU.mult).then_inc(S["decm"], 1)

            def sample_q(h):
                dve.wait_ge(S[f"loads{h % 2}"], 32 * (h // 2 + 1))
                dve.tensor_copy(Cs[:, h % 2, :, :, DH].rearrange("p b e -> p e b"), n_in_v[:, :, :, h])
                if h:
                    dve.wait_ge(S["y_s"], h)
                dve.tensor_tensor(qz, qh_s[:, h].unsqueeze(2).to_broadcast([P, 2, NB, NS]),
                                  T["batch_cols"].rearrange("p (b t) -> p b t", b=NB).unsqueeze(1).to_broadcast([P, 2, NB, NS]),
                                  ALU.mult).then_inc(S["qz"], 1)

            def sample_k(h):
                if h:
                    dve.wait_ge(S["kv_s"], 2 * NB * h)
                dve.tensor_tensor(kz[0:NS], mid(kw_s[0:NS, h, :], NB, NS, NB, DH), bc(T["batch_rows"][0:NS], NS, NB, DH),
                                  ALU.mult).then_inc(S["kz"], 1)

            def sample_state(h):
                dve.wait_ge(S["y_s"], h + 1)
                for s in range(NB):
                    for e in range(2):
                        dve.wait_ge(S["kv_s"], 2 * NB * h + 2 * s + e + 1)
                        dve.scalar_tensor_tensor(out=Cs[:, h % 2, s, e], in0=Cs[:, h % 2, s, e],
                                                 scalar=decB[:, s, h:h + 1], in1=kv_bank(2 * s + e),
                                                 op0=ALU.mult, op1=ALU.add).then_inc(S["Cs_new"], 1)
                dve.wait_ge(S["Cs_new"], 2 * NB * (h + 1))
                dve.tensor_copy(n_out_v[:, :, :, h], Cs[:, h % 2, :, :, DH].rearrange("p b e -> p e b")).then_inc(S["n_col"], 1)

            def divide(c):
                n = rows(c)
                y = of(c, yb, yb_s)
                dve.wait_ge(*of(c, (S["ycopied"], H * (c + 1)), (S["ys_copied"], H)))
                chain.then(dve.scalar_tensor_tensor(out=den[0:n], in0=y[0:n, :, DH], scalar=-1.0, in1=y[0:n, :, DH],
                                                    op0=ALU.mult, op1=ALU.max))
                chain.then(dve.tensor_tensor(den[0:n], den[0:n], floor_[0:n, of(c, c % 2, 2)], ALU.max))
                chain.then(dve.reciprocal(den[0:n], den[0:n]))
                chain.then(dve.tensor_tensor(y[0:n, :, 0:DH], y[0:n, :, 0:DH], bc(den[0:n], n, H, DH), ALU.mult))
                for h in range(H):
                    ins = dve.bn_stats(stats[0:n, h], y[0:n, h, 0:DH])
                chain.then(ins)
                for h in range(H):
                    ins = dve.bn_aggr(mv[0:n, h], stats[0:n, h])
                ins.then_inc(S["var"], 1)

            def normalise(c):
                n = rows(c)
                y = of(c, yb, yb_s)
                dve.wait_ge(S["root"], BACK.index(c) + 1)
                chain.then(dve.reciprocal(rstd[0:n, :], rstd[0:n, :]))
                for h in range(H):
                    ins = dve.tensor_scalar(y[0:n, h, 0:DH], y[0:n, h, 0:DH], mv[0:n, h, 0:1], rstd[0:n, h:h + 1],
                                            ALU.subtract, ALU.mult)
                chain.then(ins)
                oc = o[0:n, c, :].rearrange("p (h e) -> p h e", h=H)
                dve.tensor_tensor(oc, y[0:n, :, 0:DH], oc, ALU.mult).then_inc(S["ydone"], 1)

            def keep_h(c):
                n = rows(c)
                for half in range(2):
                    dve.wait_ge(S["yturned"], 2 * BACK.index(c) + half + 1)
                    k = 4 * half
                    dve.tensor_tensor(qT[:, k:k + 4, c * P:c * P + n], quarter(bank[6 + half], n),
                                      bc(col["mlstm_norm_g"][:, k:k + 4], P, 4, n), ALU.mult).then_inc(S["hm"], 1)

            diag_a(NCH)
            running_max(NCH)
            state_weights(NCH)
            mask_and_weigh(NCH)
            diag_a(0)
            weighed_scores(NCH)
            sample_decays()
            running_max(0)
            dve.wait_ge(S["dec_done"], 1)
            dve.tensor_copy(decB.rearrange("p b h -> p (b h)"), bank[0][:, 64:64 + NB * H]).then_inc(S["dec_in"], 1)
            dve.wait_ge(S["dec_in"], 1)
            dve.wait_ge(S["n_in"], 1)
            state_weights(0)
            sample_q(0)
            mask_and_weigh(0)
            sample_k(0)
            for c in range(NCH - 1):
                diag_a(c + 1)
                weighed_scores(c)
                running_max(c + 1)
                divide(c)
                prompt_state(c)
                sample_state(c)
                state_weights(c + 1)
                sample_q(c + 1)
                normalise(c)
                mask_and_weigh(c + 1)
                keep_h(c)
                sample_k(c + 1)
            weighed_scores(NCH - 1)
            divide(NCH)
            prompt_state(NCH - 1)
            sample_state(NCH - 1)
            normalise(NCH)
            dve.wait_ge(S["C_new"], NCH * 2 * H)
            dve.tensor_copy(nT_out[:, :, 0:H], Cp[:, :, :, DH].rearrange("p h e -> p e h")).then_inc(S["n_col"], 1)
            keep_h(NCH)
            divide(NCH - 1)
            normalise(NCH - 1)
            keep_h(NCH - 1)
            dve.wait_ge(S["n_out_turned"], 1)
            dve.tensor_copy(n_rows[0:H + NB * H, :], bank[3][0:H + NB * H, 0:DH]).then_inc(S["n_out_rows"], 1)

        @block.tensor
        def _(pe):
            pe.wait_ge(S["lf_done"], 1)
            for c in range(NT):
                n = rows(c)
                ins = pe.matmul(bank[0][0:n, c * H:(c + 1) * H], T["tri_s" if c == NCH else "tri_p"][0:n, 0:n], lf[0:n, c, :],
                                start=True, stop=True)
            ins.then_inc(S["b_done"], 1)
            pe.wait_ge(S["small"], 16 * (NB + 1))
            for e in range(2):
                ins = pe.transpose(bank[3][:, e * NB * H:(e + 1) * NB * H], n_rows[0:NB * H, e * P:(e + 1) * P],
                                   T["ident"][0:NB * H, 0:NB * H])
            ins.then_inc(S["n_turned"], 1)
            pe.wait_ge(S["n_in"], 1)

            def spread_a(c):
                n = rows(c)
                f = FRONT.index(c)
                pe.wait_ge(S["diagA"], f + 1)
                if f:
                    pe.wait_ge(S["probs"], f)
                pe.matmul(quarter(bank[1], n)[0:n], T["ones"][0:n, 0:n], dA[0:n, :, 0:n], start=True, stop=True).then_inc(S["bcA"], 1)

            def scores_of(c):
                n = rows(c)
                tok = slice(c * P, c * P + n)
                if c < NCH:
                    pe.wait_ge(S["probs"], FRONT.index(c))
                for h in range(H):
                    for e in range(2):
                        ins = pe.matmul(bank[3][0:n, h * P:h * P + n], kT[:, 2 * h + e, tok], qT[:, 2 * h + e, tok],
                                        start=e == 0, stop=e == 1)
                ins.then_inc(S["scores"], 1)

            def turn_k(c):
                n = rows(c)
                tok = slice(c * P, c * P + n)
                if c == 0:
                    pe.wait_ge(S["kw"], 2)
                elif c < NCH:
                    pe.wait_ge(S["C_new"], 2 * H * c)
                    pe.wait_ge(S["Cs_new"], 2 * NB * c)
                for half in range(2):
                    for j in range(4):
                        ins = pe.transpose(bank[4 + half][0:n, j * P:(j + 1) * P], kT[:, 4 * half + j, tok], T["ident"])
                    ins.then_inc(S["kturned"], 1)

            def spread_m(c):
                n = rows(c)
                f = FRONT.index(c)
                pe.wait_ge(S["mx"], f + 1)
                if f:
                    pe.wait_ge(S["ml"], f)
                if f > 1:
                    pe.wait_ge(S["ys_copied"], c)
                pe.matmul(bank[0][0:n, 32:32 + 2 * H], T["pick_s" if c == NCH else "pick_p"][0:n, 0:n], mb[0:n, :],
                          start=True, stop=True).then_inc(S["picked"], 1)
                pe.wait_ge(S["diagM"], f + 1)
                pe.matmul(quarter(bank[1], n)[0:n], T["ones"][0:n, 0:n], dM[0:n, :, 0:n], start=True, stop=True).then_inc(S["bcM"], 1)
                pe.wait_ge(S["diagW"], f + 1)
                pe.matmul(quarter(bank[2], n), T["ones"][0:n, :], dW[0:n, :, 0:n], start=True, stop=True).then_inc(S["bcW"], 1)

            def output(c, h):
                out = bank[6 + h % 2][:, 0:NE]
                if c and h < 2:
                    pe.wait_ge(S["hm"], 2 * BACK.index(c - 1) + h + 1)
                if c or h >= 2:
                    pe.wait_ge(S["ycopied"], H * c + h - 1)
                ins = pe.matmul(out, prob[:, h, :], v[:, c, h, :], start=True, stop=c == 0)
                if c:
                    for e in range(2):
                        ins = pe.matmul(out, qh[:, h, e, :], Cp[:, h, e], start=False, stop=e == 1)
                ins.then_inc(S["y"], 1)

            def sample_output(h):
                pe.wait_ge(S["qz"], h + 1)
                pe.wait_ge(S["ml"], h + 2)
                pe.wait_ge(S["dec_in"], 1)
                pe.matmul(sample_y, prob_s[0:NS, h], v[0:NS, NCH, h, :], start=True, stop=False)
                for s in range(NB):
                    for e in range(2):
                        ins = pe.matmul(sample_y, qz[:, e, s], Cs[:, h % 2, s, e], start=False, stop=s == NB - 1 and e == 1)
                ins.then_inc(S["y_s"], 1)

            def sample_products(h):
                pe.wait_ge(S["kz"], h + 1)
                for s in range(NB):
                    for e in range(2):
                        i = 2 * s + e
                        if i < 4:
                            pe.wait_ge(S["C_new"], 2 * H * (h + 1) - 3 + i)
                        else:
                            pe.wait_ge(S["Cs_new"], 2 * NB * h + i - 3)
                        pe.matmul(kv_bank(i), kz[0:NS, s, e * P:(e + 1) * P], v[0:NS, NCH, h, :],
                                  start=True, stop=True).then_inc(S["kv_s"], 1)

            def turn_h(c):
                n = rows(c)
                pe.wait_ge(S["ydone"], BACK.index(c) + 1)
                if c == NCH:
                    pe.wait_ge(S["Cs_new"], 2 * NB * H)
                for half in range(2):
                    if c == NCH - 1:
                        pe.wait_ge(S["hm"], 2 * BACK.index(NCH) + half + 1)
                    for j in range(4):
                        k = 4 * half + j
                        ins = pe.transpose(bank[6 + half][:, j * P:j * P + n], o[0:n, c, k * P:(k + 1) * P], T["ident"][0:n, 0:n])
                    ins.then_inc(S["yturned"], 1)
            spread_a(NCH)
            scores_of(NCH)
            turn_k(NCH)
            spread_m(NCH)
            spread_a(0)
            pe.wait_ge(S["decm"], 1)
            pe.matmul(bank[0][:, 64:64 + NB * H], T["ones"][0:NS, :], decm[0:NS].rearrange("p b h -> p (b h)"),
                      start=True, stop=True).then_inc(S["dec_done"], 1)
            scores_of(0)
            turn_k(0)
            pe.wait_ge(S["dec_in"], 1)
            spread_m(0)
            sample_output(0)
            for c in range(NCH):
                ahead = c < NCH - 1
                if ahead:
                    spread_a(c + 1)
                pe.wait_ge(S["probs"], FRONT.index(c) + 1)
                pe.wait_ge(S["qh"], FRONT.index(c) + 1)
                for h in range(H):
                    output(c, h)
                if ahead:
                    scores_of(c + 1)
                pe.wait_ge(S["kw"], 2 * (FRONT.index(c) + 1))
                for h in range(H):
                    for e in range(2):
                        i = 2 * h + e
                        if i in (2, 3):
                            pe.wait_ge(S["ycopied"], H * (c + 1) - 3 + i)
                        elif i > 3:
                            pe.wait_ge(S["C_new"], 2 * H * c + i - 3)
                        pe.matmul(kv_bank(i), kw[:, h, e * P:(e + 1) * P], v[:, c, h, :],
                                  start=True, stop=True).then_inc(S["kv"], 1)
                sample_products(c)
                if ahead:
                    turn_k(c + 1)
                    spread_m(c + 1)
                else:
                    turn_h(NCH)
                turn_h(c)
                if ahead:
                    sample_output(c + 1)
            pe.wait_ge(S["n_col"], H + 1)
            for e in range(2):
                ins = pe.transpose(bank[3][0:H + NB * H, e * P:(e + 1) * P], nT_out[:, e, :], T["ident"])
            ins.then_inc(S["n_out_turned"], 1)


def merge_norm_and_queries(env, hmT, kT, x1, xn2, qpT, keys):
    nc, I, A, T, bank, sem = (env[k] for k in ("nc", "I", "A", "T", "bank", "sem"))
    xnT, yrT = env["xnT"], env["yrT"]
    XG = D // GRP
    NF = 4
    NB4 = GRP // P
    wf = A.take(NF, SplitProducts.UK, GRP)
    g_row = A.take(D)
    ms = A.take(NT, 1)
    branch = [xn2.rearrange("p c d -> p (c d)")[:, 0:KD * TOK].rearrange("p (k t) -> p k t", k=KD), kT]
    merged = branch[0]
    junk = kT.rearrange("p k t -> p (k t)")[:, 0:D]
    xn2T = yrT
    w_in = I["w_in"].rearrange("(k p) c -> p k c", p=P)

    def blocks_of(name):
        return I[name].rearrange("(k p) c -> p k c", p=P)
    kinds = [(w_in[:, :, C_GR:C_GR + D], xnT), (w_in[:, :, C_GM:C_GM + D], xnT),
             (blocks_of("w_br"), yrT), (blocks_of("w_bm"), hmT), (blocks_of("w_out"), merged)]
    GATES, BRANCHES, QUERIES = XG * 2, XG * 4, XG * 5
    QG = 2 * PH // NB4
    NG = QUERIES + QG
    w_pq = blocks_of("w_pq")
    split = SplitProducts(sem, "p5", env["xs"], env["ws"], wf, NF, [NB4] * BRANCHES + [NT] * XG + [NB4] * QG)
    U = split.U
    xin, row = sem("p5_x"), sem("p5_row")
    sig, gated, merge, own = sem("p5_sigmoids"), sem("p5_gated"), sem("p5_merged"), sem("p5_own")
    x1_in, squares, roots, normed, turned, xn2T_in = (
        sem("p5_" + n) for n in ("x1", "squares", "roots", "normed", "turned", "xn2T"))
    kept, moved = sem("p5_kept"), sem("p5_moved")

    def weight(g):
        if g >= QUERIES:
            return w_pq[:, :, (g - QUERIES) * GRP:(g - QUERIES + 1) * GRP]
        return kinds[g // XG][0][:, :, (g % XG) * GRP:(g % XG + 1) * GRP]

    def operand(g):
        if g == QUERIES:
            return xn2T
        return kinds[g // XG][1] if g in (0, GATES, GATES + XG, BRANCHES) else None

    with nc.Block() as block:
        @block.gpsimd
        def _(pool):
            for s in env["finished"]:
                pool.sem_clear(s)

        @block.sync
        def _(sp):
            for g in range(NG):
                for u in range(U):
                    split.load(sp, g, u, g == 0, weight(g))
                if g == 0:
                    sp.dma_start(x1[:, 0:NCH, :], I["x_prompt"].rearrange("(t p) d -> p t d", p=P)).then_inc(xin, 16)
                    sp.dma_start(x1[0:NS, NCH, :], I["x_sample"]).then_inc(xin, 16)
                    sp.dma_start(g_row, I["norm2_row"].broadcast_to([P, D])).then_inc(row, 16)
            sp.dma_start(keys[:, 0], I["keys1"]).then_inc(moved, 16)
            sp.dma_start(keys[:, 1], I["keys2"]).then_inc(moved, 16)
            sp.wait_ge(normed, NT)
            sp.dma_start(xn2[NS:P, NCH, :], xn2[0:NS, NCH, :]).then_inc(moved, 16)
            sp.wait_ge(moved, 48)

        @block.scalar
        def _(act):
            def gates(g):
                for b in range(NB4):
                    act.wait_ge(split.steps, split.product_done(g, b))
                    for half in range(2):
                        ins = act.activation(branch[g // XG][:, (g % XG) * NB4 + b, half * HALF_TOK:(half + 1) * HALF_TOK],
                                             bank[2 * b + half][:, 0:HALF_TOK], ACT.Sigmoid)
                    ins.then_inc(sig, 1)

            def mean_square(c):
                n = rows(c)
                act.wait_ge(x1_in, NT + c + 1)
                if c:
                    act.wait_ge(squares, c)
                act.activation(junk[0:n, :], x1[0:n, c, :], ACT.Square, accum_out=ms[0:n, c, :]).then_inc(squares, 1)
                act.wait_ge(squares, c + 1)
                act.activation(ms[0:n, c, :], ms[0:n, c, :], ACT.Sqrt, bias=EPS, scale=1.0 / D).then_inc(roots, 1)

            def keep_turned(c):
                n = rows(c)
                for half in range(2):
                    act.wait_ge(turned, 2 * c + half + 1)
                    act.activation(xn2T[:, 4 * half:4 * half + 4, c * P:c * P + n], quarter(bank[5 + half], n), ACT.Copy).then_inc(xn2T_in, 1)

            def keep_queries(g):
                for b in range(NB4):
                    act.wait_ge(split.steps, split.product_done(g, b))
                    for half in range(2):
                        ins = act.activation(qpT[:, (g - QUERIES) * NB4 + b, half * HALF_TOK:(half + 1) * HALF_TOK],
                                             bank[2 * b + half][:, 0:HALF_TOK], ACT.Copy)
                    ins.then_inc(kept, 1)
            for g in range(NG):
                if g == QUERIES:
                    mean_square(0)
                    for c in range(1, NT):
                        mean_square(c)
                        keep_turned(c - 1)
                    keep_turned(NT - 1)
                    act.wait_ge(xn2T_in, 2 * NT)
                for u in range(U):
                    if g == BRANCHES:
                        act.wait_ge(merge, min(NB4 * XG, 2 * (u + 1)))
                    split.split_hi(act, g, u, g == 0, operand(g))
                    if u == 0 and 1 <= g <= GATES:
                        gates(g - 1)
                    if u == 0 and g > QUERIES:
                        keep_queries(g - 1)
            keep_queries(NG - 1)

        @block.vector
        def _(dve):
            chain = Chain(dve, own)

            def times_branch(g):
                which = (g - GATES) // XG
                for b in range(NB4):
                    dve.wait_ge(split.steps, split.product_done(g, b))
                    dve.wait_ge(sig, (which * XG + g % XG) * NB4 + b + 1)
                    for half in range(2):
                        v = branch[which][:, (g % XG) * NB4 + b, half * HALF_TOK:(half + 1) * HALF_TOK]
                        ins = dve.tensor_tensor(v, v, bank[2 * b + half][:, 0:HALF_TOK], ALU.mult)
                    ins.then_inc(gated, 1)

            def add_branches(g):
                for b in range(NB4):
                    k = (g % XG) * NB4 + b
                    dve.wait_ge(gated, XG * NB4 + k + 1)
                    dve.tensor_tensor(merged[:, k], merged[:, k], branch[1][:, k], ALU.add).then_inc(merge, 1)

            def add_x(g, c):
                n = rows(c)
                dve.wait_ge(split.steps, split.product_done(g, c))
                x = x1[0:n, c, (g % XG) * GRP:(g % XG + 1) * GRP]
                dve.tensor_tensor(x, x, bank[c][0:n, :], ALU.add).then_inc(x1_in, 1)

            def normalise(c):
                n = rows(c)
                dve.wait_ge(roots, c + 1)
                chain.then(dve.reciprocal(ms[0:n, c, :], ms[0:n, c, :]))
                dve.scalar_tensor_tensor(out=xn2[0:n, c, :], in0=x1[0:n, c, :], scalar=ms[0:n, c, :], in1=g_row[0:n, :],
                                         op0=ALU.mult, op1=ALU.mult).then_inc(normed, 1)
            dve.memset(x1[NS:P, NCH, :], 0.0)
            for g in range(NG):
                if g == BRANCHES:
                    times_branch(g - 1)
                    add_branches(g - 1)
                if g == QUERIES:
                    add_x(g - 1, 0)
                    dve.wait_ge(row, 16)
                    for c in range(1, NT):
                        add_x(g - 1, c)
                        normalise(c - 1)
                    normalise(NT - 1)
                for u in range(U):
                    split.split_lo(dve, g, u, operand(g))
                    if u == 0 and GATES < g < BRANCHES:
                        times_branch(g - 1)
                        if g == BRANCHES - 1:
                            add_branches(g - 1)
                    if u == 0 and BRANCHES < g < QUERIES:
                        dve.wait_ge(xin, 32)
                        for c in range(NT):
                            add_x(g - 1, c)

        @block.tensor
        def _(pe):
            for g in range(NG):
                def free(j, g=g):
                    if g == 0:
                        return
                    if g <= GATES:
                        pe.wait_ge(sig, NB4 * (g - 1) + j + 1)
                    elif g < BRANCHES:
                        pe.wait_ge(gated, NB4 * (g - 1 - GATES) + j + 1)
                    elif g == BRANCHES:
                        pe.wait_ge(gated, NB4 * (g - 1 - GATES) + j // 2 + 1)
                    elif g < QUERIES:
                        pe.wait_ge(x1_in, j + 1)
                    elif g > QUERIES:
                        pe.wait_ge(kept, NB4 * (g - 1 - QUERIES) + j + 1)
                if g == QUERIES:
                    for c in range(NT):
                        pe.wait_ge(normed, c + 1)

                        def free_turned(half, c=c):
                            if c:
                                pe.wait_ge(xn2T_in, 2 * (c - 1) + half + 1)
                        transpose_tile(pe, xn2[:, c, :], T["ident"], bank[5:7], rows(c), turned, free_turned)
                    pe.wait_ge(xn2T_in, 2 * NT)
                split.multiply(pe, g, bank, BRANCHES <= g < QUERIES, free)


def experts(env, x1, xn2, qpT, keys, scores):
    nc, I, O, A, T, bank, sem = (env[k] for k in ("nc", "I", "O", "A", "T", "bank", "sem"))
    R = 8
    NDIAG = 4
    AHEAD = 3
    LINKS = 13
    junk, norm_junk, g_row = A.take(D, at=0), A.take(D, at=D), A.take(D, at=2 * D)
    assert 3 * D + 2 * NKEY <= _WHERE["ones"][0]
    table = A.take(NGRP, TOPK)
    gate = A.take(NGRP, TOPK)
    stage = A.take(4, TOPK)
    dots, act_, wts = A.take(TOPK), A.take(TOPK), A.take(TOPK)
    diag = A.take(NDIAG, P)
    ms = A.take(NT, 1)
    s, s_left = A.take(2, NKEY), A.take(2, NKEY)
    vals, picks, picks_f = A.take(2, TOPK), A.take(2, TOPK), A.take(2, TOPK)
    cand, cand_left = A.take(NCAND), A.take(NCAND)
    top_s, top_p = A.take(TOPK), A.take(TOPK)
    at, at_f, found = A.take(2, TOPK), A.take(2, TOPK), A.take(2, TOPK)
    onehot = A.take(2, TOPK, TOPK)
    w, total = A.take(TOPK), A.take(1)
    u_ring, v_ring = A.take(R, D), A.take(R, D)
    u_in, v_in = [sem(f"p6_u_in{i}") for i in range(R)], [sem(f"p6_v_in{i}") for i in range(R)]
    ready, staged = sem("p6_ready"), sem("p6_staged")
    u_used, v_used = sem("p6_u_used"), sem("p6_v_used")
    gelu, weighed, diags, added = sem("p6_gelu"), sem("p6_weighed"), sem("p6_diags"), sem("p6_added")
    own, squares, roots, y_done, stored = (sem("p6_" + n) for n in ("own", "squares", "roots", "y", "stored"))
    s_in, s_read, link, expos, exped, routed, summed, gated = (
        sem("p6_" + n) for n in ("s_in", "s_read", "link", "expos", "exped", "routed", "summed", "gated"))
    scored, kept_scores = sem("p6_scored"), sem("p6_kept_scores")
    posts = sem("p6_posts")
    NPG = NCH * G_TILE

    with nc.Block() as block:
        @block.sync
        def _(sp):
            sp.dma_start(g_row, I["normf_row"].broadcast_to([P, D])).then_inc(ready, 16)
            for c in range(NT):
                sp.wait_ge(y_done, c + 1)
                dst = O["y_prompt"][c * P:(c + 1) * P, :] if c < NCH else O["y_sample"]
                sp.dma_start(dst, x1[0:rows(c), c, :]).then_inc(stored, 16)
            sp.wait_ge(stored, 16 * NT)

        @block.gpsimd
        def _(pool):
            u_idx, v_idx = stage[:, 0:2, :].bitcast(U32), stage[:, 2:4, :].bitcast(U32)

            def stage_numbers(which, place, r, count):
                pool.tensor_copy(which[:, place, :], table.bitcast(U32)[:, bass.ds(r, 1), :].rearrange("p a k -> p (a k)")).then_inc(staged, 1)
                pool.wait_ge(staged, count)
                pool.sem_inc(posts, 1)

            def gather(ring, which, place, k, rows_of, arrived, used, count):
                pool.wait_ge(used, count)
                pool.sem_inc(posts, 1)
                pool.indirect_dma_start(ring[:, k % R, :], None, rows_of,
                                        bass.IndirectOffsetOnAxis(which[:, place, k:k + 1], 0)).then_inc(arrived[k % R], 16)

            def turn(g, parity, last_u=False):
                for k in range(TOPK):
                    gather(v_ring, v_idx, parity, k, I["expert_v"], v_in, v_used, TOPK * g + (k + 1))
                    gather(u_ring, u_idx, 1 - parity, k, I["expert_u"], u_in, u_used, TOPK * g + (TOPK + k + 1))
                    if k == R:
                        stage_numbers(v_idx, 1 - parity, g + 1, 2 * g + 4)
                        if not last_u:
                            pool.wait_ge(routed, g + 3)
                            pool.sem_inc(posts, 1)
                            stage_numbers(u_idx, parity, g + 2, 2 * g + 5)

            pool.wait_ge(routed, 1)
            stage_numbers(u_idx, 0, 0, 1)
            stage_numbers(v_idx, 0, 0, 2)
            for k in range(TOPK):
                gather(u_ring, u_idx, 0, k, I["expert_u"], u_in, u_used, k + 1)
            pool.wait_ge(routed, 2)
            stage_numbers(u_idx, 1, 1, 3)
            with pool.Fori(0, NGRP // 2 - 1) as pair:
                for parity in range(2):
                    turn(2 * pair + parity, parity)
            turn(NGRP - 2, 0, last_u=True)
            for k in range(TOPK):
                gather(v_ring, v_idx, 1, k, I["expert_v"], v_in, v_used, TOPK * (NGRP - 1) + k + 1)

        @block.vector
        def _(dve):
            chain = Chain(dve, own)
            pk, tp, atu = picks.bitcast(U32), top_p.bitcast(U32), at.bitcast(U32)
            dve.memset(ms.rearrange("p a b -> p (a b)"), 0.0).then_inc(u_used, R)

            def top16_of(r):
                n = [0]

                def then(ins):
                    n[0] += 1
                    ins.then_inc(link, 1)
                    dve.wait_ge(link, LINKS * r + n[0])

                def post():
                    dve.sem_inc(posts, 1)

                dve.wait_ge(s_in, r + 1)
                post()
                for t in range(2):
                    ins = dve.max(vals[:, t, 0:8], s[:, t, :])
                then(ins)
                post()
                for t in range(2):
                    dve.max_index(pk[:, t, 0:8], vals[:, t, 0:8], s[:, t, :])
                    ins = dve.match_replace(s_left[:, t, :], vals[:, t, 0:8], s[:, t, :], LOWEST)
                ins.then_inc(s_read, 1)
                dve.wait_ge(s_read, r + 1)
                post()
                for t in range(2):
                    ins = dve.max(vals[:, t, 8:16], s_left[:, t, :])
                then(ins)
                post()
                for t in range(2):
                    ins = dve.max_index(pk[:, t, 8:16], vals[:, t, 8:16], s_left[:, t, :])
                then(ins)
                dve.tensor_copy(picks_f, pk)
                then(dve.tensor_tensor(cand.rearrange("p (i j) -> p i j", i=TOPK), bc(vals[:, 0, :], P, TOPK, TOPK),
                                       mid(vals[:, 1, :], TOPK, P, TOPK, TOPK), ALU.add))
                post()
                then(dve.max(top_s[:, 0:8], cand))
                post()
                dve.max_index(tp[:, 0:8], top_s[:, 0:8], cand)
                then(dve.match_replace(cand_left, top_s[:, 0:8], cand, LOWEST))
                post()
                then(dve.max(top_s[:, 8:16], cand_left))
                post()
                then(dve.max_index(tp[:, 8:16], top_s[:, 8:16], cand_left))
                dve.tensor_tensor(w, top_s, top_s[:, 0:1].to_broadcast([P, TOPK]), ALU.subtract).then_inc(expos, 1)
                dve.tensor_single_scalar(atu[:, 0], tp, 4, ALU.logical_shift_right)
                then(dve.tensor_single_scalar(atu[:, 1], tp, 15, ALU.bitwise_and))
                then(dve.tensor_copy(at_f, atu))
                then(dve.tensor_tensor(onehot, at_f.unsqueeze(3).to_broadcast([P, 2, TOPK, TOPK]),
                                       T["iota16"].unsqueeze(1).unsqueeze(1).to_broadcast([P, 2, TOPK, TOPK]), ALU.is_equal))
                then(dve.tensor_tensor(onehot, onehot, picks_f.unsqueeze(2).to_broadcast([P, 2, TOPK, TOPK]), ALU.mult))
                then(dve.tensor_reduce(found, onehot, AX, ALU.add))
                e_out = table.bitcast(U32)[:, bass.ds(r, 1), :].rearrange("p a k -> p (a k)")
                dve.scalar_tensor_tensor(out=e_out, in0=found[:, 0], scalar=float(NKEY), in1=found[:, 1], op0=ALU.mult,
                                         op1=ALU.add).then_inc(routed, 1)
                assert n[0] == LINKS, n

            def weights_of(r):
                dve.wait_ge(exped, r + 1)
                dve.tensor_reduce(total, w, AX, ALU.add).then_inc(summed, 1)
                dve.wait_ge(summed, 2 * r + 1)
                dve.reciprocal(total, total).then_inc(summed, 1)
                dve.wait_ge(summed, 2 * r + 2)
                dve.tensor_scalar(gate[:, bass.ds(r, 1), :].rearrange("p a k -> p (a k)"), w, total, None, ALU.mult).then_inc(gated, 1)

            def tile_of(ap, g):
                return ap[:, bass.ds(g // G_TILE, 1), :].rearrange("p a d -> p (a d)")

            def dots_of(g, weights_at=None):
                for k in range(TOPK):
                    dve.wait_ge(u_in[k % R], 32 * g + (16 * (k // R) + 16))
                    dve.scalar_tensor_tensor(out=junk, in0=u_ring[:, k % R, :], scalar=1.0, in1=tile_of(xn2, g), op0=ALU.mult,
                                             op1=ALU.mult, accum_out=dots[:, k:k + 1]).then_inc(u_used, 1)
                    dve.wait_ge(u_used, TOPK * g + (k + R + 1))
                    if weights_at is not None and k == R:
                        weights_of(weights_at)

            def weigh(g):
                dve.wait_ge(gelu, g + 1)
                dve.wait_ge(gated, g + 1)
                dve.tensor_tensor(wts, act_, gate[:, bass.ds(g, 1), :].rearrange("p a k -> p (a k)"), ALU.mult).then_inc(weighed, 1)

            def add(g):
                dve.wait_ge(v_used, TOPK * g + (TOPK + R))
                for j in range(2):
                    x = x1[:, bass.ds(g // G_TILE, 1), j * GRP:(j + 1) * GRP].rearrange("p a d -> p (a d)")
                    dve.tensor_tensor(x, x, bank[j][:, :], ALU.add).then_inc(added, 1)

            def turn(g, ahead):
                dots_of(g + 1, g + AHEAD - 1 if ahead else None)
                dve.wait_ge(diags, TOPK * g + TOPK)
                weigh(g + 1)
                add(g)
                if ahead:
                    top16_of(g + AHEAD)

            def last_norm(tiles):
                dve.wait_ge(ready, 16)
                for c in tiles:
                    n = rows(c)
                    dve.wait_ge(roots, c + 1)
                    chain.then(dve.reciprocal(ms[0:n, c, :], ms[0:n, c, :]))
                    dve.scalar_tensor_tensor(out=x1[0:n, c, :], in0=x1[0:n, c, :], scalar=ms[0:n, c, :], in1=g_row[0:n, :],
                                             op0=ALU.mult, op1=ALU.mult).then_inc(y_done, 1)

            top16_of(0)
            weights_of(0)
            top16_of(1)
            dots_of(0, weights_at=1)
            weigh(0)
            top16_of(2)
            with dve.Fori(0, NGRP - AHEAD) as g:
                turn(g, True)
            weights_of(NGRP - 1)
            last_norm(range(NCH))
            with dve.Fori(NGRP - AHEAD, NGRP - 1) as g:
                turn(g, False)
            add(NGRP - 1)
            last_norm(range(NCH, NT))

        @block.scalar
        def _(act):
            def stage_scores(r):
                if not isinstance(r, int) or r:
                    act.wait_ge(s_read, r)
                if isinstance(r, int):
                    act.wait_ge(kept_scores, r // 2 + 1)
                act.activation(s, scores[:, bass.ds(r, 1), :].rearrange("p a (t k) -> p (a t) k", t=2), ACT.Copy).then_inc(s_in, 1)

            def exps(r):
                act.wait_ge(expos, r + 1)
                act.activation(w, w, ACT.Exp).then_inc(exped, 1)

            def gelu_of(g):
                act.wait_ge(u_used, TOPK * g + (TOPK + R))
                act.activation(act_, dots, ACT.Gelu).then_inc(gelu, 1)

            def turn(g, spread, ahead=True, last=False):
                if ahead:
                    stage_scores(g + AHEAD)
                act.wait_ge(weighed, g + 1)
                for k in range(TOPK):
                    act.wait_ge(v_used, TOPK * g + (k + R - NDIAG + 1))
                    act.activation(diag[:, k % NDIAG, :], spread, ACT.Copy, scale=wts[:, k:k + 1]).then_inc(diags, 1)
                    if ahead and k == NDIAG:
                        exps(g + AHEAD - 1)
                if not last:
                    gelu_of(g + 1)

            def norm_sums(tiles, groups):
                act.wait_ge(added, 2 * groups + 1)
                for c in tiles:
                    n = rows(c)
                    if c:
                        act.wait_ge(squares, c)
                    act.activation(norm_junk[0:n, :], x1[0:n, c, :], ACT.Square, accum_out=ms[0:n, c, :]).then_inc(squares, 1)
                act.wait_ge(squares, tiles[-1] + 1)
                for c in tiles:
                    n = rows(c)
                    act.activation(ms[0:n, c, :], ms[0:n, c, :], ACT.Sqrt, bias=EPS, scale=1.0 / D).then_inc(roots, 1)

            for i in range(NGRP // 2):
                act.wait_ge(scored, i + 1)
                act.activation(scores[:, 2 * i:2 * i + 2, :], bank[2 + i % 4][:, :].rearrange("p (g k) -> p g k", g=2),
                               ACT.Copy).then_inc(kept_scores, 1)
                if i in (0, 3):
                    stage_scores((0, 3).index(i))
                if i in (8, 15):
                    exps((8, 15).index(i))
            act.wait_ge(kept_scores, NGRP // 2)
            gelu_of(0)
            stage_scores(2)
            with act.Fori(0, NPG) as g:
                turn(g, T["ident"])
            turn(NPG, T["fold2"])
            exps(NGRP - 1)
            norm_sums(range(NCH), NPG)
            with act.Fori(NPG + 1, NGRP - 1) as g:
                turn(g, T["fold2"], ahead=False)
            turn(NGRP - 1, T["fold2"], ahead=False, last=True)
            norm_sums(range(NCH, NT), NGRP)

        @block.tensor
        def _(pe):
            pe.sem_inc(v_used, R)
            pe.sem_inc(added, 1)
            for i in range(NGRP // 2):
                if i >= 4:
                    pe.wait_ge(kept_scores, i - 3)
                for r in (2 * i, 2 * i + 1):
                    c, h = r // G_TILE, r % G_TILE
                    parts = [(slice(0, P), h)] if c < NCH else [(slice(0, NS), h), (slice(NS, P), h + G_SAMPLE)]
                    for where, head in parts:
                        for t in range(2):
                            ins = pe.matmul(bank[2 + i % 4][where, (r % 2) * 2 * NKEY + t * NKEY:(r % 2) * 2 * NKEY + (t + 1) * NKEY],
                                            qpT[:, 2 * head + t, c * P:c * P + rows(c)], keys[:, t], start=True, stop=True)
                ins.then_inc(scored, 1)
            with pe.Fori(0, NGRP) as g:
                for k in range(TOPK):
                    if k == 0:
                        pe.wait_ge(added, 2 * g + 1)
                    pe.wait_ge(diags, TOPK * g + (k + 1))
                    pe.wait_ge(v_in[k % R], 32 * g + (16 * (k // R) + 16))
                    for j in range(2):
                        ins = pe.matmul(bank[j][:, :], diag[:, k % NDIAG, :], v_ring[:, k % R, j * GRP:(j + 1) * GRP],
                                        start=k == 0, stop=k == TOPK - 1)
                    ins.then_inc(v_used, 1)


OUTS = {
    "y_prompt": (SEQ, D), "y_sample": (NS, D),
    "ret_p": (H, DK, DV), "C_p": (H, DH, DH), "n_p": (H, DH), "m_p": (1, H), "conv_p": (CW - 1, D),
    "ret_s": (NB, H, DK, DV), "C_s": (NB, H, DH, DH), "n_s": (NB * H, DH), "m_s": (NB, H), "conv_s": (NB * (CW - 1), D),
}
SHAPES = [(1, SEQ, D), (NB, TS, D), (1, 1, H, DK, DV), (1, 1, H, DH, DH), (1, 1, H, DH), (1, 1, H), (1, 1, CW - 1, D),
          (1, NB, H, DK, DV), (1, NB, H, DH, DH), (1, NB, H, DH), (1, NB, H), (1, NB, CW - 1, D)]


def layout(inputs):
    a = {k: np.asarray(v) for k, v in inputs.items()}
    per_channel = [a["norm1_g"][0], a["norm2_g"][0], a["ret_norm_g"][0].reshape(-1), a["mlstm_norm_g"][0].reshape(-1),
                   a["conv_b"][0]] + [a["conv_w"][0, j] for j in range(CW)]
    return {
        "x_prompt": a["x_prompt"][0], "x_sample": a["x_sample"].reshape(NS, D),
        "state_ret": a["state_ret"][0], "state_C": a["state_mlstm_C"][0], "state_n": a["state_mlstm_n"][0].reshape(NB * H, DH),
        "state_m": a["state_mlstm_m"][0], "state_conv": a["state_conv"][0].reshape(NB * (CW - 1), D),
        "w_in": a["w_in"][0], "w_mq": a["w_mq"][0], "w_mk": a["w_mk"][0], "w_br": a["w_br"][0], "w_bm": a["w_bm"][0],
        "w_out": a["w_out"][0], "w_pq": a["w_pq"][0],
        "keys1": np.ascontiguousarray(a["sub_keys1"][0].T), "keys2": np.ascontiguousarray(a["sub_keys2"][0].T),
        "expert_u": a["expert_u"][0], "expert_v": a["expert_v"][0],
        "bias": np.concatenate([a["b_i"], a["b_f"]], 1), "norm2_row": a["norm2_g"], "normf_row": a["norm_f_g"].reshape(1, D),
        "cols": np.ascontiguousarray(np.stack(per_channel).reshape(len(COLS), KD, P).transpose(2, 0, 1)).reshape(P, -1),
        "tables": _TABLES,
    }


def kernel(**inputs):
    import concourse.bacc as _bacc
    from concourse.bass_utils import run_bass_kernel_spmd as _run

    nc = _bacc.Bacc("TRN2", target_bir_lowering=False, num_devices=1)
    arrays = {f"in_{k}": np.ascontiguousarray(v) for k, v in layout(inputs).items()}
    I = {k[3:]: nc.dram_tensor(k, v.shape, mybir.dt.from_np(v.dtype), kind="ExternalInput").ap() for k, v in arrays.items()}
    O = {k: nc.dram_tensor(f"out_{k}", s, F32, kind="ExternalOutput").ap() for k, s in OUTS.items()}
    program(nc, I, O)
    r = _run(nc, [arrays], core_ids=[0])
    return tuple(r.results[0][f"out_{k}"].reshape(s) for k, s in zip(OUTS, SHAPES))
```
